# Optimizing a Trainium2 kernel written in Bass

```python
import math, functools
import jax, jax.numpy as jnp
from jax import lax
import numpy as np

D_MODEL = 1024
BATCH = 1
SEQ = 512
DEPTH = 2
DEC_BATCH = 8
DEC_SEQ = 4
PAST_LEN = 2048
PAGE_SIZE = 128

F32 = jnp.float32
BRANCH_WIDTH = D_MODEL // 2
N_BRANCH = 4
A_HEAD_DIM = 64
A_HEADS = BRANCH_WIDTH // A_HEAD_DIM
A_KV_HEADS = A_HEADS // 2
IDX_HEADS = 8
IDX_DIM = 64
TOPK_MAX = 256
Q_BLOCK = 128
R_HEADS = 4
R_DK = BRANCH_WIDTH // R_HEADS
R_DV = BRANCH_WIDTH // R_HEADS
R_CHUNK = 128
ROPE_BASE = 10000.0
H_HEADS = 4
H_DK = 128
H_DV = BRANCH_WIDTH // H_HEADS
H_CHUNK = 64
MIN_FORGET = 1e-30
M_HEAD_DIM = 64
M_HEADS = BRANCH_WIDTH // M_HEAD_DIM
M_INNER = M_HEADS * M_HEAD_DIM
M_GROUPS = 2
M_STATE = 128
M_CONV = 4
M_CHUNK = 128
M_CONV_DIM = M_INNER + 2 * M_GROUPS * M_STATE
D_FF = -(-8 * D_MODEL // (3 * 256)) * 256
RMS_EPS = 1e-6
GN_EPS = 1e-6
MASK_VALUE = -1e30

SPLIT_SIZES = (
    A_HEADS * A_HEAD_DIM, A_KV_HEADS * A_HEAD_DIM, A_KV_HEADS * A_HEAD_DIM,
    IDX_HEADS * IDX_DIM, IDX_DIM, IDX_HEADS,
    R_HEADS * R_DK, R_HEADS * R_DK, R_HEADS * R_DV, R_HEADS * R_DV,
    H_HEADS * H_DK, H_HEADS * H_DK, H_HEADS * H_DV, H_HEADS * H_DV,
    M_INNER, M_CONV_DIM, M_HEADS,
    N_BRANCH * D_MODEL,
)
SPLIT_POINTS = tuple(sum(SPLIT_SIZES[:i + 1]) for i in range(len(SPLIT_SIZES) - 1))
D_IN = sum(SPLIT_SIZES)

kernel_name = 'hybrid_dsa_retnet_hgrn2_mamba2_step'

def rmsnorm(x, g=None, eps=RMS_EPS):
    xf = x.astype(F32)
    y = xf * lax.rsqrt(jnp.mean(xf * xf, axis=-1, keepdims=True) + eps)
    if g is not None:
        y = y * g.astype(F32)
    return y.astype(x.dtype)

def pick_chunk(T, chunk):
    return chunk if T % chunk == 0 else T

def chunked_scan(step, S0, xs, chunk):
    B, T = xs[0].shape[:2]
    n = T // chunk
    xs_c = tuple(jnp.swapaxes(a.reshape(B, n, chunk, *a.shape[2:]), 0, 1) for a in xs)
    S, ys = lax.scan(lambda s, inp: step(s, *inp), S0, xs_c)
    ys = jnp.swapaxes(ys, 0, 1)
    return S, ys.reshape(B, T, *ys.shape[3:])

def rotary(x, pos):
    half = x.shape[-1] // 2
    inv_freq = ROPE_BASE ** (-jnp.arange(half, dtype=F32) / half)
    ang = pos.astype(F32)[:, None] * inv_freq[None, :]
    c = jnp.cos(ang)[None, :, None, :]
    s = jnp.sin(ang)[None, :, None, :]
    x1, x2 = x[..., :half], x[..., half:]
    return jnp.concatenate([x1 * c - x2 * s, x1 * s + x2 * c], axis=-1)

def sparse_attention_block(q, iq, iw, keys_k, keys_v, keys_i, q_pos, k_pos, topk):
    B, Tq = q.shape[:2]
    logits = jnp.einsum('bqhd,bld->bqhl', iq.astype(F32), keys_i.astype(F32)) * IDX_DIM ** -0.5
    score = jnp.einsum('bqh,bqhl->bql', iw.astype(F32), jax.nn.relu(logits))
    admissible = k_pos[None, :] <= q_pos[:, None]
    score = jnp.where(admissible[None], score, MASK_VALUE)
    top_score, idx = lax.top_k(score, topk)
    valid = top_score > 0.5 * MASK_VALUE
    gather = jax.vmap(lambda kv, ix: kv[ix])
    k_sel = gather(keys_k, idx).astype(F32)
    v_sel = gather(keys_v, idx).astype(F32)
    qg = q.astype(F32).reshape(B, Tq, A_KV_HEADS, A_HEADS // A_KV_HEADS, A_HEAD_DIM)
    s = jnp.einsum('bqgrd,bqkgd->bqgrk', qg, k_sel) * A_HEAD_DIM ** -0.5
    s = jnp.where(valid[:, :, None, None, :], s, MASK_VALUE)
    p = jax.nn.softmax(s, axis=-1)
    o = jnp.einsum('bqgrk,bqkgd->bqgrd', p, v_sel)
    return o.reshape(B, Tq, A_HEADS * A_HEAD_DIM)

def attention_prompt(q, iq, iw, k, v, ik):
    B, T = q.shape[:2]
    topk = min(TOPK_MAX, T // 4)
    pos = jnp.arange(T, dtype=jnp.int32)

    def block(i):
        s0 = i * Q_BLOCK
        sl = lambda a: lax.dynamic_slice_in_dim(a, s0, Q_BLOCK, axis=1)
        return sparse_attention_block(sl(q), sl(iq), sl(iw), k, v, ik,
                                      lax.dynamic_slice_in_dim(pos, s0, Q_BLOCK, axis=0), pos, topk)

    out = lax.map(block, jnp.arange(T // Q_BLOCK))
    return jnp.swapaxes(out, 0, 1).reshape(B, T, A_HEADS * A_HEAD_DIM)

def gather_pages(cache_l, page_table):
    pages = cache_l[page_table]
    return pages.reshape(page_table.shape[0], page_table.shape[1] * PAGE_SIZE, *cache_l.shape[2:])

def retention_chunk(S, q, k, v, log_gamma):
    C = q.shape[1]
    n = jnp.arange(C, dtype=F32)
    diff = n[:, None] - n[None, :]
    decay = jnp.where(diff >= 0, jnp.exp(log_gamma[:, None, None] * jnp.maximum(diff, 0.0)), 0.0)
    scores = jnp.einsum('bnhd,bmhd->bhnm', q, k) * decay[None]
    intra = jnp.einsum('bhnm,bmhe->bnhe', scores, v)
    q_decay = jnp.exp(log_gamma[None, :] * (n[:, None] + 1.0))
    cross = jnp.einsum('bnhd,bhde->bnhe', q * q_decay[None, :, :, None], S)
    k_decay = jnp.exp(log_gamma[None, :] * (C - 1.0 - n)[:, None])
    S_new = jnp.exp(log_gamma * C)[None, :, None, None] * S + \
        jnp.einsum('bmhd,bmhe->bhde', k * k_decay[None, :, :, None], v)
    return S_new, intra + cross

def retention_mixer(q, k, v, g, pos, S0):
    B, T, _ = q.shape
    q = rotary(q.astype(F32).reshape(B, T, R_HEADS, R_DK), pos)
    k = rotary(k.astype(F32).reshape(B, T, R_HEADS, R_DK), pos) * R_DK ** -0.5
    v = v.astype(F32).reshape(B, T, R_HEADS, R_DV)
    log_gamma = jnp.log1p(-jnp.exp2(-5.0 - jnp.arange(R_HEADS, dtype=F32)))
    step = functools.partial(retention_chunk, log_gamma=log_gamma)
    S, o = chunked_scan(step, S0.astype(F32), (q, k, v), pick_chunk(T, R_CHUNK))
    mu = jnp.mean(o, axis=-1, keepdims=True)
    var = jnp.mean(jnp.square(o - mu), axis=-1, keepdims=True)
    o = (o - mu) * lax.rsqrt(var + GN_EPS)
    return jax.nn.silu(g.astype(F32)) * o.reshape(B, T, R_HEADS * R_DV), S

def hgrn_lower_bounds(lb_param):
    p = jax.nn.softmax(lb_param.astype(F32), axis=0)
    return jnp.cumsum(p, axis=0) - p[0]

def gla_chunk(S, q, k, v, logf):
    C = q.shape[1]
    G = jnp.cumsum(logf, axis=1)
    mask = jnp.tril(jnp.ones((C, C), dtype=bool))
    diff = G[:, :, None] - G[:, None, :]
    decay = jnp.exp(jnp.where(mask[None, :, :, None, None], diff, MASK_VALUE))
    A = jnp.einsum('bnmhd,bmhd->bhnm', q[:, :, None] * decay, k)
    intra = jnp.einsum('bhnm,bmhe->bnhe', A, v)
    cross = jnp.einsum('bnhd,bhde->bnhe', q * jnp.exp(G), S)
    G_last = G[:, -1]
    S_new = jnp.exp(G_last)[..., None] * S + \
        jnp.einsum('bmhd,bmhe->bhde', k * jnp.exp(G[:, -1:] - G), v)
    return S_new, intra + cross

def hgrn2_mixer(q, f, i, g, lb, norm_g, S0):
    B, T, _ = q.shape
    q = jax.nn.silu(q.astype(F32)).reshape(B, T, H_HEADS, H_DK) * H_DK ** -0.5
    f = f.astype(F32)
    lb = lb.astype(F32)
    forget = lb + (1.0 - lb) * jax.nn.sigmoid(f)
    logf = jnp.log(jnp.maximum(forget, MIN_FORGET))
    k = (1.0 - lb) * jax.nn.sigmoid(-f)
    rs = lambda a, d: a.reshape(B, T, H_HEADS, d)
    S, o = chunked_scan(gla_chunk, S0.astype(F32),
                        (q, rs(k, H_DK), rs(i.astype(F32), H_DV), rs(logf, H_DK)), pick_chunk(T, H_CHUNK))
    o = rmsnorm(o, norm_g)
    return jax.nn.silu(g.astype(F32)) * o.reshape(B, T, H_HEADS * H_DV), S

def causal_conv(u, buf, w, b):
    T = u.shape[1]
    up = jnp.concatenate([buf, u], axis=1)
    y = b
    for j in range(M_CONV):
        y = y + up[:, j:j + T] * w[j]
    return jax.nn.silu(y), up[:, T:]

def ssd_chunk(h, x, dt, a, Bm, Cm):
    C = x.shape[1]
    cum = jnp.cumsum(a, axis=1)
    mask = jnp.tril(jnp.ones((C, C), dtype=bool))
    seg = jnp.exp(jnp.where(mask[None, :, :, None], cum[:, :, None, :] - cum[:, None, :, :], MASK_VALUE))
    CB = jnp.einsum('bnhs,bmhs->bnmh', Cm, Bm)
    intra = jnp.einsum('bnmh,bmhp->bnhp', CB * seg * dt[:, None, :, :], x)
    cross = jnp.einsum('bnhs,bhps->bnhp', Cm, h) * jnp.exp(cum)[..., None]
    w = jnp.exp(cum[:, -1:] - cum) * dt
    h_new = jnp.exp(cum[:, -1])[:, :, None, None] * h + jnp.einsum('bmhp,bmhs->bhps', x * w[..., None], Bm)
    return h_new, intra + cross

def mamba2_mixer(z, xbc, dt_raw, A_log, dt_bias, D_skip, conv_w, conv_b, norm_g, h0, conv_buf):
    B, T, _ = z.shape
    xbc, new_buf = causal_conv(xbc.astype(F32), conv_buf.astype(F32), conv_w.astype(F32), conv_b.astype(F32))
    x, Bm, Cm = jnp.split(xbc, [M_INNER, M_INNER + M_GROUPS * M_STATE], axis=-1)
    x = x.reshape(B, T, M_HEADS, M_HEAD_DIM)
    rep = M_HEADS // M_GROUPS
    Bm = jnp.repeat(Bm.reshape(B, T, M_GROUPS, M_STATE), rep, axis=2)
    Cm = jnp.repeat(Cm.reshape(B, T, M_GROUPS, M_STATE), rep, axis=2)
    dt = jax.nn.softplus(dt_raw.astype(F32) + dt_bias.astype(F32))
    a = -jnp.exp(A_log.astype(F32)) * dt
    h, y = chunked_scan(ssd_chunk, h0.astype(F32), (x, dt, a, Bm, Cm), pick_chunk(T, M_CHUNK))
    y = y + D_skip.astype(F32)[:, None] * x
    y = y.reshape(B, T, M_INNER) * jax.nn.silu(z.astype(F32))
    y = rmsnorm(y.reshape(B, T, M_GROUPS, M_INNER // M_GROUPS)).reshape(B, T, M_INNER) * norm_g.astype(F32)
    return y, h, new_buf

def trunk_layer(x, pos, lp, states, past):
    B, T, _ = x.shape
    dtype = x.dtype
    h = rmsnorm(x, lp['norm1'])
    (a_q, a_k, a_v, a_iq, a_ik, a_iw, r_q, r_k, r_v, r_g,
     c_q, c_f, c_i, c_g, m_z, m_xbc, m_dt, gates) = jnp.split(h @ lp['w_in'], SPLIT_POINTS, axis=-1)
    q = rmsnorm(a_q.reshape(B, T, A_HEADS, A_HEAD_DIM), lp['q_norm'])
    k = rmsnorm(a_k.reshape(B, T, A_KV_HEADS, A_HEAD_DIM), lp['k_norm'])
    v = a_v.reshape(B, T, A_KV_HEADS, A_HEAD_DIM)
    iq = a_iq.reshape(B, T, IDX_HEADS, IDX_DIM)
    iw = a_iw * IDX_HEADS ** -0.5
    if past is None:
        o_a = attention_prompt(q, iq, iw, k, v, a_ik)
    else:
        keys_k = jnp.concatenate([past[0].astype(dtype), k], axis=1)
        keys_v = jnp.concatenate([past[1].astype(dtype), v], axis=1)
        keys_i = jnp.concatenate([past[2].astype(dtype), a_ik], axis=1)
        L = keys_k.shape[1]
        o_a = sparse_attention_block(q, iq, iw, keys_k, keys_v, keys_i, pos,
                                     jnp.arange(L, dtype=jnp.int32), min(TOPK_MAX, L // 4))
    o_b, ret_new = retention_mixer(r_q, r_k, r_v, r_g, pos, states[0])
    o_c, hgrn_new = hgrn2_mixer(c_q, c_f, c_i, c_g, lp['lb'], lp['hgrn_norm'], states[1])
    o_d, ssm_new, conv_new = mamba2_mixer(m_z, m_xbc, m_dt, lp['A_log'], lp['dt_bias'], lp['D_skip'],
                                          lp['conv_w'], lp['conv_b'], lp['ssm_norm'], states[2], states[3])
    branches = jnp.stack([o_a, o_b, o_c, o_d], axis=2).astype(dtype)
    up = jnp.einsum('btnw,nwd->btnd', branches, lp['w_branch'])
    g = jax.nn.sigmoid(gates.reshape(B, T, N_BRANCH, D_MODEL).astype(F32))
    merged = jnp.sum(g * up.astype(F32), axis=2).astype(dtype)
    x = x + merged @ lp['w_out']
    ff_gate, ff_up = jnp.split(rmsnorm(x, lp['norm2']) @ lp['w_gu'], 2, axis=-1)
    x = x + (jax.nn.silu(ff_gate) * ff_up) @ lp['w_down']
    return x, (k, v, a_ik, ret_new, hgrn_new, ssm_new, conv_new)

def setup_inputs(seed: int = 0) -> dict:
    key = jax.random.key(seed)
    k = jax.random.split(key, 32)
    n_pages = PAST_LEN // PAGE_SIZE
    n_used = DEC_BATCH * n_pages
    n_pool = n_used + -(-n_used // 4)

    def nrm(kk, shape, scale=1.0):
        return scale * jax.random.normal(kk, shape, F32)

    def gain(kk, shape, scale=0.02):
        return 1.0 + scale * jax.random.normal(kk, shape, F32)

    x_prompt = nrm(k[0], (BATCH, SEQ, D_MODEL))
    x_sample = nrm(k[1], (DEC_BATCH, DEC_SEQ, D_MODEL))
    cache_k = nrm(k[2], (DEPTH, n_pool, PAGE_SIZE, A_KV_HEADS, A_HEAD_DIM))
    cache_v = nrm(k[3], (DEPTH, n_pool, PAGE_SIZE, A_KV_HEADS, A_HEAD_DIM))
    cache_kidx = nrm(k[4], (DEPTH, n_pool, PAGE_SIZE, IDX_DIM))
    state_ret = nrm(k[5], (DEPTH, DEC_BATCH, R_HEADS, R_DK, R_DV), 0.5)
    state_hgrn = nrm(k[6], (DEPTH, DEC_BATCH, H_HEADS, H_DK, H_DV), 0.5)
    state_ssm = nrm(k[7], (DEPTH, DEC_BATCH, M_HEADS, M_HEAD_DIM, M_STATE), 0.5)
    state_conv = nrm(k[8], (DEPTH, DEC_BATCH, M_CONV - 1, M_CONV_DIM))
    page_table = jax.random.permutation(k[9], n_pool)[:n_used].reshape(DEC_BATCH, n_pages).astype(jnp.int32)
    norm1_g = gain(k[10], (DEPTH, D_MODEL))
    w_in = nrm(k[11], (DEPTH, D_MODEL, D_IN), D_MODEL ** -0.5)
    q_norm_g = gain(k[12], (DEPTH, A_HEAD_DIM))
    k_norm_g = gain(k[13], (DEPTH, A_HEAD_DIM))
    lb_param = nrm(k[14], (DEPTH, H_HEADS * H_DK), 0.1)
    hgrn_norm_g = gain(k[15], (DEPTH, H_DV))
    A_log = jnp.log(jax.random.uniform(k[16], (DEPTH, M_HEADS), F32, 1.0, 16.0))
    dt0 = jnp.exp(jax.random.uniform(k[17], (DEPTH, M_HEADS), F32, math.log(1e-3), math.log(1e-1)))
    dt_bias = dt0 + jnp.log(-jnp.expm1(-dt0))
    D_skip = gain(k[18], (DEPTH, M_HEADS), 0.1)
    conv_w = nrm(k[19], (DEPTH, M_CONV, M_CONV_DIM), M_CONV ** -0.5)
    conv_b = nrm(k[20], (DEPTH, M_CONV_DIM), 0.02)
    ssm_norm_g = gain(k[21], (DEPTH, M_INNER))
    w_branch = nrm(k[22], (DEPTH, N_BRANCH, BRANCH_WIDTH, D_MODEL), BRANCH_WIDTH ** -0.5)
    w_out = nrm(k[23], (DEPTH, D_MODEL, D_MODEL), D_MODEL ** -0.5)
    norm2_g = gain(k[24], (DEPTH, D_MODEL))
    w_gu = nrm(k[25], (DEPTH, D_MODEL, 2 * D_FF), D_MODEL ** -0.5)
    w_down = nrm(k[26], (DEPTH, D_FF, D_MODEL), D_FF ** -0.5)
    return {'x_prompt': x_prompt, 'x_sample': x_sample, 'cache_k': cache_k, 'cache_v': cache_v,
            'cache_kidx': cache_kidx, 'state_ret': state_ret, 'state_hgrn': state_hgrn,
            'state_ssm': state_ssm, 'state_conv': state_conv, 'page_table': page_table,
            'norm1_g': norm1_g, 'w_in': w_in, 'q_norm_g': q_norm_g, 'k_norm_g': k_norm_g,
            'lb_param': lb_param, 'hgrn_norm_g': hgrn_norm_g, 'A_log': A_log, 'dt_bias': dt_bias,
            'D_skip': D_skip, 'conv_w': conv_w, 'conv_b': conv_b, 'ssm_norm_g': ssm_norm_g,
            'w_branch': w_branch, 'w_out': w_out, 'norm2_g': norm2_g, 'w_gu': w_gu, 'w_down': w_down}

def reference(x_prompt, x_sample, cache_k, cache_v, cache_kidx, state_ret, state_hgrn, state_ssm,
              state_conv, page_table, norm1_g, w_in, q_norm_g, k_norm_g, lb_param, hgrn_norm_g,
              A_log, dt_bias, D_skip, conv_w, conv_b, ssm_norm_g, w_branch, w_out, norm2_g, w_gu, w_down):
    B, T = x_prompt.shape[:2]
    TS = x_sample.shape[1]
    past_len = page_table.shape[1] * PAGE_SIZE
    pos_p = jnp.arange(T, dtype=jnp.int32)
    pos_s = past_len + jnp.arange(TS, dtype=jnp.int32)
    lower_bounds = hgrn_lower_bounds(lb_param)
    zero_states = (jnp.zeros((B, R_HEADS, R_DK, R_DV), F32),
                   jnp.zeros((B, H_HEADS, H_DK, H_DV), F32),
                   jnp.zeros((B, M_HEADS, M_HEAD_DIM, M_STATE), F32),
                   jnp.zeros((B, M_CONV - 1, M_CONV_DIM), F32))
    out_p = [[] for _ in range(7)]
    out_s = [[] for _ in range(7)]
    xp, xs = x_prompt, x_sample
    for l in range(DEPTH):
        lp = dict(norm1=norm1_g[l], w_in=w_in[l], q_norm=q_norm_g[l], k_norm=k_norm_g[l],
                  lb=lower_bounds[l], hgrn_norm=hgrn_norm_g[l], A_log=A_log[l], dt_bias=dt_bias[l],
                  D_skip=D_skip[l], conv_w=conv_w[l], conv_b=conv_b[l], ssm_norm=ssm_norm_g[l],
                  w_branch=w_branch[l], w_out=w_out[l], norm2=norm2_g[l], w_gu=w_gu[l], w_down=w_down[l])
        xp, new_p = trunk_layer(xp, pos_p, lp, zero_states, None)
        past = (gather_pages(cache_k[l], page_table), gather_pages(cache_v[l], page_table),
                gather_pages(cache_kidx[l], page_table))
        st = (state_ret[l], state_hgrn[l], state_ssm[l], state_conv[l])
        xs, new_s = trunk_layer(xs, pos_s, lp, st, past)
        for i in range(7):
            out_p[i].append(new_p[i])
            out_s[i].append(new_s[i])
    dtypes = (cache_k.dtype, cache_v.dtype, cache_kidx.dtype, state_ret.dtype,
              state_hgrn.dtype, state_ssm.dtype, state_conv.dtype)
    k_p, v_p, kidx_p, ret_p, hgrn_p, ssm_p, conv_p = [jnp.stack(a).astype(d) for a, d in zip(out_p, dtypes)]
    k_s, v_s, kidx_s, ret_s, hgrn_s, ssm_s, conv_s = [jnp.stack(a).astype(d) for a, d in zip(out_s, dtypes)]
    y_prompt = xp
    y_sample = xs
    return (y_prompt, y_sample, k_p, v_p, kidx_p, ret_p, hgrn_p, ssm_p, conv_p,
            k_s, v_s, kidx_s, ret_s, hgrn_s, ssm_s, conv_s)


_drawn_inputs = setup_inputs


def setup_inputs(seed=0):
    import zlib

    import numpy as np

    out = dict(_drawn_inputs(seed))
    spreads = {}
    factors = {'q_norm_g': 8.0,
     'k_norm_g': 2.753,
     'hgrn_norm_g': 6.395,
     'ssm_norm_g': 3.671,
     'norm2_g': 2.894}
    for name, (base, spread) in spreads.items():
        noise = np.random.default_rng([zlib.crc32(name.encode()), seed]).standard_normal(out[name].shape)
        drawn = base * np.exp(spread * noise) if base else spread * noise
        out[name] = __import__('jax').numpy.asarray(drawn.astype(out[name].dtype))
    for name, factor in factors.items():
        out[name] = (out[name] * factor).astype(out[name].dtype)
    return out
```

```python
from contextlib import ExitStack

import numpy as np

import concourse.bass as bass
from concourse import mybir

ALU = mybir.AluOpType
ACT = mybir.ActivationFunctionType
F32 = mybir.dt.float32
I32 = mybir.dt.int32
AX = mybir.AxisListType.X

P = 128
DM = 1024
SEQ = 512
DEPTH = 2
NB = 8
TS = 4
NS = NB * TS
NT = SEQ // P
T = SEQ + NS
PAST = 2048
PAGE = 128
NPG = PAST // PAGE
LK = PAST + NS
KC = DM // P
DFF = 2816
FC = DFF // P
EPS = 1e-6
NEG = -1e30
TAKEN = -3.0e38
TOPK_P = min(256, SEQ // 4)
TOPK_S = min(256, (PAST + TS) // 4)

A_Q, A_K, A_V, A_IQ, A_IK, A_IW = 0, 512, 768, 1024, 1536, 1600
R_Q, C_Q, M_Z, M_X, M_DT, GATES = 1608, 3656, 5704, 6216, 7240, 7248
D_IN = 11344

C = {}
_at = 0
for _n, _w in (("ident", 128), ("ones", 128), ("tri", 128), ("after", 128), ("tri_s", 32), ("after_s", 32),
               ("seqhot", 8), ("qmask", 256), ("bb", 16), ("lv_sum", 7 * 128), ("lv_mask", 7 * 128),
               ("lv_side", 7), ("rdec", 4 * 128), ("rq", 4), ("rk", 4), ("rdec_s", 4 * 32), ("rq_s", 4),
               ("rk_s", 4), ("cos", 5 * 64), ("sin", 5 * 64), ("neg", 128), ("neg_s", 32), ("eps", 1),
               ("rep", 2 * 128), ("wsel", 2 * NS), ("hsel", 8)):
    C[_n] = (_at, _w)
    _at += _w
NCONST = _at
AN = 19900


def constants():
    c = np.zeros((P, NCONST), np.float64)

    def put(name, a):
        a = np.asarray(a, np.float64)
        a = a.reshape(a.shape[0], -1)
        c[:a.shape[0], C[name][0]:C[name][0] + a.shape[1]] = a

    i = np.arange(P)
    k, n = i[:, None], i[None, :]
    put("ident", np.eye(P))
    put("ones", np.ones((P, P)))
    put("tri", k <= n)
    put("after", k > n)
    t = np.arange(NS)
    same = (t[:, None] // TS) == (t[None, :] // TS)
    put("tri_s", (t[:, None] <= t[None, :]) & same)
    put("after_s", (t[:, None] > t[None, :]) & same)
    put("seqhot", (t[:, None] // TS) == np.arange(NB)[None])
    put("qmask", np.broadcast_to((np.arange(NB)[:, None] == t[None, :] // TS)[None], (P, NB, NS)))
    put("bb", np.broadcast_to(np.eye(4)[None], (P, 4, 4)))
    sums, masks, sides = [], [], []
    for lv in range(7):
        w = 1 << lv
        block = i // (2 * w)
        right = (i // w) % 2 == 1
        ref = block * 2 * w + w - 1
        s = np.where(right[None, :], (k > ref[None, :]) & (k <= n), (k > n) & (k <= ref[None, :]))
        sums.append(s)
        masks.append((block[:, None] == block[None, :]) & ~right[:, None] & right[None, :])
        sides.append(right)
    put("lv_sum", np.stack(sums, 1))
    put("lv_mask", np.stack(masks, 1))
    put("lv_side", np.stack(sides, 1))
    lg = np.log1p(-np.exp2(-5.0 - np.arange(4)))
    sc = 128 ** -0.5
    put("rdec", np.stack([np.where(k <= n, np.exp(-g * (k + 1.0)) * sc, 0.0) for g in lg], 1))
    put("rq", np.exp(lg[None] * (i[:, None] + 1.0)))
    put("rk", np.exp(lg[None] * (127.0 - i[:, None])) * sc)
    ts = t % TS
    put("rdec_s", np.stack([np.where((t[:, None] <= t[None, :]) & same, np.exp(-g * (ts[:, None] + 1.0)) * sc, 0.0)
                            for g in lg], 1))
    put("rq_s", np.exp(lg[None] * (ts[:, None] + 1.0)))
    put("rk_s", np.exp(lg[None] * (TS - 1.0 - ts[:, None])) * sc)
    freq = (np.float32(10000.0) ** (-np.arange(64, dtype=np.float32) / np.float32(64))).astype(np.float32)
    pos = np.zeros((P, 5), np.float32)
    for tt in range(4):
        pos[:, tt] = tt * P + i
    pos[:NS, 4] = PAST + ts
    ang = (pos[:, :, None] * freq[None, None]).astype(np.float32).astype(np.float64)
    put("cos", np.cos(ang))
    put("sin", np.sin(ang))
    put("neg", np.where(n <= k, 0.0, NEG))
    put("neg_s", np.where((t[None, :] <= t[:, None]) & same, 0.0, NEG))
    put("eps", np.full((P, 1), EPS))
    rep = np.zeros((NS, 2, 4, 8, TS))
    for b in range(NB):
        for tq in range(TS):
            rep[b * TS + tq, b // 4, b % 4, :, tq] = 1
    put("rep", rep)
    r = np.arange(P)
    wsel = np.zeros((P, 2, NB, TS))
    for g in range(2):
        wsel[r, g, 4 * g + r // 32, r % TS] = 1
    put("wsel", wsel)
    put("hsel", (r[:, None] // TS) % 8 == np.arange(8)[None])
    return c.astype(np.float32)


LAYER_SEMS = ("proj_ready", "proj_taken", "weights_in0", "weights_in1", "down_job_done", "dve_step", "act_step")


def trunk(nc, inp, out):
    es = ExitStack()
    with es:
        sems, stage_sems, stage_stack = {}, {}, [None]

        def S(name):
            if name in LAYER_SEMS:
                if name not in sems:
                    sems[name] = es.enter_context(nc.semaphore(name))
                return sems[name]
            if name not in stage_sems:
                stage_sems[name] = stage_stack[0].enter_context(nc.semaphore(name))
            return stage_sems[name]

        def part(run, *args):
            with ExitStack() as stack:
                stage_stack[0] = stack
                run(*args)
                with nc.Block() as block:
                    @block.sync
                    def _(sp):
                        for sem in stage_sems.values():
                            sp.sem_clear(sem)
                stage_sems.clear()

        def sb(name, n):
            return es.enter_context(nc.sbuf_tensor(name, [P, n], F32))

        def bc(ap, axis, n):
            u = ap.unsqueeze(axis)
            shape = list(u.shape)
            shape[axis] = n
            return u.broadcast_to(shape)

        xT_ = sb("xT", KC * T)
        hT_ = sb("hT", KC * T)
        brT_ = sb("branchT", 16 * T)
        ring_ = sb("ring", 2 * KC * 512)
        cst = sb("cst", NCONST)
        lbt = sb("lb_both", 2 * 512)
        par = sb("layer_params", 2112)
        ptab = es.enter_context(nc.sbuf_tensor("ptab", [1, NB * NPG], I32))
        arena = sb("arena", AN)
        ps = [es.enter_context(nc.psum_tensor(f"ps{i}", [P, 512], F32)) for i in range(8)]
        xT = xT_[:, :].rearrange("p (c t) -> p c t", c=KC)
        hT = hT_[:, :].rearrange("p (c t) -> p c t", c=KC)
        brT = brT_[:, :].rearrange("p (c t) -> p c t", c=16)
        slot = [ring_[:, i * 4096:(i + 1) * 4096] for i in range(2)]

        def K(name):
            return cst[:, C[name][0]:C[name][0] + C[name][1]]

        ident, ones, tri, after = K("ident"), K("ones"), K("tri"), K("after")
        eps = K("eps")

        class Arena:
            def __init__(self, t, at=0, end=None):
                self.t, self.at, self.end = t, at, end

            def take(self, *dims):
                n = int(np.prod(dims))
                a = self.t[:, self.at:self.at + n]
                self.at += n
                assert self.end is None or self.at <= self.end, self.at
                if len(dims) == 1:
                    return a
                names = "abcd"[:len(dims)]
                return a.rearrange(f"p ({' '.join(names)}) -> p {' '.join(names)}",
                                   **{x: d for x, d in zip(names, dims)})

        pa = Arena(par, 0, 2112)
        g1, g2 = pa.take(KC), pa.take(KC)
        gq, gk = pa.take(64), pa.take(64)
        ghg, dtb, alog, dskip = pa.take(128), pa.take(8), pa.take(8), pa.take(8)
        gssm = pa.take(512)
        cw, cb = pa.take(4, 8), pa.take(8)
        lb, oml = pa.take(512), pa.take(512)

        class Chain:
            def __init__(self, name):
                self.sem, self.n = S(name), 0

            def link(self, eng, ins):
                ins.then_inc(self.sem, 1)
                self.n += 1
                eng.wait_ge(self.sem, self.n)

        vch, ach = Chain("dve_step"), Chain("act_step")

        jobs = [("aq", A_Q, 512), ("akv", A_K, 512), ("iq", A_IQ, 512), ("ikiw", A_IK, 72)]
        jobs += [(f"r{i}", R_Q + 512 * i, 512) for i in range(4)]
        jobs += [(f"c{i}", C_Q + 512 * i, 512) for i in range(4)]
        jobs += [("z", M_Z, 512), ("xbc0", M_X, 512), ("xbc1", M_X + 512, 512), ("dt", M_DT, 8)]
        for db in range(2):
            for n in range(4):
                jobs += [(f"gate{db}{n}", GATES + n * DM + db * 512, 512), (f"wb{db}{n}", (n, db), 512)]
        jobs += [(f"wo{db}", db, 512) for db in range(2)]
        jobs += [(f"gu{i}", i, 512) for i in range(11)]
        jobs += [(f"dn{db}{r}", (db, r), 512) for db in range(2) for r in range(3)]
        J = {name: i for i, (name, _, _) in enumerate(jobs)}
        issued = [0]

        def groups(j):
            n = 0
            for name, _, _ in jobs[:j + 1]:
                n += 5 if name[0] in "rcz" or name in ("aq", "akv", "ikiw", "dt") else 4
            return n

        def slot3(j):
            return slot[j % 2].rearrange("p (c n) -> p c n", c=KC)

        def stream(sp, upto, l):
            for j in range(issued[0], min(upto, len(jobs))):
                name, at, w = jobs[j]
                if j >= 2:
                    if jobs[j - 2][0][:2] == "dn":
                        sp.wait_ge(S("down_job_done"), j - 2 - J["dn00"] + 1)
                    else:
                        sp.wait_ge(S("proj_ready"), groups(j - 2))
                dst = slot3(j)
                lay = bass.ds(l, 1)
                if name[:2] == "wb":
                    src = inp["w_branch"][lay, at[0]].rearrange("o (c p) n -> p (o c) n", p=P)[:, :, at[1] * 512:at[1] * 512 + 512]
                    sp.dma_start(dst[:, 0:4, :], src).then_inc(S(f"weights_in{j % 2}"), 16)
                elif name[:2] == "wo":
                    src = inp["w_out"][lay].rearrange("o (c p) n -> p (o c) n", p=P)[:, :, at * 512:at * 512 + 512]
                    sp.dma_start(dst, src).then_inc(S(f"weights_in{j % 2}"), 16)
                elif name[:2] == "gu":
                    src = inp["w_gu"][lay].rearrange("o (c p) (u n) -> p u (o c) n", p=P, u=2)
                    for u in range(2):
                        sp.dma_start(dst[:, :, u * 256:u * 256 + 256],
                                     src[:, u, :, at * 256:at * 256 + 256]).then_inc(S(f"weights_in{j % 2}"), 16)
                elif name[:2] == "dn":
                    n = min(8, FC - 8 * at[1])
                    src = inp["w_down"][lay].rearrange("o (c p) n -> p (o c) n", p=P)[:, at[1] * 8:at[1] * 8 + n, at[0] * 512:at[0] * 512 + 512]
                    sp.dma_start(dst[:, 0:n, :], src).then_inc(S(f"weights_in{j % 2}"), 16)
                else:
                    src = inp["w_in"][lay].rearrange("o (c p) n -> p (o c) n", p=P)[:, :, at:at + w]
                    sp.dma_start(dst[:, :, 0:w], src).then_inc(S(f"weights_in{j % 2}"), 16)
            issued[0] = max(issued[0], upto)

        def arrived(pe, j):
            n = sum(32 if jobs[i][0][:2] == "gu" else 16 for i in range(j % 2, j + 1, 2))
            pe.wait_ge(S(f"weights_in{j % 2}"), n)

        tiles = [(tt * P, P) for tt in range(NT)] + [(SEQ, NS)]
        kpe, kact = [0], [0]

        def proj_natural(pe, j, w):
            arrived(pe, j)
            for t0, m in tiles:
                k = kpe[0]
                if k >= 2:
                    pe.wait_ge(S("proj_taken"), k - 1)
                for c in range(KC):
                    mm = pe.matmul(ps[k % 2][0:m, 0:w], hT[:, c, t0:t0 + m], slot3(j)[:, c, 0:w],
                                   start=(c == 0), stop=(c == KC - 1))
                mm.then_inc(S("proj_ready"), 1)
                kpe[0] += 1

        def proj_transposed(pe, j, src, kn, dcs, col, banks=(0, 1, 2, 3), taken="proj_taken", first=None):
            arrived(pe, j)
            for dc in dcs:
                k = kpe[0] if first is None else first
                if k >= 2:
                    pe.wait_ge(S(taken), k - 1)
                for c in range(kn):
                    w = slot3(j)[:, c, col(dc):col(dc) + 128]
                    pe.matmul(ps[banks[k % 2]][:, :], w, src[:, c, 0:SEQ], start=(c == 0), stop=(c == kn - 1))
                    mm = pe.matmul(ps[banks[2 + k % 2]][:, 0:NS], w, src[:, c, SEQ:T],
                                   start=(c == 0), stop=(c == kn - 1))
                mm.then_inc(S("proj_ready"), 1)
                if first is None:
                    kpe[0] += 1
                else:
                    first += 1

        def prologue():
            ar = Arena(arena, 0, AN)
            xnat = ar.take(5, DM)
            with nc.Block() as block:
                @block.sync
                def _(sp):
                    sp.dma_start(cst[:, :], inp["consts"]).then_inc(S("consts_in"), 16)
                    sp.dma_start(xnat[:, 0:4, :], inp["x_prompt"].rearrange("o (t p) d -> p (o t) d", p=P)).then_inc(S("x_in"), 16)
                    sp.dma_start(xnat[0:NS, 4, :], inp["x_sample"].rearrange("b t d -> (b t) d")).then_inc(S("x_in"), 16)
                    sp.dma_start(ptab[:, :], inp["page_table"].rearrange("(o b) g -> o (b g)", o=1)).then_inc(S("x_in"), 16)
                    sp.dma_start(lbt[:, :], inp["lb_param"].rearrange("(o l) n -> o (l n)", o=1).broadcast_to([P, 2 * 512])).then_inc(S("lb_in"), 16)
                    sp.wait_ge(S("x_in"), 48)

                @block.tensor
                def _(pe):
                    pe.wait_ge(S("consts_in"), 16)
                    pe.wait_ge(S("x_in"), 48)
                    for c in range(KC):
                        if c >= 2:
                            pe.wait_ge(S("x_taken"), c - 1)
                        for tt, (t0, m) in enumerate(tiles):
                            dst = ps[c % 2][:, t0:t0 + m] if m == P else ps[2 + c % 2][:, 0:m]
                            mm = pe.transpose(dst, xnat[0:m, tt, c * P:c * P + P], ident[0:m, 0:m])
                        mm.then_inc(S("x_turned"), 1)

                @block.scalar
                def _(act):
                    for c in range(KC):
                        act.wait_ge(S("x_turned"), c + 1)
                        act.activation(xT[:, c, 0:SEQ], ps[c % 2][:, :], ACT.Copy)
                        act.activation(xT[:, c, SEQ:T], ps[2 + c % 2][:, 0:NS], ACT.Copy).then_inc(S("x_taken"), 1)
                    act.wait_ge(S("lb_shifted"), 1)
                    act.activation(lbt[:, :], lbt[:, :], ACT.Exp).then_inc(S("lb_exp"), 1)

                @block.vector
                def _(dve):
                    tmp = ar.take(512)
                    l0, l1 = lbt[:, 0:512], lbt[:, 512:1024]
                    dve.wait_ge(S("lb_in"), 16)
                    vch.link(dve, dve.tensor_tensor(tmp, l0, l1, ALU.max))
                    vch.link(dve, dve.tensor_tensor(l0, l0, tmp, ALU.subtract))
                    dve.tensor_tensor(l1, l1, tmp, ALU.subtract).then_inc(S("lb_shifted"), 1)
                    dve.wait_ge(S("lb_exp"), 1)
                    vch.link(dve, dve.tensor_tensor(tmp, l0, l1, ALU.add))
                    vch.link(dve, dve.reciprocal(tmp, tmp))
                    vch.link(dve, dve.tensor_tensor(l0, l0, tmp, ALU.mult))
                    vch.link(dve, dve.tensor_tensor(l1, l1, tmp, ALU.mult))
                    vch.link(dve, dve.tensor_tensor(l1, l0, l1, ALU.add))
                    vch.link(dve, dve.tensor_tensor(l1, l1, l0, ALU.subtract))
                    vch.link(dve, dve.tensor_tensor(l0, l0, l0, ALU.subtract))

        part(prologue)
        with nc.Block() as block:
            @block.sync
            def _(sp):
                sp.sem_clear(S("dve_step"))
        vch.n = 0

        def rms_stage(gain, uses, l, prologue):
            ar = Arena(arena)
            rstd = ar.take(T)
            with nc.Block() as block:
                @block.sync
                def _(sp):
                    if prologue:
                        lay = bass.ds(l, 1)

                        def col(name):
                            return inp[name][lay].rearrange("o (c p) -> p (o c)", p=P)

                        def row(name):
                            a = inp[name][lay]
                            return a.broadcast_to([P, a.shape[1]])
                        with nc.allow_non_contiguous_dma(reason="small columns of parameters"):
                            sp.dma_start(g1, col("norm1_g")).then_inc(S("params_in"), 16)
                            sp.dma_start(g2, col("norm2_g")).then_inc(S("params_in"), 16)
                            sp.dma_start(cb, col("conv_b")).then_inc(S("params_in"), 16)
                            for j in range(4):
                                sp.dma_start(cw[:, j, :], inp["conv_w"][lay, j].rearrange("o (c p) -> p (o c)", p=P)).then_inc(S("params_in"), 16)
                        for dst, name in ((gq, "q_norm_g"), (gk, "k_norm_g"), (ghg, "hgrn_norm_g"), (dtb, "dt_bias"),
                                          (alog, "A_log"), (dskip, "D_skip"), (gssm, "ssm_norm_g")):
                            sp.dma_start(dst, row(name)).then_inc(S("params_in"), 16)
                        sp.wait_ge(S("params_in"), 16 * 14)
                    stream(sp, uses, l)

                @block.vector
                def _(dve):
                    dve.tensor_tensor(hT[:, :, :], xT[:, :, :], xT[:, :, :], ALU.mult).then_inc(S("sq_ready"), 1)
                    dve.wait_ge(S("rstd_ready"), 1)
                    if prologue:
                        dve.wait_ge(S("params_in"), 16 * 14)
                        vch.link(dve, dve.tensor_copy(lb, lbt[:, bass.ds(l * 512, 512)]))
                        vch.link(dve, dve.tensor_scalar(oml, lb, -1.0, 1.0, ALU.mult, ALU.add))
                    for c in range(KC):
                        dve.scalar_tensor_tensor(hT[:, c, :], xT[:, c, :], gain[:, c:c + 1], rstd[:, :], ALU.mult, ALU.mult)

                @block.tensor
                def _(pe):
                    pe.wait_ge(S("sq_ready"), 1)
                    for c in range(KC):
                        pe.matmul(ps[0][:, :], ones, hT[:, c, 0:SEQ], start=(c == 0), stop=(c == KC - 1))
                    for c in range(KC):
                        mm = pe.matmul(ps[1][:, 0:NS], ones, hT[:, c, SEQ:T], start=(c == 0), stop=(c == KC - 1))
                    mm.then_inc(S("sq_summed"), 1)

                @block.scalar
                def _(act):
                    act.wait_ge(S("sq_summed"), 1)
                    act.activation(rstd[:, 0:SEQ], ps[0][:, :], ACT.Ln, bias=eps, scale=1.0 / DM)
                    ach.link(act, act.activation(rstd[:, SEQ:T], ps[1][:, 0:NS], ACT.Ln, bias=eps, scale=1.0 / DM))
                    act.activation(rstd[:, :], rstd[:, :], ACT.Exp, scale=-0.5).then_inc(S("rstd_ready"), 1)

        def stage_a(l):
            lay = bass.ds(l, 1)
            ar = Arena(arena, 0, AN)
            vn = ar.take(5, 256)
            kTs = ar.take(2, NS)
            iwn = ar.take(5, 8)
            qT = ar.take(4, T)
            idx_at = ar.at
            ikT = ar.take(T)
            iqT = ar.take(4, T)
            keep = ar.at
            k2T = ar.take(4, T)
            kn = ar.take(5, 256)
            ikd = ar.take(5, 2, 64)
            qn = ar.take(5, 512)
            tmp = ar.take(5, 512)
            kdup = ar.take(5, 4, 2, 64)
            ssq, ssk = ar.take(5 * 8), ar.take(5 * 4)
            with nc.Block() as block:
                @block.sync
                def _(sp):
                    stream(sp, J["r1"] + 1, l)

                @block.gpsimd
                def _(pool):
                    for a in (qn, kn, vn, iwn):
                        ins = pool.memset(a[:, 4, :], 1.0)
                    ins = pool.memset(ikd[:, 4, :, :], 1.0)
                    ins.then_inc(S("a_padded"), 1)

                @block.tensor
                def _(pe):
                    proj_natural(pe, J["aq"], 512)
                    proj_natural(pe, J["akv"], 512)
                    proj_transposed(pe, J["iq"], hT, KC, range(4), lambda dc: dc * 128)
                    proj_natural(pe, J["ikiw"], 72)

                @block.scalar
                def _(act):
                    act.wait_ge(S("a_padded"), 1)
                    for job in ("aq", "akv", "iq", "ikiw"):
                        for i, (t0, m) in enumerate(tiles[:4] if job == "iq" else tiles):
                            k = kact[0]
                            act.wait_ge(S("proj_ready"), k + 1)
                            b = ps[k % 2]
                            if job == "aq":
                                ins = act.activation(qn[0:m, i, :], b[0:m, :], ACT.Copy)
                            elif job == "akv":
                                act.activation(kn[0:m, i, :], b[0:m, 0:256], ACT.Copy)
                                ins = act.activation(vn[0:m, i, :], b[0:m, 256:512], ACT.Copy)
                            elif job == "iq":
                                act.activation(iqT[:, i, 0:SEQ], b[:, :], ACT.Copy)
                                ins = act.activation(iqT[:, i, SEQ:T], ps[2 + k % 2][:, 0:NS], ACT.Copy)
                            else:
                                for u in range(2):
                                    act.activation(ikd[0:m, i, u, :], b[0:m, 0:64], ACT.Copy)
                                ins = act.activation(iwn[0:m, i, :], b[0:m, 64:72], ACT.Copy, scale=8 ** -0.5)
                            ins.then_inc(S("proj_taken"), 1)
                            kact[0] += 1
            with nc.Block() as block:
                @block.vector
                def _(dve):
                    for a, nh, ss, g, sem in ((qn, 8, ssq, gq, "q"), (kn, 4, ssk, gk, "k")):
                        a2 = a.rearrange("p t (h d) -> p (t h) d", d=64)
                        t2 = tmp.rearrange("p t n -> p (t n)")[:, 0:5 * nh * 64].rearrange("p (g d) -> p g d", d=64)
                        vch.link(dve, dve.tensor_tensor(t2, a2, a2, ALU.mult))
                        dve.tensor_reduce(ss, t2, AX, ALU.add).then_inc(S("qk_sq"), 1)
                        dve.wait_ge(S("qk_rstd"), 1 if sem == "q" else 2)
                        vch.link(dve, dve.tensor_tensor(a2, a2, bc(ss, 2, 64), ALU.mult))
                        dve.tensor_tensor(a2, a2, bc(g, 1, 5 * nh), ALU.mult).then_inc(S(sem + "_normed"), 1)
                    dve.wait_ge(S("k_normed"), 1)
                    for u in range(2):
                        ins = dve.tensor_copy(kdup[:, :, :, u, :], kn.rearrange("p t (h d) -> p t h d", d=64))
                        ins.then_inc(S("k_doubled"), 1)

                @block.scalar
                def _(act):
                    for i, ss in enumerate((ssq, ssk)):
                        act.wait_ge(S("qk_sq"), i + 1)
                        ach.link(act, act.activation(ss, ss, ACT.Ln, bias=eps, scale=1.0 / 64))
                        act.activation(ss, ss, ACT.Exp, scale=-0.5).then_inc(S("qk_rstd"), 1)
                    for g in range(10):
                        act.wait_ge(S("a_turned"), g + 1)
                        if g < 9:
                            dst = qT[:, g] if g < 4 else k2T[:, g - 4] if g < 8 else ikT
                            act.activation(dst[:, 0:SEQ], ps[g % 2][:, :], ACT.Copy)
                            ins = act.activation(dst[:, SEQ:T], ps[2 + g % 2][:, 0:NS], ACT.Copy)
                        else:
                            ins = act.activation(kTs, ps[4][:, 0:2 * NS].rearrange("p (j t) -> p j t", j=2), ACT.Copy)
                        ins.then_inc(S("a_turn_taken"), 1)

                @block.tensor
                def _(pe):
                    pe.wait_ge(S("q_normed"), 1)
                    for g in range(10):
                        if g == 4:
                            pe.wait_ge(S("k_doubled"), 2)
                        if g >= 2:
                            pe.wait_ge(S("a_turn_taken"), g - 1)
                        if g == 9:
                            for j in range(2):
                                mm = pe.transpose(ps[4][:, j * NS:j * NS + NS], kn[0:NS, 4, j * P:j * P + P], ident[0:NS, 0:NS])
                            mm.then_inc(S("a_turned"), 1)
                            continue
                        for i, (t0, m) in enumerate(tiles):
                            if g < 4:
                                src = qn[0:m, i, g * P:g * P + P]
                            elif g < 8:
                                src = kdup[0:m, i, g - 4].rearrange("p u d -> p (u d)")
                            else:
                                src = ikd[0:m, i].rearrange("p u d -> p (u d)")
                            dst = ps[g % 2][:, t0:t0 + m] if m == P else ps[2 + g % 2][:, 0:m]
                            mm = pe.transpose(dst, src, ident[0:m, 0:m])
                        mm.then_inc(S("a_turned"), 1)

                @block.sync
                def _(sp):
                    def rows(name):
                        return out[name][lay].rearrange("o b (t p) h d -> p (o b t) (h d)", p=P)
                    sp.wait_ge(S("k_normed"), 1)
                    sp.dma_start(rows("k_prompt"), kn[:, 0:4, :]).then_inc(S("a_stored"), 16)
                    sp.dma_start(rows("v_prompt"), vn[:, 0:4, :]).then_inc(S("a_stored"), 16)
                    sp.dma_start(out["kidx_prompt"][lay].rearrange("o b (t p) d -> p (o b t) d", p=P), ikd[:, 0:4, 0, :]).then_inc(S("a_stored"), 16)
                    sp.dma_start(out["k_sample"][lay].rearrange("o b t h d -> (o b t) (h d)"), kn[0:NS, 4, :]).then_inc(S("a_stored"), 16)
                    sp.dma_start(out["v_sample"][lay].rearrange("o b t h d -> (o b t) (h d)"), vn[0:NS, 4, :]).then_inc(S("a_stored"), 16)
                    sp.dma_start(out["kidx_sample"][lay].rearrange("o b t d -> (o b t) d"), ikd[0:NS, 4, 0, :]).then_inc(S("a_stored"), 16)
                    sp.wait_ge(S("a_stored"), 96)

            ar = Arena(arena, keep + 4 * T, AN)
            R = ar.take(2, 512)
            score, work, bias = ar.take(512), ar.take(512), ar.take(512)
            m8 = ar.take(2, 8)
            St, Pr = ar.take(2, 512), ar.take(2, 512)
            PT = ar.take(2, 512)
            on = ar.take(2, 512)
            mx, sm = ar.take(2, 8), ar.take(2, 8)
            with nc.Block() as block:
                @block.tensor
                def _(pe):
                    for i in range(NT):
                        L = (i + 1) * P
                        q0 = i * P
                        for h in range(8):
                            n = i * 8 + h
                            r = (h % 2) * 64
                            if n >= 2:
                                pe.wait_ge(S("idx_relu"), n - 1)
                            pe.matmul(ps[n % 2][:, 0:L], iqT[r:r + 64, h // 2, q0:q0 + P], ikT[r:r + 64, 0:L]).then_inc(S("idx_logits"), 1)

                        def scores(h):
                            n = i * 8 + h
                            r = (h % 2) * 64
                            if n >= 2:
                                pe.wait_ge(S("att_biased"), n - 1)
                            pe.matmul(ps[2 + n % 2][:, 0:L], qT[r:r + 64, h // 2, q0:q0 + P], k2T[r:r + 64, h // 2, 0:L]).then_inc(S("att_scores"), 1)

                        def values(h):
                            n = i * 8 + h
                            if n >= 2:
                                pe.wait_ge(S("probT_taken"), n - 1)
                            pe.wait_ge(S("att_probs"), n + 1)
                            for s in range(i + 1):
                                mm = pe.transpose(ps[4 + n % 2][:, s * P:s * P + P], Pr[:, n % 2, s * P:s * P + P], ident)
                            mm.then_inc(S("probT_ready"), 1)
                            pe.wait_ge(S("probT_taken"), n + 1)
                            if h == 0 and i >= 2:
                                pe.wait_ge(S("att_out"), 8 * (i - 1))
                            for s in range(i + 1):
                                mm = pe.matmul(ps[6][:, h * 64:h * 64 + 64], PT[:, n % 2, s * P:s * P + P],
                                               vn[:, s, (h // 2) * 64:(h // 2) * 64 + 64], start=(s == 0), stop=(s == i))
                            mm.then_inc(S("att_values"), 1)
                            pe.wait_ge(S("att_out"), n + 1)
                        scores(0)
                        for h in range(8):
                            if h < 7:
                                scores(h + 1)
                            values(h)
                        if i >= 1:
                            pe.wait_ge(S("att_turn_taken"), i)
                        for c in range(4):
                            mm = pe.transpose(ps[7][:, c * P:c * P + P], on[:, i % 2, c * P:c * P + P], ident)
                        mm.then_inc(S("att_turned"), 1)

                @block.scalar
                def _(act):
                    for i in range(NT):
                        L = (i + 1) * P
                        for h in range(8):
                            n = i * 8 + h
                            act.wait_ge(S("idx_logits"), n + 1)
                            if n >= 2:
                                act.wait_ge(S("idx_summed"), n - 1)
                            act.activation(R[:, n % 2, 0:L], ps[n % 2][:, 0:L], ACT.Relu, scale=0.125).then_inc(S("idx_relu"), 1)
                        for h in range(8):
                            n = i * 8 + h
                            act.wait_ge(S("att_max"), n + 1)
                            if n >= 2:
                                act.wait_ge(S("probT_ready"), n - 1)
                            act.activation(Pr[:, n % 2, 0:L], St[:, n % 2, 0:L], ACT.Exp, bias=mx[:, n % 2, 0:1],
                                           accum_out=sm[:, n % 2, 0:1]).then_inc(S("att_probs"), 1)
                            act.wait_ge(S("probT_ready"), n + 1)
                            if n >= 2:
                                act.wait_ge(S("att_values"), n - 1)
                            act.activation(PT[:, n % 2, 0:L], ps[4 + n % 2][:, 0:L], ACT.Copy).then_inc(S("probT_taken"), 1)
                        act.wait_ge(S("att_turned"), i + 1)
                        act.activation(brT[:, 0:4, i * P:i * P + P], ps[7][:, :].rearrange("p (c t) -> p c t", c=4), ACT.Copy).then_inc(S("att_turn_taken"), 1)

                @block.vector
                def _(dve):
                    for i in range(NT):
                        L = (i + 1) * P
                        dve.wait_ge(S("idx_relu"), i * 8 + 1)
                        vch.link(dve, dve.memset(score[:, 0:L], 0.0))
                        for h in range(8):
                            n = i * 8 + h
                            dve.wait_ge(S("idx_relu"), n + 1)
                            ins = dve.scalar_tensor_tensor(score[:, 0:L], R[:, n % 2, 0:L], iwn[:, i, h:h + 1],
                                                           score[:, 0:L], ALU.mult, ALU.add)
                            ins.then_inc(S("idx_summed"), 1)
                            dve.wait_ge(S("idx_summed"), n + 1)
                        vch.link(dve, dve.tensor_tensor(score[:, L - P:L], score[:, L - P:L], K("neg"), ALU.add))
                        topk(dve, score[:, 0:L], work[:, 0:L], bias[:, 0:L], m8, TOPK_P if L > TOPK_P else L)
                        vch.link(dve, dve.tensor_tensor(bias[:, L - P:L], bias[:, L - P:L], K("neg"), ALU.add))
                        for h in range(8):
                            n = i * 8 + h
                            dve.wait_ge(S("att_scores"), n + 1)
                            if n >= 2:
                                dve.wait_ge(S("att_probs"), n - 1)
                            dve.scalar_tensor_tensor(St[:, n % 2, 0:L], ps[2 + n % 2][:, 0:L], 0.125, bias[:, 0:L],
                                                     ALU.mult, ALU.add).then_inc(S("att_biased"), 1)
                            dve.wait_ge(S("att_biased"), n + 1)
                            dve.tensor_reduce(mx[:, n % 2, 0:1], St[:, n % 2, 0:L], AX, ALU.max, negate=True).then_inc(S("att_max"), 1)
                            dve.wait_ge(S("att_probs"), n + 1)
                            vch.link(dve, dve.reciprocal(sm[:, n % 2, 1:2], sm[:, n % 2, 0:1]))
                            dve.wait_ge(S("att_values"), n + 1)
                            if h == 0 and i >= 2:
                                dve.wait_ge(S("att_turned"), i - 1)
                            dve.tensor_scalar(on[:, i % 2, h * 64:h * 64 + 64], ps[6][:, h * 64:h * 64 + 64],
                                              sm[:, n % 2, 1:2], None, ALU.mult).then_inc(S("att_out"), 1)
            stage_a_sample(l, idx_at, keep, vn, kTs, iwn, qT, ikT, iqT)

        def topk(dve, score, work, bias, m8, k):
            if k >= score.shape[1]:
                vch.link(dve, dve.memset(bias, 0.0))
                return
            for r in range(k // 8):
                src = score if r == 0 else work
                m = m8[0:score.shape[0], r % 2, :]
                vch.link(dve, dve.max(m, src))
                vch.link(dve, dve.match_replace(work, m, src, TAKEN))
            vch.link(dve, dve.tensor_scalar(bias, work, TAKEN, NEG, ALU.not_equal, ALU.mult))

        def stage_a_sample(l, idx_at, keep, vn, kTs, iwn, qT, ikT, iqT):
            lay = bass.ds(l, 1)
            ar = Arena(arena, keep, AN)
            bias = ar.take(LK)
            keep2 = ar.at
            score, work = ar.take(LK), ar.take(LK)
            iqh = ar.take(8, 8, 4)
            IQP = ar.take(8, 4, 32)
            kx = ar.take(4, 4, 64)
            ikc = ar.take(2, 512)
            R = ar.take(2, 512)
            WS = ar.take(2, NS)
            w8, wcol = ar.take(2, 8), ar.take(2)
            m8 = ar.take(2, 8)
            steps = [(g, c, bb) for g in range(2) for c in range(4) for bb in range(4)]
            with nc.Block() as block:
                @block.sync
                def _(sp):
                    for s, (g, c, bb) in enumerate(steps):
                        if s >= 4:
                            sp.wait_ge(S("kidx_turned"), s - 3)
                        for pg in range(4):
                            at = (4 * g + bb) * NPG + 4 * c + pg
                            page = sp.value_load(ptab[0:1, at:at + 1], min_val=0, max_val=inp["cache_kidx"].shape[1] - 1)
                            sp.dma_start(kx[:, s % 4, pg, :], inp["cache_kidx"][lay, bass.ds(page, 1)].rearrange("o q t d -> (o q t) d")).then_inc(S(f"kidx_in{s % 4}"), 16)

                @block.tensor
                def _(pe):
                    for g in range(2):
                        mm = pe.matmul(ps[6][:, g * 8:g * 8 + 8], K("rep")[0:NS, g * P:g * P + P], iwn[0:NS, 4, :])
                    mm.then_inc(S("w_spread"), 1)
                    pe.wait_ge(S("iq_padded"), 1)
                    pe.wait_ge(S("wsel_ready"), 1)

                    def turn(s):
                        pe.wait_ge(S(f"kidx_in{s % 4}"), 64 * (s // 4 + 1))
                        if s >= 2:
                            pe.wait_ge(S("ikc_ready"), s - 1)
                        for pg in range(4):
                            mm = pe.transpose(ps[s % 2][0:64, pg * P:pg * P + P], kx[:, s % 4, pg, :], ident)
                        mm.then_inc(S("kidx_turned"), 1)

                    def weigh(u, w):
                        pe.wait_ge(S("sidx_relu"), u + 1)
                        if u >= 2:
                            pe.wait_ge(S("sidx_taken"), u - 1)
                        pe.matmul(ps[4 + u % 2][0:NS, 0:w], WS[:, u // 5, :], R[:, u % 2, 0:w]).then_inc(S("sidx_weighed"), 1)

                    turn(0)
                    for g in range(2):
                        for c in range(5):
                            u = g * 5 + c
                            if u >= 2:
                                pe.wait_ge(S("sidx_relu"), u - 1)
                            for bb in range(4):
                                if c < 4:
                                    s = (g * 4 + c) * 4 + bb
                                    if s + 1 < len(steps):
                                        turn(s + 1)
                                    pe.wait_ge(S("ikc_ready"), s + 1)
                                    mm = pe.matmul(ps[2 + u % 2][:, :], IQP[0:64, 4 * g + bb].rearrange("p a n -> p (a n)"),
                                                   ikc[0:64, s % 2, :], start=(bb == 0), stop=(bb == 3))
                                    if bb < 3:
                                        mm.then_inc(S("ikc_used"), 1)
                                else:
                                    mm = pe.matmul(ps[2 + u % 2][:, 0:NS], IQP[0:64, 4 * g + bb].rearrange("p a n -> p (a n)"),
                                                   ikT[0:64, SEQ:T], start=(bb == 0), stop=(bb == 3))
                            mm.then_inc(S("sidx_logits"), 1)
                            if u >= 1:
                                weigh(u - 1, NS if (u - 1) % 5 == 4 else 512)
                    weigh(9, NS)

                @block.scalar
                def _(act):
                    for g in range(2):
                        for c in range(5):
                            u = g * 5 + c
                            if c < 4:
                                for bb in range(4):
                                    s = u // 5 * 16 + c * 4 + bb
                                    act.wait_ge(S("kidx_turned"), s + 1)
                                    if s >= 2:
                                        q = s - 2
                                        act.wait_ge(S("ikc_used"), q // 4 * 3 + min(q % 4 + 1, 3))
                                        if q % 4 == 3:
                                            act.wait_ge(S("sidx_logits"), q // 16 * 5 + q % 16 // 4 + 1)
                                    act.activation(ikc[0:64, s % 2, :], ps[s % 2][0:64, :], ACT.Copy).then_inc(S("ikc_ready"), 1)
                            w = 512 if c < 4 else NS
                            act.wait_ge(S("sidx_logits"), u + 1)
                            if u >= 2:
                                act.wait_ge(S("sidx_weighed"), u - 1)
                            act.activation(R[:, u % 2, 0:w], ps[2 + u % 2][:, 0:w], ACT.Relu, scale=0.125).then_inc(S("sidx_relu"), 1)

                @block.vector
                def _(dve):
                    for h in range(8):
                        r = (h % 2) * 64
                        ins = dve.tensor_copy(iqh[0:64, :, h, :], iqT[r:r + 64, h // 2, SEQ:T].rearrange("p (b t) -> p b t", b=NB))
                    vch.link(dve, ins)
                    bb = K("bb").rearrange("p (a b) -> p a b", a=4)
                    for b in range(NB):
                        ins = dve.tensor_tensor(IQP[0:64, b], bc(iqh[0:64, b].rearrange("p h t -> p (h t)"), 1, 4),
                                                bc(bb[0:64, b % 4], 2, 32), ALU.mult)
                    ins.then_inc(S("iq_padded"), 1)
                    dve.wait_ge(S("w_spread"), 1)
                    for g in range(2):
                        vch.link(dve, dve.tensor_tensor(w8[:, g, :], ps[6][:, g * 8:g * 8 + 8], K("hsel"), ALU.mult))
                        vch.link(dve, dve.tensor_reduce(wcol[:, g:g + 1], w8[:, g, :], AX, ALU.add))
                        ins = dve.tensor_scalar(WS[:, g, :], K("wsel")[:, g * NS:g * NS + NS], wcol[:, g:g + 1], None, ALU.mult)
                    ins.then_inc(S("wsel_ready"), 1)
                    for u in range(10):
                        c, w = u % 5, (512 if u % 5 < 4 else NS)
                        dst = score[0:NS, c * 512:c * 512 + w]
                        dve.wait_ge(S("sidx_weighed"), u + 1)
                        if u < 5:
                            dve.tensor_copy(dst, ps[4 + u % 2][0:NS, 0:w]).then_inc(S("sidx_taken"), 1)
                        else:
                            dve.wait_ge(S("sidx_taken"), u - 4)
                            dve.tensor_tensor(dst, dst, ps[4 + u % 2][0:NS, 0:w], ALU.add).then_inc(S("sidx_taken"), 1)
                    dve.wait_ge(S("sidx_taken"), 10)
                    vch.link(dve, dve.tensor_tensor(score[0:NS, PAST:LK], score[0:NS, PAST:LK], K("neg_s")[0:NS], ALU.add))
                    topk(dve, score[0:NS], work[0:NS], bias[0:NS], m8, TOPK_S)
                    dve.tensor_tensor(bias[0:NS, PAST:LK], bias[0:NS, PAST:LK], K("neg_s")[0:NS], ALU.add)
            ar = Arena(arena, idx_at, keep)
            kp = ar.take(2, 4, 256)
            ar = Arena(arena, keep2, AN)
            QP = ar.take(8, 2, 4, 32)
            qz = ar.take(2, 8, 8, 4)
            KT = ar.take(2, 2, 512)
            St = ar.take(LK)
            PT = ar.take(17, P)
            vp = ar.take(2, 4, 256)
            mx, sm = ar.take(2), ar.take(4)

            def load_pages(sp, dst, name, b, c, sem):
                for pg in range(4):
                    at = b * NPG + 4 * c + pg
                    page = sp.value_load(ptab[0:1, at:at + 1], min_val=0, max_val=inp[name].shape[1] - 1)
                    sp.dma_start(dst[:, pg, :], inp[name][lay, bass.ds(page, 1)].rearrange("o q t g d -> (o q t) (g d)")).then_inc(S(sem), 16)

            with nc.Block() as block:
                @block.sync
                def _(sp):
                    for g in range(2):
                        for x in range(16):
                            s = 16 * g + x
                            if s >= 2:
                                sp.wait_ge(S("k_turned"), s - 1)
                            load_pages(sp, kp[:, s % 2], "cache_k", 4 * g + x % 4, x // 4, f"kpage_in{s % 2}")
                        for s in range(16 * g, 16 * g + 16):
                            if s >= 2:
                                sp.wait_ge(S("v_used"), s - 1)
                            load_pages(sp, vp[:, s % 2], "cache_v", s // 4, s % 4, f"vpage_in{s % 2}")

                @block.gpsimd
                def _(pool):
                    pool.memset(qz, 0.0).then_inc(S("qz_zero"), 1)

                @block.tensor
                def _(pe):
                    pe.wait_ge(S("q_padded"), 1)

                    def turn(s):
                        pe.wait_ge(S(f"kpage_in{s % 2}"), 64 * (s // 2 + 1))
                        if s >= 2:
                            pe.wait_ge(S("kt_ready"), s - 1)
                        for j in range(2):
                            for pg in range(4):
                                mm = pe.transpose(ps[(s % 2) * 2 + j][:, pg * P:pg * P + P], kp[:, s % 2, pg, j * P:j * P + P], ident)
                        mm.then_inc(S("k_turned"), 1)

                    for g in range(2):
                        turn(16 * g)
                        for c in range(5):
                            u = g * 10 + c
                            w = 512 if c < 4 else NS
                            if u >= 2:
                                pe.wait_ge(S("sa_taken"), u - 1)
                            for bb in range(4):
                                b = 4 * g + bb
                                s = g * 16 + c * 4 + bb
                                if c < 4:
                                    if (s + 1) % 16:
                                        turn(s + 1)
                                    pe.wait_ge(S("kt_ready"), s + 1)
                                for j in range(2):
                                    rhs = KT[:, s % 2, j, :] if c < 4 else kTs[:, j, :]
                                    mm = pe.matmul(ps[4 + u % 2][:, 0:w], QP[:, b, j].rearrange("p a n -> p (a n)"), rhs,
                                                   start=(bb == 0 and j == 0), stop=False)
                                if c < 4:
                                    mm.then_inc(S("kt_used"), 1)
                            pe.matmul(ps[4 + u % 2][:, 0:w], K("rep")[0:NS, g * P:g * P + P], bias[0:NS, c * 512:c * 512 + w],
                                      start=False, stop=True).then_inc(S("sa_ready"), 1)
                        for qd in range(5):
                            u = g * 10 + 5 + qd
                            pe.wait_ge(S("sa_taken"), u - 1)
                            pe.wait_ge(S("sprobs_ready"), g + 1)
                            for x in range(4 if qd < 4 else 1):
                                kt = qd * 4 + x
                                m = P if kt < 16 else NS
                                mm = pe.transpose(ps[4 + u % 2][0:m, x * P:x * P + P], St[:, kt * P:kt * P + m], ident)
                            mm.then_inc(S("sa_ready"), 1)
                        pe.wait_ge(S("sa_taken"), g * 10 + 10)
                        for bb in range(4):
                            b = 4 * g + bb
                            for c in range(4):
                                sv = b * 4 + c
                                pe.wait_ge(S(f"vpage_in{sv % 2}"), 64 * (sv // 2 + 1))
                                for pg in range(4):
                                    for j in range(2):
                                        col = bb * 32 + j * 16
                                        mm = pe.matmul(ps[6 + j][:, b * 16:b * 16 + 16], vp[:, sv % 2, pg, j * P:j * P + P],
                                                       PT[:, c * 4 + pg, col:col + 16], start=(c == 0 and pg == 0), stop=False)
                                mm.then_inc(S("v_used"), 1)
                            for j in range(2):
                                col = bb * 32 + j * 16
                                mm = pe.matmul(ps[6 + j][:, b * 16:b * 16 + 16], vn[0:NS, 4, j * P:j * P + P],
                                               PT[0:NS, 16, col:col + 16], start=False, stop=True)
                        mm.then_inc(S("sv_done"), 1)

                @block.scalar
                def _(act):
                    for g in range(2):
                        for c in range(5):
                            u = g * 10 + c
                            w = 512 if c < 4 else NS
                            if c < 4:
                                for bb in range(4):
                                    s = g * 16 + c * 4 + bb
                                    act.wait_ge(S("k_turned"), s + 1)
                                    if s >= 2:
                                        act.wait_ge(S("kt_used"), s - 1)
                                    for j in range(2):
                                        ins = act.activation(KT[:, s % 2, j, :], ps[(s % 2) * 2 + j][:, :], ACT.Copy)
                                    ins.then_inc(S("kt_ready"), 1)
                            act.wait_ge(S("sa_ready"), u + 1)
                            act.activation(St[:, c * 512:c * 512 + w], ps[4 + u % 2][:, 0:w], ACT.Copy, scale=0.125).then_inc(S("sa_taken"), 1)
                        act.wait_ge(S("smax_ready"), g + 1)
                        act.activation(St[:, :], St[:, :], ACT.Exp, bias=mx[:, g:g + 1], accum_out=sm[:, g:g + 1]).then_inc(S("sexp_ready"), 1)
                        if g == 1:
                            act.wait_ge(S("sv_done"), 1)
                        for qd in range(5):
                            u = g * 10 + 5 + qd
                            act.wait_ge(S("sa_ready"), u + 1)
                            if qd < 4:
                                ins = act.activation(PT[:, qd * 4:qd * 4 + 4, :], ps[4 + u % 2][:, :].rearrange("p (a n) -> p a n", a=4), ACT.Copy)
                            else:
                                ins = act.activation(PT[0:NS, 16, :], ps[4 + u % 2][0:NS, 0:P], ACT.Copy)
                            ins.then_inc(S("sa_taken"), 1)

                @block.vector
                def _(dve):
                    dve.wait_ge(S("qz_zero"), 1)
                    for h in range(8):
                        r, j, g2 = (h % 2) * 64, h // 4, (h // 2) % 2
                        ins = dve.tensor_copy(qz[g2 * 64:g2 * 64 + 64, j, :, h, :], qT[r:r + 64, h // 2, SEQ:T].rearrange("p (b t) -> p b t", b=NB))
                    vch.link(dve, ins)
                    bb = K("bb").rearrange("p (a b) -> p a b", a=4)
                    for b in range(NB):
                        for j in range(2):
                            ins = dve.tensor_tensor(QP[:, b, j], bc(qz[:, j, b].rearrange("p h t -> p (h t)"), 1, 4),
                                                    bc(bb[:, b % 4], 2, 32), ALU.mult)
                    ins.then_inc(S("q_padded"), 1)
                    for g in range(2):
                        dve.wait_ge(S("sa_taken"), g * 10 + 5)
                        dve.tensor_reduce(mx[:, g:g + 1], St[:, :], AX, ALU.max, negate=True).then_inc(S("smax_ready"), 1)
                        dve.wait_ge(S("sexp_ready"), g + 1)
                        vch.link(dve, dve.reciprocal(sm[:, 2 + g:3 + g], sm[:, g:g + 1]))
                        dve.tensor_scalar(St[:, :], St[:, :], sm[:, 2 + g:3 + g], None, ALU.mult).then_inc(S("sprobs_ready"), 1)
                    dve.wait_ge(S("sv_done"), 2)
                    for h in range(8):
                        r, j, g2 = (h % 2) * 64, h // 4, (h // 2) % 2
                        src = ps[6 + j][g2 * 64:g2 * 64 + 64, 0:128].rearrange("p (b h t) -> p b h t", b=NB, h=4)[:, :, h % 4, :]
                        dve.tensor_copy(brT[r:r + 64, h // 2, SEQ:T].rearrange("p (b t) -> p b t", b=NB), src)

        GAMMA = [1.0 - 2.0 ** (-5 - h) for h in range(4)]

        def stage_linear(l, kind):
            lay = bass.ds(l, 1)
            ret = kind == "r"
            br0 = 4 if ret else 8

            def Z(name):
                return S(kind + "_" + name)

            ar = Arena(arena, 0, AN)
            sc = Arena(brT_, 12 * T, 16 * T)
            q, k, v, g = (ar.take(5, 512) for _ in range(4))
            sf = None if ret else ar.take(5, 512)
            S0 = ar.take(NB, 4, P)
            Sp = ar.take(4, P)
            qT, kT, A = sc.take(4 * P), sc.take(4 * P), sc.take(4 * P)
            kd = sc.take(512)
            t1 = ar.take(512)
            t2 = ar.take(512)
            E = ar.take(512)
            sm = ar.take(3, 4)
            dec = ar.take(NB, 4)
            if ret:
                Vx = ar.take(NB, P)
                qm = ar.take(NB, NS)
                qr, kr = ar.take(512), ar.take(512)
            else:
                lf = sf
                qmC = q[:, 0, 0:256].rearrange("p (b t) -> p b t", b=NB)
                VxC = q[:, 1:3, :].rearrange("p t n -> p (t n)").rearrange("p (b e) -> p b e", b=NB)
            with nc.Block() as block:
                @block.sync
                def _(sp):
                    stream(sp, J["r3" if ret else "c3"] + 3, l)
                    name = "state_ret" if ret else "state_hgrn"
                    for b in range(0, NB, 2):
                        sp.dma_start(S0[:, b:b + 2].rearrange("p b h e -> p (b h) e"),
                                     inp[name][lay, b:b + 2].rearrange("o b h d e -> d (o b h) e")).then_inc(Z("state_in"), 16)

                @block.tensor
                def _(pe):
                    for i in range(4):
                        proj_natural(pe, J[f"{kind}{i}"], 512)

                @block.scalar
                def _(act):
                    for i in range(4):
                        for tt, (t0, m) in enumerate(tiles):
                            n = kact[0]
                            act.wait_ge(S("proj_ready"), n + 1)
                            b = ps[n % 2][0:m, :]
                            if ret:
                                ins = act.activation((q, k, v, g)[i][0:m, tt, :], b, ACT.Silu if i == 3 else ACT.Copy)
                            elif i == 1:
                                act.activation(sf[0:m, tt, :], b, ACT.Sigmoid)
                                ins = act.activation(k[0:m, tt, :], b, ACT.Sigmoid, scale=-1.0)
                            else:
                                ins = act.activation((q, k, v, g)[i][0:m, tt, :], b, ACT.Copy if i == 2 else ACT.Silu)
                            ins.then_inc(S("proj_taken"), 1)
                            kact[0] += 1
            nlv = [7, 7, 7, 7, 2]
            lv0 = [0, 7, 14, 21, 28]
            with nc.Block() as block:
                @block.tensor
                def _(pe):
                    for i, (t0, m) in enumerate(tiles):
                        last = i == 4
                        triu, aft = (K("tri_s")[0:NS], K("after_s")[0:NS]) if last else (tri, after)
                        if i >= 1:
                            pe.wait_ge(Z("y_taken"), i)
                        if not ret:
                            pe.wait_ge(Z("logf"), i + 1)
                            pe.matmul(ps[3][0:m, :], triu, lf[0:m, i, :])
                            mm = pe.matmul(ps[4][0:m, :], aft, lf[0:m, i, :])
                            for h in range(4):
                                w = lf[0:m, i, h * P:h * P + P]
                                if last:
                                    mm = pe.matmul(ps[5][:, h * NB:h * NB + NB], w, K("seqhot")[0:NS])
                                else:
                                    mm = pe.matmul(ps[5][:, h:h + 1], w, ones[:, 0:1])
                            mm.then_inc(Z("cum"), 1)
                            for x in range(nlv[i]):
                                n = lv0[i] + x
                                pe.matmul(ps[0][0:m, :], K("lv_sum").rearrange("p (l t) -> p l t", l=7)[0:m, x, 0:m], lf[0:m, i, :]).then_inc(Z("lv_z"), 1)
                                pe.wait_ge(Z("lv_x"), n + 1)
                                for h in range(4):
                                    mm = pe.transpose(ps[1][:, h * m:h * m + m], t2[0:m, h * P:h * P + P], ident[0:m, 0:m])
                                mm.then_inc(Z("lv_turned"), 1)
                                pe.wait_ge(Z("lv_turn_taken"), n + 1)
                                if n >= 1:
                                    pe.wait_ge(Z("lv_added"), n)
                                for h in range(4):
                                    xT_h = kT[:, h * m:h * m + m]
                                    mm = pe.matmul(ps[2][0:m, h * m:h * m + m], xT_h, xT_h)
                                mm.then_inc(Z("lv_product"), 1)
                        pe.wait_ge(Z("qk_ready" if ret else "weights"), i + 1)
                        for h in range(4):
                            mm = pe.transpose(ps[0][:, h * m:h * m + m], (qr if ret else t1)[0:m, h * P:h * P + P], ident[0:m, 0:m])
                        if ret:
                            for h in range(4):
                                mm = pe.transpose(ps[1][:, h * m:h * m + m], kr[0:m, h * P:h * P + P], ident[0:m, 0:m])
                        mm.then_inc(Z("turned"), 1)
                        pe.wait_ge(Z("turn_taken"), i + 1)
                        if ret:
                            for h in range(4):
                                mm = pe.matmul(ps[2][0:m, h * m:h * m + m], kT[:, h * m:h * m + m], qT[:, h * m:h * m + m])
                            mm.then_inc(Z("scores"), 1)
                        pe.wait_ge(Z("weights"), i + 1)
                        if last:
                            pe.wait_ge(Z("state_in"), 64)
                        for h in range(4):
                            o = ps[6][0:m, h * P:h * P + P]
                            mm = pe.matmul(o, A[0:m, h * m:h * m + m], v[0:m, i, h * P:h * P + P], start=True, stop=(i == 0))
                            if last:
                                pe.wait_ge(Z("q_masked"), h + 1)
                                for b in range(NB):
                                    mm = pe.matmul(o, (qm if ret else qmC)[:, b, :], S0[:, b, h, :], start=False, stop=(b == NB - 1))
                                mm.then_inc(Z("q_mask_used"), 1)
                            elif i > 0:
                                mm = pe.matmul(o, qT[:, h * m:h * m + m], Sp[:, h, :], start=False, stop=True)
                        if not last:
                            for h in range(4):
                                mm = pe.matmul(ps[7][:, h * P:h * P + P], kd[0:m, h * P:h * P + P], v[0:m, i, h * P:h * P + P])
                            mm.then_inc(Z("out"), 1)
                        else:
                            for h in range(4):
                                pe.wait_ge(Z("v_masked"), h + 1)
                                for half in range(2):
                                    n = 2 * h + half
                                    if n >= 2:
                                        pe.wait_ge(Z("state_new"), n - 1)
                                    pe.matmul(ps[3 + n % 2][:, :], kd[0:NS, h * P:h * P + P],
                                              (Vx if ret else VxC)[0:NS, half * 4:half * 4 + 4, :].rearrange("p b e -> p (b e)")).then_inc(Z("state_add"), 1)
                        pe.wait_ge(Z("y"), i + 1)
                        for h in range(4):
                            mm = pe.transpose(ps[5][:, h * m:h * m + m], t2[0:m, h * P:h * P + P], ident[0:m, 0:m])
                        mm.then_inc(Z("y_turned"), 1)

                @block.scalar
                def _(act):
                    for i, (t0, m) in enumerate(tiles):
                        last = i == 4
                        if not ret:
                            act.wait_ge(Z("forget"), i + 1)
                            act.activation(t1[0:m, :], t1[0:m, :], ACT.Ln)
                            act.activation(t2[0:m, :], t2[0:m, :], ACT.Ln).then_inc(Z("logs"), 1)
                            act.wait_ge(Z("cum"), i + 1)
                            act.activation(E[0:m, :], ps[3][0:m, :], ACT.Exp)
                            act.activation(t1[0:m, :], ps[4][0:m, :], ACT.Exp)
                            if last:
                                ins = act.activation(dec, ps[5][:, 0:4 * NB].rearrange("p (h b) -> p b h", h=4), ACT.Exp)
                            else:
                                ins = act.activation(dec[:, 0, :], ps[5][:, 0:4], ACT.Exp)
                            ins.then_inc(Z("decays"), 1)
                            for x in range(nlv[i]):
                                n = lv0[i] + x
                                act.wait_ge(Z("lv_z"), n + 1)
                                act.wait_ge(Z("lv_e_free"), n + 1)
                                act.activation(E[0:m, :], ps[0][0:m, :], ACT.Exp).then_inc(Z("lv_e"), 1)
                                act.wait_ge(Z("lv_turned"), n + 1)
                                act.activation(kT[:, 0:4 * m], ps[1][:, 0:4 * m], ACT.Copy).then_inc(Z("lv_turn_taken"), 1)
                        act.wait_ge(Z("turned"), i + 1)
                        if ret:
                            act.activation(kT[:, 0:4 * m], ps[1][:, 0:4 * m], ACT.Copy)
                        act.activation(qT[:, 0:4 * m], ps[0][:, 0:4 * m], ACT.Copy).then_inc(Z("turn_taken"), 1)
                        act.wait_ge(Z("sq"), i + 1)
                        ach.link(act, act.activation(sm[0:m, 1, :], sm[0:m, 1, :], ACT.Ln, bias=eps[0:m], scale=1.0 / P))
                        act.activation(sm[0:m, 1, :], sm[0:m, 1, :], ACT.Exp, scale=-0.5).then_inc(Z("rstd"), 1)
                        act.wait_ge(Z("y_turned"), i + 1)
                        act.activation(brT[:, br0:br0 + 4, t0:t0 + m], ps[5][:, 0:4 * m].rearrange("p (h t) -> p h t", h=4), ACT.Copy).then_inc(Z("y_taken"), 1)

                @block.vector
                def _(dve):
                    hv = lambda a, m: a[0:m, :].rearrange("p (h d) -> p h d", h=4)
                    L = vch.link
                    for i, (t0, m) in enumerate(tiles):
                        last = i == 4
                        if ret:
                            cs = bc(K("cos").rearrange("p (t f) -> p t f", t=5)[0:m, i, :], 1, 4)
                            sn = bc(K("sin").rearrange("p (t f) -> p t f", t=5)[0:m, i, :], 1, 4)
                            a1, a2 = hv(t1, m)[:, :, 0:64], hv(t1, m)[:, :, 64:128]
                            if i >= 1:
                                dve.wait_ge(Z("y_turned"), i)
                            for src, dst in ((q, qr), (k, kr)):
                                x1, x2 = hv(src[:, i], m)[:, :, 0:64], hv(src[:, i], m)[:, :, 64:128]
                                y1, y2 = hv(dst, m)[:, :, 0:64], hv(dst, m)[:, :, 64:128]
                                dve.tensor_tensor(y1, x1, cs, ALU.mult)
                                dve.tensor_tensor(a1, x2, sn, ALU.mult)
                                dve.tensor_tensor(y2, x1, sn, ALU.mult)
                                L(dve, dve.tensor_tensor(a2, x2, cs, ALU.mult))
                                dve.tensor_tensor(y1, y1, a1, ALU.subtract)
                                L(dve, dve.tensor_tensor(y2, y2, a2, ALU.add))
                            L(dve, dve.tensor_tensor(hv(qr, m), hv(qr, m), bc(K("rq_s" if last else "rq")[0:m], 2, P), ALU.mult))
                            dve.tensor_tensor(hv(kd, m), hv(kr, m), bc(K("rk_s" if last else "rk")[0:m], 2, P), ALU.mult).then_inc(Z("qk_ready"), 1)
                            dve.wait_ge(Z("scores"), i + 1)
                            dve.tensor_tensor(A[0:m, 0:4 * m], ps[2][0:m, 0:4 * m], K("rdec_s" if last else "rdec")[0:m], ALU.mult).then_inc(Z("weights"), 1)
                        else:
                            qi, ki, fi = q[0:m, i, :], k[0:m, i, :], sf[0:m, i, :]
                            if i >= 1:
                                dve.wait_ge(Z("y_turned"), i)
                            L(dve, dve.tensor_tensor(fi, fi, oml[0:m], ALU.mult))
                            L(dve, dve.tensor_tensor(fi, fi, lb[0:m], ALU.add))
                            dve.tensor_scalar(t1[0:m, :], fi, 2.0 ** -60, None, ALU.max)
                            L(dve, dve.tensor_scalar(t2[0:m, :], fi, 1e-30, 2.0 ** -60, ALU.max, ALU.min))
                            dve.tensor_scalar(t2[0:m, :], t2[0:m, :], 2.0 ** 60, None, ALU.mult).then_inc(Z("forget"), 1)
                            dve.tensor_tensor(ki, ki, oml[0:m], ALU.mult)
                            L(dve, dve.tensor_scalar(qi, qi, P ** -0.5, None, ALU.mult))
                            dve.wait_ge(Z("logs"), i + 1)
                            L(dve, dve.tensor_tensor(fi, t1[0:m, :], t2[0:m, :], ALU.add))
                            dve.tensor_tensor(t2[0:m, :], qi, ki, ALU.mult).then_inc(Z("logf"), 1)
                            dve.wait_ge(Z("logf"), i + 1)
                            L(dve, dve.tensor_reduce(sm[0:m, 2, :], hv(t2, m), AX, ALU.add))
                            dve.wait_ge(Z("decays"), i + 1)
                            L(dve, dve.tensor_tensor(kd[0:m, :], ki, t1[0:m, :], ALU.mult))
                            L(dve, dve.tensor_tensor(t1[0:m, :], qi, E[0:m, :], ALU.mult))
                            L(dve, dve.tensor_tensor(qi, qi, ki, ALU.subtract))
                            dve.memset(A[0:m, 0:4 * m], 0.0).then_inc(Z("lv_e_free"), 1)
                            dve.wait_ge(Z("lv_e_free"), lv0[i] + 1)
                            for x in range(nlv[i]):
                                n = lv0[i] + x
                                L(dve, dve.scalar_tensor_tensor(t2[0:m, :], qi, K("lv_side")[0:m, x:x + 1], ki, ALU.mult, ALU.add))
                                dve.wait_ge(Z("lv_e"), n + 1)
                                dve.tensor_tensor(t2[0:m, :], t2[0:m, :], E[0:m, :], ALU.mult).then_inc(Z("lv_x"), 1)
                                dve.wait_ge(Z("lv_product"), n + 1)
                                msk = bc(K("lv_mask").rearrange("p (l t) -> p l t", l=7)[0:m, x, 0:m], 1, 4)
                                dm = t2[0:m, 0:4 * m].rearrange("p (h n) -> p h n", h=4)
                                dve.tensor_tensor(dm, ps[2][0:m, 0:4 * m].rearrange("p (h n) -> p h n", h=4), msk, ALU.mult).then_inc(Z("lv_added"), 1)
                                dve.wait_ge(Z("lv_added"), n + 1)
                                ins = dve.tensor_tensor(A[0:m, 0:4 * m], A[0:m, 0:4 * m], t2[0:m, 0:4 * m], ALU.add)
                                if x < nlv[i] - 1:
                                    ins.then_inc(Z("lv_e_free"), 1)
                                    dve.wait_ge(Z("lv_e_free"), n + 2)
                                else:
                                    ins.then_inc(Z("weights"), 1)
                        if last:
                            dve.wait_ge(Z("turn_taken"), i + 1)
                            qmv = qm if ret else qmC
                            vxv = Vx if ret else VxC
                            msk = K("qmask").rearrange("p (b t) -> p b t", b=NB)
                            for h in range(4):
                                if h >= 1:
                                    dve.wait_ge(Z("q_mask_used"), h)
                                dve.tensor_tensor(qmv, bc(qT[:, h * NS:h * NS + NS], 1, NB), msk, ALU.mult).then_inc(Z("q_masked"), 1)
                            for h in range(4):
                                if h >= 1:
                                    dve.wait_ge(Z("state_add"), 2 * h)
                                dve.tensor_tensor(vxv[0:NS], bc(v[0:NS, 4, h * P:h * P + P], 1, NB), bc(K("seqhot")[0:NS], 2, P), ALU.mult).then_inc(Z("v_masked"), 1)
                                for half in range(2):
                                    n = 2 * h + half
                                    dve.wait_ge(Z("state_add"), n + 1)
                                    if h == 0 and half == 0:
                                        dve.wait_ge(Z("q_mask_used"), 4)
                                    st = S0[:, half * 4:half * 4 + 4, h, :]
                                    add = ps[3 + n % 2][:, :].rearrange("p (b e) -> p b e", b=4)
                                    if ret:
                                        dve.scalar_tensor_tensor(st, st, GAMMA[h] ** TS, add, ALU.mult, ALU.add).then_inc(Z("state_new"), 1)
                                    else:
                                        L(dve, dve.tensor_tensor(st, st, bc(dec[:, half * 4:half * 4 + 4, h], 2, P), ALU.mult))
                                        dve.tensor_tensor(st, st, add, ALU.add).then_inc(Z("state_new"), 1)
                        else:
                            dve.wait_ge(Z("out"), i + 1)
                            for h in range(4):
                                add = ps[7][:, h * P:h * P + P]
                                if i == 0:
                                    ins = dve.tensor_copy(Sp[:, h, :], add)
                                else:
                                    ins = dve.scalar_tensor_tensor(Sp[:, h, :], Sp[:, h, :], GAMMA[h] ** P if ret else dec[:, 0, h:h + 1], add, ALU.mult, ALU.add)
                            if i == 3:
                                ins.then_inc(Z("prompt_state"), 1)
                            else:
                                L(dve, ins)
                        o = hv(ps[6], m)
                        y, w = hv(t2, m), hv(t1, m)
                        if ret:
                            L(dve, dve.tensor_reduce(sm[0:m, 0, :], o, AX, ALU.add))
                            L(dve, dve.tensor_scalar(sm[0:m, 0, :], sm[0:m, 0, :], 1.0 / P, None, ALU.mult))
                            L(dve, dve.tensor_tensor(y, o, bc(sm[0:m, 0, :], 2, P), ALU.subtract))
                        else:
                            for h in range(4):
                                ins = dve.scalar_tensor_tensor(y[:, h], hv(v[:, i], m)[:, h], sm[0:m, 2, h:h + 1], o[:, h], ALU.mult, ALU.add)
                            L(dve, ins)
                        if not ret:
                            dve.wait_ge(Z("turned"), i + 1)
                        L(dve, dve.tensor_tensor(w, y, y, ALU.mult))
                        dve.tensor_reduce(sm[0:m, 1, :], w, AX, ALU.add).then_inc(Z("sq"), 1)
                        dve.wait_ge(Z("rstd"), i + 1)
                        L(dve, dve.tensor_tensor(y, y, bc(sm[0:m, 1, :], 2, P), ALU.mult))
                        if not ret:
                            L(dve, dve.tensor_tensor(y, y, bc(ghg[0:m], 1, 4), ALU.mult))
                        dve.tensor_tensor(t2[0:m, :], t2[0:m, :], g[0:m, i, :], ALU.mult).then_inc(Z("y"), 1)

                @block.sync
                def _(sp):
                    name = "ret" if ret else "hgrn"
                    sp.wait_ge(Z("prompt_state"), 1)
                    sp.dma_start(out[name + "_prompt"][lay].rearrange("o b h d e -> d (o b h) e"), Sp).then_inc(Z("stored"), 16)
                    sp.wait_ge(Z("state_new"), 8)
                    sp.dma_start(out[name + "_sample"][lay].rearrange("o b h d e -> d (o b h) e"), S0.rearrange("p b h e -> p (b h) e")).then_inc(Z("stored"), 16)
                    sp.wait_ge(Z("stored"), 32)

        def stage_ssm(l):
            lay = bass.ds(l, 1)
            ar = Arena(arena, 0, AN)
            z = ar.take(5, 512)
            dt, a = ar.take(5, 8), ar.take(5, 8)
            xc = ar.take(8, T)
            keep = ar.at
            raw = ar.take(8, SEQ + 3)
            raws = ar.take(8, NB, 7)
            cst_in = ar.take(DM)
            cp, cs = ar.take(DM), ar.take(DM)
            tail = ar.take(8, NB * 3)
            acc, accs = ar.take(2, SEQ), ar.take(2, NS)
            ut, au = ar.take(5, 8), ar.take(5, 8)
            ea = ar.take(8)
            with nc.Block() as block:
                @block.sync
                def _(sp):
                    sp.dma_start(cst_in[0:24, :], inp["state_conv"][lay].rearrange("o b j n -> (o b j) n")).then_inc(S("conv_in"), 16)
                    stream(sp, J["dt"] + 3, l)

                @block.gpsimd
                def _(pool):
                    pool.memset(raw[:, :, 0:3], 0.0)
                    pool.memset(dt[:, 4, :], 0.0).then_inc(S("d_padded"), 1)

                @block.tensor
                def _(pe):
                    proj_natural(pe, J["z"], 512)
                    for i in range(2):
                        proj_transposed(pe, J[f"xbc{i}"], hT, KC, range(4), lambda dc: dc * 128)
                    proj_natural(pe, J["dt"], 8)
                    pe.wait_ge(S("conv_in"), 16)
                    for c in range(8):
                        mm = pe.transpose(ps[4][:, c * 24:c * 24 + 24], cst_in[0:24, c * P:c * P + P], ident[0:24, 0:24])
                    mm.then_inc(S("conv_in_turned"), 1)

                @block.scalar
                def _(act):
                    act.wait_ge(S("d_padded"), 1)
                    for job in ("z", "xbc0", "xbc1", "dt"):
                        for i, (t0, m) in enumerate(tiles[:4] if job[0] == "x" else tiles):
                            n = kact[0]
                            act.wait_ge(S("proj_ready"), n + 1)
                            b = ps[n % 2]
                            if job == "z":
                                ins = act.activation(z[0:m, i, :], b[0:m, :], ACT.Silu)
                            elif job == "dt":
                                ins = act.activation(dt[0:m, i, :], b[0:m, 0:8], ACT.Copy)
                            else:
                                c = 4 * int(job[3]) + i
                                act.activation(raw[:, c, 3:SEQ + 3], b[:, :], ACT.Copy)
                                ins = act.activation(raws[:, c, :, 3:7], ps[2 + n % 2][:, 0:NS].rearrange("p (b t) -> p b t", b=NB), ACT.Copy)
                            ins.then_inc(S("proj_taken"), 1)
                            kact[0] += 1
                    act.wait_ge(S("conv_in_turned"), 1)
                    for c in range(8):
                        act.activation(raws[:, c, :, 0:3], ps[4][:, c * 24:c * 24 + 24].rearrange("p (b j) -> p b j", b=NB), ACT.Copy)
            with nc.Block() as block:
                @block.vector
                def _(dve):
                    L = vch.link
                    dve.tensor_copy(tail.rearrange("p c (b j) -> p c b j", b=NB), raws[:, :, :, 4:7]).then_inc(S("tail_ready"), 1)
                    L(dve, dve.tensor_tensor(ut, dt, bc(dtb, 1, 5), ALU.add))
                    L(dve, dve.tensor_scalar(au, ut, -1.0, None, ALU.mult))
                    dve.tensor_tensor(au, au, ut, ALU.max).then_inc(S("dt_abs"), 1)
                    dve.wait_ge(S("dt_log"), 1)
                    L(dve, dve.scalar_tensor_tensor(dt, ut, 0.0, au, ALU.max, ALU.add))
                    dve.scalar_tensor_tensor(a, dt, -1.0, bc(ea, 1, 5), ALU.mult, ALU.mult)
                    for c in range(8):
                        if c >= 2:
                            dve.wait_ge(S("conv_taken"), c - 1)
                        ap_, as_ = acc[:, c % 2, :], accs[:, c % 2, :].rearrange("p (b t) -> p b t", b=NB)
                        dve.tensor_scalar(ap_, raw[:, c, 0:SEQ], cw[:, 0, c:c + 1], cb[:, c:c + 1], ALU.mult, ALU.add)
                        L(dve, dve.tensor_scalar(as_, raws[:, c, :, 0:4], cw[:, 0, c:c + 1], cb[:, c:c + 1], ALU.mult, ALU.add))
                        for j in range(1, 4):
                            dve.scalar_tensor_tensor(ap_, raw[:, c, j:j + SEQ], cw[:, j, c:c + 1], ap_, ALU.mult, ALU.add)
                            ins = dve.scalar_tensor_tensor(as_, raws[:, c, :, j:j + 4], cw[:, j, c:c + 1], as_, ALU.mult, ALU.add)
                            if j < 3:
                                L(dve, ins)
                        ins.then_inc(S("conv_ready"), 1)

                @block.scalar
                def _(act):
                    act.wait_ge(S("dt_abs"), 1)
                    act.activation(ea, alog, ACT.Exp)
                    ach.link(act, act.activation(au, au, ACT.Exp, scale=-1.0))
                    act.activation(au, au, ACT.Ln, bias=ones[:, 0:1]).then_inc(S("dt_log"), 1)
                    for c in range(8):
                        act.wait_ge(S("conv_ready"), c + 1)
                        act.activation(xc[:, c, 0:SEQ], acc[:, c % 2, :], ACT.Silu)
                        act.activation(xc[:, c, SEQ:T], accs[:, c % 2, :], ACT.Silu).then_inc(S("conv_taken"), 1)
                    act.wait_ge(S("conv_state_turned"), 1)
                    for half in range(2):
                        act.activation(cp[0:3, half * 512:half * 512 + 512], ps[half][0:3, :], ACT.Copy)
                        ins = act.activation(cs[0:24, half * 512:half * 512 + 512], ps[2 + half][0:24, :], ACT.Copy)
                    ins.then_inc(S("conv_state_ready"), 1)

                @block.tensor
                def _(pe):
                    pe.wait_ge(S("tail_ready"), 1)
                    for c in range(8):
                        at = c % 4 * P
                        pe.transpose(ps[c // 4][0:3, at:at + P], raw[:, c, SEQ:SEQ + 3], ident)
                        mm = pe.transpose(ps[2 + c // 4][0:24, at:at + P], tail[:, c, :], ident)
                    mm.then_inc(S("conv_state_turned"), 1)

                @block.sync
                def _(sp):
                    sp.wait_ge(S("conv_state_ready"), 1)
                    sp.dma_start(out["conv_prompt"][lay].rearrange("o b j n -> (o b j) n"), cp[0:3, :]).then_inc(S("conv_stored"), 16)
                    sp.dma_start(out["conv_sample"][lay].rearrange("o b j n -> (o b j) n"), cs[0:24, :]).then_inc(S("conv_stored"), 16)
                    sp.wait_ge(S("conv_stored"), 32)
            ar = Arena(arena, keep, AN)
            h0 = ar.take(NB, 4, P)
            hs = ar.take(NB, 512)
            AW, W = ar.take(8 * P), ar.take(8 * P)
            xn, xw, hp, y = ar.take(512), ar.take(512), ar.take(512), ar.take(512)
            t_x = AW[:, 512:1024]
            Bn = ar.take(256)
            ec = ar.take(3, 8)
            wt = ar.take(8)
            ss = ar.take(2)
            dec = ar.take(4, NB)
            t = AW[:, 0:512]
            CM = W[:, 512:768].rearrange("p (b t) -> p b t", b=NB)
            Bx = AW.rearrange("p (b s) -> p b s", b=NB)
            with nc.Block() as block:
                @block.sync
                def _(sp):
                    for b in range(0, NB, 2):
                        sp.dma_start(h0[:, b:b + 2].rearrange("p b q s -> p (b q) s"),
                                     inp["state_ssm"][lay, b:b + 2].rearrange("o b (q x) p s -> (x p) (o b q) s", x=2)).then_inc(S("ssm_in"), 16)
                    sp.wait_ge(S("ssm_new"), 8)
                    sp.dma_start(out["ssm_sample"][lay].rearrange("o b (q x) p s -> (x p) (o b q) s", x=2), h0.rearrange("p b q s -> p (b q) s")).then_inc(S("ssm_stored"), 16)
                    sp.wait_ge(S("ssm_prompt_ready"), 1)
                    sp.dma_start(out["ssm_prompt"][lay].rearrange("o b (q x) p s -> (x p) (o b q) s", x=2), hp.rearrange("p (q s) -> p q s", q=4)).then_inc(S("ssm_stored"), 16)
                    sp.wait_ge(S("ssm_stored"), 32)

                @block.tensor
                def _(pe):
                    for i, (t0, m) in enumerate(tiles):
                        last = i == 4
                        triu, aft = (K("tri_s")[0:NS], K("after_s")[0:NS]) if last else (tri, after)
                        if i >= 1:
                            pe.wait_ge(S("d_y_taken"), i)
                        if last:
                            pe.wait_ge(S("ssm_prompt_ready"), 1)
                        for c in range(4):
                            pe.transpose(ps[0][0:m, c * P:c * P + P], xc[:, c, t0:t0 + m], ident)
                        for c in range(2):
                            pe.transpose(ps[1][0:m, c * P:c * P + P], xc[:, 4 + c, t0:t0 + m], ident)
                        for c in range(2):
                            pe.matmul(ps[2][0:m, c * m:c * m + m], xc[:, 4 + c, t0:t0 + m], xc[:, 6 + c, t0:t0 + m])
                        pe.matmul(ps[2][0:m, 256:264], triu, a[0:m, i, :])
                        mm = pe.matmul(ps[2][0:m, 264:272], aft, a[0:m, i, :])
                        if not last:
                            mm = pe.matmul(ps[2][:, 272:280], ones, a[:, i, :])
                        mm.then_inc(S("d_turned"), 1)
                        pe.wait_ge(S("d_segs"), i + 1)
                        for h in range(8):
                            mm = pe.matmul(ps[3 + h // 4][0:m, h % 4 * m:h % 4 * m + m], AW[0:m, h * m:h * m + m], triu)
                        mm.then_inc(S("d_seg_sums"), 1)
                        if last:
                            pe.wait_ge(S("ssm_in"), 64)
                            for b in range(NB):
                                if b >= 2:
                                    pe.wait_ge(S("hs_taken"), b - 1)
                                for qq in range(4):
                                    mm = pe.transpose(ps[6 + b % 2][:, qq * P:qq * P + P], h0[:, b, qq, :], ident)
                                mm.then_inc(S("hs_turned"), 1)
                            pe.wait_ge(S("hs_taken"), 8)
                        pe.wait_ge(S("d_weights"), i + 1)
                        for h in range(8):
                            mm = pe.matmul(ps[5][0:m, h * 64:h * 64 + 64], W[0:m, h * m:h * m + m], t_x[0:m, h * 64:h * 64 + 64])
                        if not last:
                            for gg in range(2):
                                if i > 0:
                                    pe.matmul(ps[6][0:m, gg * 256:gg * 256 + 256], xc[:, 6 + gg, t0:t0 + m], hp[:, gg * 256:gg * 256 + 256])
                                mm = pe.matmul(ps[7][:, gg * 256:gg * 256 + 256], Bn[0:m, gg * P:gg * P + P], xw[0:m, gg * 256:gg * 256 + 256])
                            mm.then_inc(S("d_out"), 1)
                        else:
                            mm.then_inc(S("d_out"), 1)
                            for gg in range(2):
                                pe.wait_ge(S("c_masked"), gg + 1)
                                for b in range(NB):
                                    mm = pe.matmul(ps[6][0:NS, gg * 256:gg * 256 + 256], CM[:, b, :], hs[:, b, gg * 256:gg * 256 + 256],
                                                   start=(b == 0), stop=(b == NB - 1))
                                mm.then_inc(S("c_mask_used"), 1)
                            pe.wait_ge(S("a_spread"), 1)
                            for qq in range(4):
                                mm = pe.matmul(ps[1][:, qq * NB:qq * NB + NB], y[0:NS, qq * P:qq * P + P], K("seqhot")[0:NS])
                            mm.then_inc(S("ssm_decay_sums"), 1)
                            for n in range(8):
                                qq, half = n // 2, n % 2
                                pe.wait_ge(S("b_masked"), qq // 2 + 1)
                                if n >= 2:
                                    pe.wait_ge(S("ssm_new"), n - 1)
                                pe.matmul(ps[3 + n % 2][:, :], xw[0:NS, qq * P:qq * P + P],
                                          Bx[0:NS, half * 4:half * 4 + 4, :].rearrange("p b s -> p (b s)")).then_inc(S("ssm_add"), 1)
                        pe.wait_ge(S("d_y"), i + 1)
                        for c in range(4):
                            mm = pe.transpose(ps[0][:, c * m:c * m + m], y[0:m, c * P:c * P + P], ident[0:m, 0:m])
                        mm.then_inc(S("d_y_turned"), 1)
                        if i == 3:
                            for qq in range(4):
                                mm = pe.transpose(ps[1][:, qq * P:qq * P + P], hp[:, qq * P:qq * P + P], ident)
                            mm.then_inc(S("hp_turned"), 1)

                @block.scalar
                def _(act):
                    for i, (t0, m) in enumerate(tiles):
                        last = i == 4
                        act.wait_ge(S("d_turned"), i + 1)
                        act.activation(xn[0:m, :], ps[0][0:m, :], ACT.Copy)
                        act.activation(Bn[0:m, :], ps[1][0:m, 0:256], ACT.Copy)
                        k = 2 if last else 3
                        act.activation(ec[0:m, 0:k, :], ps[2][0:m, 256:256 + 8 * k].rearrange("p (k h) -> p k h", k=k), ACT.Exp).then_inc(S("d_taken"), 1)
                        act.wait_ge(S("d_seg_sums"), i + 1)
                        for half in range(2):
                            ins = act.activation(W[0:m, half * 4 * m:half * 4 * m + 4 * m], ps[3 + half][0:m, 0:4 * m], ACT.Exp)
                        ins.then_inc(S("d_seg_exp"), 1)
                        if last:
                            for b in range(NB):
                                act.wait_ge(S("hs_turned"), b + 1)
                                act.activation(hs[:, b, :], ps[6 + b % 2][:, :], ACT.Copy).then_inc(S("hs_taken"), 1)
                            act.wait_ge(S("ssm_decay_sums"), 1)
                            act.activation(dec.rearrange("p q b -> p (q b)"), ps[1][:, 0:32], ACT.Exp).then_inc(S("ssm_decays"), 1)
                        act.wait_ge(S("d_sq"), i + 1)
                        ach.link(act, act.activation(ss[0:m, :], ss[0:m, :], ACT.Ln, bias=eps[0:m], scale=1.0 / 256))
                        act.activation(ss[0:m, :], ss[0:m, :], ACT.Exp, scale=-0.5).then_inc(S("d_rstd"), 1)
                        act.wait_ge(S("d_y_turned"), i + 1)
                        act.activation(brT[:, 12:16, t0:t0 + m], ps[0][:, 0:4 * m].rearrange("p (c t) -> p c t", c=4), ACT.Copy).then_inc(S("d_y_taken"), 1)
                        if i == 3:
                            act.wait_ge(S("hp_turned"), 1)
                            act.activation(hp[:, :], ps[1][:, :], ACT.Copy).then_inc(S("ssm_prompt_ready"), 1)

                @block.vector
                def _(dve):
                    L = vch.link

                    def v3(x, m, k):
                        return x[0:m].rearrange("p (k d) -> p k d", k=k)
                    for i, (t0, m) in enumerate(tiles):
                        last = i == 4
                        triu, aft = (K("tri_s")[0:NS], K("after_s")[0:NS]) if last else (tri, after)
                        dve.tensor_tensor(AW[0:m, 0:8 * m].rearrange("p (h n) -> p h n", h=8), bc(aft, 1, 8), bc(a[0:m, i, :], 2, m), ALU.mult).then_inc(S("d_segs"), 1)
                        dve.wait_ge(S("d_taken"), i + 1)
                        cbm = ps[2][0:m, 0:2 * m].rearrange("p (g n) -> p g n", g=2)
                        L(dve, dve.tensor_tensor(v3(y, m, 1)[:, 0, 0:2 * m].rearrange("p (g n) -> p g n", g=2), cbm, bc(triu, 1, 2), ALU.mult))
                        L(dve, dve.tensor_tensor(wt[0:m, :], ec[0:m, 1, :], dt[0:m, i, :], ALU.mult))
                        L(dve, dve.tensor_tensor(v3(xw, m, 8), v3(xn, m, 8), bc(wt[0:m, :], 2, 64), ALU.mult))
                        dve.wait_ge(S("d_seg_exp"), i + 1)
                        L(dve, dve.tensor_tensor(v3(t_x, m, 8), v3(xn, m, 8), bc(dt[0:m, i, :], 2, 64), ALU.mult))
                        dve.tensor_tensor(W[0:m, 0:8 * m].rearrange("p (g h n) -> p g h n", g=2, h=4), W[0:m, 0:8 * m].rearrange("p (g h n) -> p g h n", g=2, h=4),
                                          bc(y[0:m, 0:2 * m].rearrange("p (g n) -> p g n", g=2), 2, 4), ALU.mult).then_inc(S("d_weights"), 1)
                        dve.wait_ge(S("d_out"), i + 1)
                        if last:
                            msk = K("qmask").rearrange("p (b t) -> p b t", b=NB)
                            L(dve, dve.tensor_copy(v3(y, NS, 8), bc(a[0:NS, 4, :], 2, 64)))
                            dve.tensor_copy(v3(y, NS, 8), bc(a[0:NS, 4, :], 2, 64)).then_inc(S("a_spread"), 1)
                            for gg in range(2):
                                if gg:
                                    dve.wait_ge(S("c_mask_used"), 1)
                                dve.tensor_tensor(CM, bc(xc[:, 6 + gg, SEQ:T], 1, NB), msk, ALU.mult).then_inc(S("c_masked"), 1)
                            dve.wait_ge(S("ssm_decays"), 1)
                            dve.wait_ge(S("c_mask_used"), 2)
                            for n in range(8):
                                qq, half = n // 2, n % 2
                                if n % 4 == 0:
                                    if n:
                                        dve.wait_ge(S("ssm_add"), 4)
                                    dve.tensor_tensor(Bx[0:NS], bc(Bn[0:NS, qq // 2 * P:qq // 2 * P + P], 1, NB), bc(K("seqhot")[0:NS], 2, P), ALU.mult).then_inc(S("b_masked"), 1)
                                dve.wait_ge(S("ssm_add"), n + 1)
                                st = h0[:, half * 4:half * 4 + 4, qq, :]
                                L(dve, dve.tensor_tensor(st, st, bc(dec[:, qq, half * 4:half * 4 + 4], 2, P), ALU.mult))
                                dve.tensor_tensor(st, st, ps[3 + n % 2][:, :].rearrange("p (b s) -> p b s", b=4), ALU.add).then_inc(S("ssm_new"), 1)
                            dve.wait_ge(S("ssm_new"), 8)
                        else:
                            if i == 0:
                                L(dve, dve.tensor_copy(hp[:, :], ps[7][:, :]))
                            else:
                                L(dve, dve.tensor_tensor(v3(hp, P, 8), v3(hp, P, 8), bc(ec[:, 2, :], 2, 64), ALU.mult))
                                L(dve, dve.tensor_tensor(hp[:, :], hp[:, :], ps[7][:, :], ALU.add))
                        L(dve, dve.tensor_tensor(v3(t, m, 8), v3(xn, m, 8), bc(dskip[0:m, :], 2, 64), ALU.mult))
                        L(dve, dve.tensor_tensor(t[0:m, :], t[0:m, :], ps[5][0:m, :], ALU.add))
                        if i > 0:
                            L(dve, dve.tensor_tensor(v3(y, m, 8), ps[6][0:m, :].rearrange("p (k d) -> p k d", k=8), bc(ec[0:m, 0, :], 2, 64), ALU.mult))
                            L(dve, dve.tensor_tensor(t[0:m, :], t[0:m, :], y[0:m, :], ALU.add))
                        L(dve, dve.tensor_tensor(y[0:m, :], t[0:m, :], z[0:m, i, :], ALU.mult))
                        L(dve, dve.tensor_tensor(t[0:m, :], y[0:m, :], y[0:m, :], ALU.mult))
                        dve.tensor_reduce(ss[0:m, :], v3(t, m, 2), AX, ALU.add).then_inc(S("d_sq"), 1)
                        dve.wait_ge(S("d_rstd"), i + 1)
                        L(dve, dve.tensor_tensor(v3(y, m, 2), v3(y, m, 2), bc(ss[0:m, :], 2, 256), ALU.mult))
                        dve.tensor_tensor(y[0:m, :], y[0:m, :], gssm[0:m, :], ALU.mult).then_inc(S("d_y"), 1)
                        dve.wait_ge(S("d_y_turned"), i + 1)

        def stage_merge(l):
            ar = Arena(arena, 0, AN)
            sg = ar.take(4, T)
            mg = ar.take(8, T)
            tm = ar.take(2, T)
            base = groups(J["dt"])
            base_o = groups(J["wb13"])
            with nc.Block() as block:
                @block.sync
                def _(sp):
                    stream(sp, J["wo1"] + 3, l)

                @block.tensor
                def _(pe):
                    for db in range(2):
                        for n in range(4):
                            k = (db * 4 + n) * 4
                            proj_transposed(pe, J[f"gate{db}{n}"], hT, KC, range(4), lambda dc: dc * 128, taken="gate_taken", first=k)
                            proj_transposed(pe, J[f"wb{db}{n}"], brT[:, 4 * n:4 * n + 4, :], 4, range(4), lambda dc: dc * 128,
                                            banks=(4, 5, 6, 7), taken="up_taken", first=k)
                    pe.wait_ge(S("gate_taken"), 32)
                    pe.wait_ge(S("merged"), 32)
                    for db in range(2):
                        proj_transposed(pe, J[f"wo{db}"], mg, KC, range(4), lambda dc: dc * 128, taken="out_taken", first=db * 4)

                @block.scalar
                def _(act):
                    for k in range(32):
                        grp, dc = k // 4, k % 4
                        act.wait_ge(S("proj_ready"), base + grp * 8 + dc + 1)
                        if k >= 4:
                            act.wait_ge(S("up_taken"), k - 3)
                        act.activation(sg[:, dc, 0:SEQ], ps[k % 2][:, :], ACT.Sigmoid)
                        act.activation(sg[:, dc, SEQ:T], ps[2 + k % 2][:, 0:NS], ACT.Sigmoid).then_inc(S("gate_taken"), 1)

                @block.vector
                def _(dve):
                    for k in range(32):
                        grp, dc = k // 4, k % 4
                        db, n = grp // 4, grp % 4
                        dve.wait_ge(S("gate_taken"), k + 1)
                        dve.wait_ge(S("proj_ready"), base + grp * 8 + 4 + dc + 1)
                        if k >= 2:
                            dve.wait_ge(S("merged"), k - 1)
                        dst = mg[:, db * 4 + dc] if n == 0 else tm[:, k % 2]
                        ins = dve.tensor_tensor(dst[:, 0:SEQ], ps[4 + k % 2][:, :], sg[:, dc, 0:SEQ], ALU.mult)
                        ins = dve.tensor_tensor(dst[:, SEQ:T], ps[6 + k % 2][:, 0:NS], sg[:, dc, SEQ:T], ALU.mult)
                        ins.then_inc(S("up_taken"), 1)
                        if n == 0:
                            dve.engine_nop().then_inc(S("merged"), 1)
                        else:
                            dve.wait_ge(S("up_taken"), k + 1)
                            dve.tensor_tensor(mg[:, db * 4 + dc], mg[:, db * 4 + dc], dst, ALU.add).then_inc(S("merged"), 1)
                    for k in range(8):
                        dve.wait_ge(S("proj_ready"), base_o + k + 1)
                        dve.tensor_tensor(xT[:, k, 0:SEQ], xT[:, k, 0:SEQ], ps[k % 2][:, :], ALU.add)
                        dve.tensor_tensor(xT[:, k, SEQ:T], xT[:, k, SEQ:T], ps[2 + k % 2][:, 0:NS], ALU.add).then_inc(S("out_taken"), 1)

        def stage_ff(l):
            ar = Arena(arena, 0, AN)
            ff = ar.take(FC, T)
            sg = ar.take(2, T)
            base = groups(J["wo1"])
            with nc.Block() as block:
                @block.sync
                def _(sp):
                    stream(sp, len(jobs), l)

                @block.tensor
                def _(pe):
                    for i in range(11):
                        for x in range(2):
                            n = 2 * i + x
                            proj_transposed(pe, J[f"gu{i}"], hT, KC, [x], lambda dc: dc * 128, taken="ffg_taken", first=n)
                            proj_transposed(pe, J[f"gu{i}"], hT, KC, [x], lambda dc: 256 + dc * 128,
                                            banks=(4, 5, 6, 7), taken="ffu_taken", first=n)
                    pe.wait_ge(S("ffu_taken"), FC)
                    pe.wait_ge(S("ffg_taken"), FC)
                    for db in range(2):
                        if db:
                            pe.wait_ge(S("down_taken"), 4)
                        for r in range(3):
                            j = J[f"dn{db}{r}"]
                            arrived(pe, j)
                            for c in range(min(8, FC - 8 * r)):
                                fc = 8 * r + c
                                for dc in range(4):
                                    w = slot3(j)[:, c, dc * P:dc * P + P]
                                    pe.matmul(ps[dc][:, :], w, ff[:, fc, 0:SEQ], start=(fc == 0), stop=(fc == FC - 1))
                                    mm = pe.matmul(ps[4 + dc][:, 0:NS], w, ff[:, fc, SEQ:T], start=(fc == 0), stop=(fc == FC - 1))
                            mm.then_inc(S("down_job_done"), 1)

                @block.scalar
                def _(act):
                    for n in range(FC):
                        act.wait_ge(S("proj_ready"), base + 2 * n + 1)
                        if n >= 2:
                            act.wait_ge(S("ffu_taken"), n - 1)
                        act.activation(sg[:, n % 2, 0:SEQ], ps[n % 2][:, :], ACT.Silu)
                        act.activation(sg[:, n % 2, SEQ:T], ps[2 + n % 2][:, 0:NS], ACT.Silu).then_inc(S("ffg_taken"), 1)

                @block.vector
                def _(dve):
                    for n in range(FC):
                        dve.wait_ge(S("ffg_taken"), n + 1)
                        dve.wait_ge(S("proj_ready"), base + 2 * n + 2)
                        dve.tensor_tensor(ff[:, n, 0:SEQ], ps[4 + n % 2][:, :], sg[:, n % 2, 0:SEQ], ALU.mult)
                        dve.tensor_tensor(ff[:, n, SEQ:T], ps[6 + n % 2][:, 0:NS], sg[:, n % 2, SEQ:T], ALU.mult).then_inc(S("ffu_taken"), 1)
                    for db in range(2):
                        dve.wait_ge(S("down_job_done"), 3 * (db + 1))
                        for dc in range(4):
                            k = db * 4 + dc
                            dve.tensor_tensor(xT[:, k, 0:SEQ], xT[:, k, 0:SEQ], ps[dc][:, :], ALU.add)
                            dve.tensor_tensor(xT[:, k, SEQ:T], xT[:, k, SEQ:T], ps[4 + dc][:, 0:NS], ALU.add).then_inc(S("down_taken"), 1)

        with nc.Fori(0, DEPTH) as l:
            part(rms_stage, g1, 2, l, True)
            part(stage_a, l)
            part(stage_linear, l, "r")
            part(stage_linear, l, "c")
            part(stage_ssm, l)
            part(stage_merge, l)
            part(rms_stage, g2, 0, l, False)
            part(stage_ff, l)
            with nc.Block() as block:
                @block.sync
                def _(sp):
                    for name in LAYER_SEMS:
                        sp.sem_clear(S(name))

        def epilogue():
            ar = Arena(arena, 0, AN)
            yn = ar.take(5, DM)
            with nc.Block() as block:
                @block.tensor
                def _(pe):
                    for u in range(10):
                        i, half = u // 2, u % 2
                        t0, m = tiles[i]
                        if u >= 2:
                            pe.wait_ge(S("end_taken"), u - 1)
                        for c in range(4):
                            mm = pe.transpose(ps[u % 2][0:m, c * P:c * P + P], xT[:, half * 4 + c, t0:t0 + m], ident)
                        mm.then_inc(S("end_turned"), 1)

                @block.scalar
                def _(act):
                    for u in range(10):
                        i, half = u // 2, u % 2
                        m = tiles[i][1]
                        act.wait_ge(S("end_turned"), u + 1)
                        act.activation(yn[0:m, i, half * 512:half * 512 + 512], ps[u % 2][0:m, :], ACT.Copy).then_inc(S("end_taken"), 1)

                @block.sync
                def _(sp):
                    sp.wait_ge(S("end_taken"), 10)
                    sp.dma_start(out["y_prompt"].rearrange("o (t p) d -> p (o t) d", p=P), yn[:, 0:4, :]).then_inc(S("end_stored"), 16)
                    sp.dma_start(out["y_sample"].rearrange("b t d -> (b t) d"), yn[0:NS, 4, :]).then_inc(S("end_stored"), 16)
                    sp.wait_ge(S("end_stored"), 32)

        part(epilogue)


OUTS = [("y_prompt", (1, SEQ, DM)), ("y_sample", (NB, TS, DM)),
        ("k_prompt", (DEPTH, 1, SEQ, 4, 64)), ("v_prompt", (DEPTH, 1, SEQ, 4, 64)), ("kidx_prompt", (DEPTH, 1, SEQ, 64)),
        ("ret_prompt", (DEPTH, 1, 4, P, P)), ("hgrn_prompt", (DEPTH, 1, 4, P, P)), ("ssm_prompt", (DEPTH, 1, 8, 64, P)),
        ("conv_prompt", (DEPTH, 1, 3, DM)),
        ("k_sample", (DEPTH, NB, TS, 4, 64)), ("v_sample", (DEPTH, NB, TS, 4, 64)), ("kidx_sample", (DEPTH, NB, TS, 64)),
        ("ret_sample", (DEPTH, NB, 4, P, P)), ("hgrn_sample", (DEPTH, NB, 4, P, P)), ("ssm_sample", (DEPTH, NB, 8, 64, P)),
        ("conv_sample", (DEPTH, NB, 3, DM))]


def build(nc, arrays):
    inp = {n: nc.dram_tensor(f"in_{n}", a.shape, mybir.dt.from_np(a.dtype), kind="ExternalInput").ap() for n, a in arrays.items()}
    out = {n: nc.dram_tensor(f"out_{n}", s, F32, kind="ExternalOutput").ap() for n, s in OUTS}
    trunk(nc, inp, out)


def kernel(**inputs):
    import concourse.bacc as bacc
    from concourse.bass_utils import run_bass_kernel_spmd

    arrays = {n: np.ascontiguousarray(a) for n, a in inputs.items()}
    arrays["consts"] = constants()
    nc = bacc.Bacc("TRN2", target_bir_lowering=False, num_devices=1)
    build(nc, arrays)
    r = run_bass_kernel_spmd(nc, [{f"in_{n}": a for n, a in arrays.items()}], core_ids=[0])
    return tuple(r.results[0][f"out_{n}"] for n, _ in OUTS)
```

```python
from contextlib import ExitStack

import numpy as np

import concourse.bass as bass
from concourse import mybir

ALU = mybir.AluOpType
ACT = mybir.ActivationFunctionType
F32 = mybir.dt.float32
I32 = mybir.dt.int32
AX = mybir.AxisListType.X

P = 128
DM = 1024
SEQ = 512
DEPTH = 2
NB = 8
TS = 4
NS = NB * TS
NT = SEQ // P
T = SEQ + NS
PAST = 2048
PAGE = 128
NPG = PAST // PAGE
LK = PAST + NS
KC = DM // P
DFF = 2816
FC = DFF // P
EPS = 1e-6
NEG = -1e30
TAKEN = -3.0e38
TOPK_P = min(256, SEQ // 4)
TOPK_S = min(256, (PAST + TS) // 4)

A_Q, A_K, A_V, A_IQ, A_IK, A_IW = 0, 512, 768, 1024, 1536, 1600
R_Q, C_Q, M_Z, M_X, M_DT, GATES = 1608, 3656, 5704, 6216, 7240, 7248
D_IN = 11344

C = {}
_at = 0
for _n, _w in (("ident", 128), ("ones", 128), ("tri", 128), ("after", 128), ("tri_s", 32), ("after_s", 32),
               ("seqhot", 8), ("qmask", 256), ("bb", 16), ("lv_sum", 7 * 128), ("lv_mask", 7 * 128),
               ("lv_side", 7), ("rdec", 4 * 128), ("rq", 4), ("rk", 4), ("rdec_s", 4 * 32), ("rq_s", 4),
               ("rk_s", 4), ("cos", 5 * 64), ("sin", 5 * 64), ("neg", 128), ("neg_s", 32), ("eps", 1),
               ("rep", 2 * 128), ("wsel", 2 * NS), ("hsel", 8)):
    C[_n] = (_at, _w)
    _at += _w
NCONST = _at
AN = 17840


def constants():
    c = np.zeros((P, NCONST), np.float64)

    def put(name, a):
        a = np.asarray(a, np.float64)
        a = a.reshape(a.shape[0], -1)
        c[:a.shape[0], C[name][0]:C[name][0] + a.shape[1]] = a

    i = np.arange(P)
    k, n = i[:, None], i[None, :]
    put("ident", np.eye(P))
    put("ones", np.ones((P, P)))
    put("tri", k <= n)
    put("after", k > n)
    t = np.arange(NS)
    same = (t[:, None] // TS) == (t[None, :] // TS)
    put("tri_s", (t[:, None] <= t[None, :]) & same)
    put("after_s", (t[:, None] > t[None, :]) & same)
    put("seqhot", (t[:, None] // TS) == np.arange(NB)[None])
    put("qmask", np.broadcast_to((np.arange(NB)[:, None] == t[None, :] // TS)[None], (P, NB, NS)))
    put("bb", np.broadcast_to(np.eye(4)[None], (P, 4, 4)))
    sums, masks, sides = [], [], []
    for lv in range(7):
        w = 1 << lv
        block = i // (2 * w)
        right = (i // w) % 2 == 1
        ref = block * 2 * w + w - 1
        s = np.where(right[None, :], (k > ref[None, :]) & (k <= n), (k > n) & (k <= ref[None, :]))
        sums.append(s)
        masks.append((block[:, None] == block[None, :]) & ~right[:, None] & right[None, :])
        sides.append(right)
    put("lv_sum", np.stack(sums, 1))
    put("lv_mask", np.stack(masks, 1))
    put("lv_side", np.stack(sides, 1))
    lg = np.log1p(-np.exp2(-5.0 - np.arange(4)))
    sc = 128 ** -0.5
    put("rdec", np.stack([np.where(k <= n, np.exp(-g * (k + 1.0)) * sc, 0.0) for g in lg], 1))
    put("rq", np.exp(lg[None] * (i[:, None] + 1.0)))
    put("rk", np.exp(lg[None] * (127.0 - i[:, None])) * sc)
    ts = t % TS
    put("rdec_s", np.stack([np.where((t[:, None] <= t[None, :]) & same, np.exp(-g * (ts[:, None] + 1.0)) * sc, 0.0)
                            for g in lg], 1))
    put("rq_s", np.exp(lg[None] * (ts[:, None] + 1.0)))
    put("rk_s", np.exp(lg[None] * (TS - 1.0 - ts[:, None])) * sc)
    freq = (np.float32(10000.0) ** (-np.arange(64, dtype=np.float32) / np.float32(64))).astype(np.float32)
    pos = np.zeros((P, 5), np.float32)
    for tt in range(4):
        pos[:, tt] = tt * P + i
    pos[:NS, 4] = PAST + ts
    ang = (pos[:, :, None] * freq[None, None]).astype(np.float32).astype(np.float64)
    put("cos", np.cos(ang))
    put("sin", np.sin(ang))
    put("neg", np.where(n <= k, 0.0, NEG))
    put("neg_s", np.where((t[None, :] <= t[:, None]) & same, 0.0, NEG))
    put("eps", np.full((P, 1), EPS))
    rep = np.zeros((NS, 2, 4, 8, TS))
    for b in range(NB):
        for tq in range(TS):
            rep[b * TS + tq, b // 4, b % 4, :, tq] = 1
    put("rep", rep)
    r = np.arange(P)
    wsel = np.zeros((P, 2, NB, TS))
    for g in range(2):
        wsel[r, g, 4 * g + r // 32, r % TS] = 1
    put("wsel", wsel)
    put("hsel", (r[:, None] // TS) % 8 == np.arange(8)[None])
    return c.astype(np.float32)


HALF = T // 2
LAYER_SEMS = ("proj_ready", "taken_act", "taken_dve", "weights_in0", "weights_in1", "down_job_done", "dve_step", "act_step",
              "merged", "spilled0", "spilled1", "spilled2", "spilled3", "ret_stored", "hgrn_stored", "ssm_stored")


def trunk(nc, inp, out):
    es = ExitStack()
    with es:
        sems, stage_sems, stage_stack = {}, {}, [None]

        def S(name):
            if name in LAYER_SEMS:
                if name not in sems:
                    sems[name] = es.enter_context(nc.semaphore(name))
                return sems[name]
            if name not in stage_sems:
                stage_sems[name] = stage_stack[0].enter_context(nc.semaphore(name))
            return stage_sems[name]

        def part(run, *args):
            with ExitStack() as stack:
                stage_stack[0] = stack
                run(*args)
                with nc.Block() as block:
                    @block.sync
                    def _(sp):
                        for sem in stage_sems.values():
                            sp.sem_clear(sem)
                stage_sems.clear()

        def sb(name, n):
            return es.enter_context(nc.sbuf_tensor(name, [P, n], F32))

        def bc(ap, axis, n):
            u = ap.unsqueeze(axis)
            shape = list(u.shape)
            shape[axis] = n
            return u.broadcast_to(shape)

        xT_ = sb("xT", KC * T)
        hT_ = sb("hT", KC * T)
        brT_ = sb("branchT", 16 * T)
        ring_ = sb("ring", 2 * KC * 512)
        cst = sb("cst", NCONST)
        lbt = sb("lb_both", 2 * 512)
        par = sb("layer_params", 2112)
        ptab = es.enter_context(nc.sbuf_tensor("ptab", [1, NB * NPG], I32))
        stage = sb("stage", 4 * 512)
        arena = sb("arena", AN)
        spill = nc.dram_tensor("spill", [9, T, 512], F32).ap()
        spill_x = nc.dram_tensor("spill_x", [DM, T], F32).ap()
        spill_dt = nc.dram_tensor("spill_dt", [T, 8], F32).ap()
        ps = [es.enter_context(nc.psum_tensor(f"ps{i}", [P, 512], F32)) for i in range(8)]
        xT = xT_[:, :].rearrange("p (c t) -> p c t", c=KC)
        hT = hT_[:, :].rearrange("p (c t) -> p c t", c=KC)
        brT = brT_[:, :].rearrange("p (c t) -> p c t", c=16)
        slot = [ring_[:, i * 4096:(i + 1) * 4096] for i in range(2)]

        def K(name):
            return cst[:, C[name][0]:C[name][0] + C[name][1]]

        ident, ones, tri, after = K("ident"), K("ones"), K("tri"), K("after")
        eps = K("eps")

        sg = arena[:, AN - 4 * T:AN].rearrange("p (c t) -> p c t", c=4)
        merge_tmp = arena[:, AN - 5 * T:AN - 4 * T].rearrange("p (i t) -> p i t", i=2)
        mg = arena[:, AN - 13 * T:AN - 5 * T].rearrange("p (c t) -> p c t", c=8)
        ANB = AN - 13 * T

        class Arena:
            def __init__(self, t, at=0, end=None):
                self.t, self.at, self.end = t, at, end

            def take(self, *dims):
                n = int(np.prod(dims))
                a = self.t[:, self.at:self.at + n]
                self.at += n
                assert self.end is None or self.at <= self.end, self.at
                if len(dims) == 1:
                    return a
                names = "abcd"[:len(dims)]
                return a.rearrange(f"p ({' '.join(names)}) -> p {' '.join(names)}",
                                   **{x: d for x, d in zip(names, dims)})

        pa = Arena(par, 0, 2112)
        g1, g2 = pa.take(KC), pa.take(KC)
        gq, gk = pa.take(64), pa.take(64)
        ghg, dtb, alog, dskip = pa.take(128), pa.take(8), pa.take(8), pa.take(8)
        gssm = pa.take(512)
        cw, cb = pa.take(4, 8), pa.take(8)
        lb, oml = pa.take(512), pa.take(512)

        class Chain:
            def __init__(self, name):
                self.sem, self.n = S(name), 0

            def link(self, eng, ins):
                ins.then_inc(self.sem, 1)
                self.n += 1
                eng.wait_ge(self.sem, self.n)

        vch, ach = Chain("dve_step"), Chain("act_step")

        jobs = [("aq", A_Q, 512), ("akv", A_K, 512), ("iq", A_IQ, 512), ("ikiw", A_IK, 72)]
        jobs += [(f"r{i}", R_Q + 512 * i, 512) for i in range(4)]
        jobs += [(f"c{i}", C_Q + 512 * i, 512) for i in range(4)]
        jobs += [("z", M_Z, 512), ("xbc0", M_X, 512), ("xbc1", M_X + 512, 512), ("dt", M_DT, 8)]
        for n in range(4):
            for db in range(2):
                jobs += [(f"gate{n}{db}", GATES + n * DM + db * 512, 512), (f"wb{n}{db}", (n, db), 512)]
        jobs += [(f"wo{db}", db, 512) for db in range(2)]
        jobs += [(f"gu{i}", i, 512) for i in range(11)]
        jobs += [(f"dn{db}{r}", (db, r), 512) for db in range(2) for r in range(3)]
        J = {name: i for i, (name, _, _) in enumerate(jobs)}
        issued = [0]

        def slot3(j):
            return slot[j % 2].rearrange("p (c n) -> p c n", c=KC)

        def stream(sp, upto, l):
            for j in range(issued[0], min(upto, len(jobs))):
                name, at, w = jobs[j]
                if j >= 2:
                    if jobs[j - 2][0][:2] == "dn":
                        sp.wait_ge(S("down_job_done"), j - 2 - J["dn00"] + 1)
                    else:
                        sp.wait_ge(S("proj_ready"), END[jobs[j - 2][0]])
                dst = slot3(j)
                lay = bass.ds(l, 1)
                if name[:2] == "wb":
                    src = inp["w_branch"][lay, at[0]].rearrange("o (c p) n -> p (o c) n", p=P)[:, :, at[1] * 512:at[1] * 512 + 512]
                    sp.dma_start(dst[:, 0:4, :], src).then_inc(S(f"weights_in{j % 2}"), 16)
                elif name[:2] == "wo":
                    src = inp["w_out"][lay].rearrange("o (c p) n -> p (o c) n", p=P)[:, :, at * 512:at * 512 + 512]
                    sp.dma_start(dst, src).then_inc(S(f"weights_in{j % 2}"), 16)
                elif name[:2] == "gu":
                    src = inp["w_gu"][lay].rearrange("o (c p) (u n) -> p u (o c) n", p=P, u=2)
                    for u in range(2):
                        sp.dma_start(dst[:, :, u * 256:u * 256 + 256],
                                     src[:, u, :, at * 256:at * 256 + 256]).then_inc(S(f"weights_in{j % 2}"), 16)
                elif name[:2] == "dn":
                    n = min(8, FC - 8 * at[1])
                    src = inp["w_down"][lay].rearrange("o (c p) n -> p (o c) n", p=P)[:, at[1] * 8:at[1] * 8 + n, at[0] * 512:at[0] * 512 + 512]
                    sp.dma_start(dst[:, 0:n, :], src).then_inc(S(f"weights_in{j % 2}"), 16)
                else:
                    src = inp["w_in"][lay].rearrange("o (c p) n -> p (o c) n", p=P)[:, :, at:at + w]
                    sp.dma_start(dst[:, :, 0:w], src).then_inc(S(f"weights_in{j % 2}"), 16)
            issued[0] = max(issued[0], upto)

        def arrived(pe, j):
            n = sum(32 if jobs[i][0][:2] == "gu" else 16 for i in range(j % 2, j + 1, 2))
            pe.wait_ge(S(f"weights_in{j % 2}"), n)

        tiles = [(tt * P, P) for tt in range(NT)] + [(SEQ, NS)]
        kpe, kact = [0], [0]

        table = []
        END = {}
        for name, _, _ in jobs:
            if name[:2] == "dn":
                continue
            if name[:2] == "gu":
                for col in (0, 256, 128, 384):
                    table += [(name, False, col, half, KC, "dve" if col >= 256 else "act") for half in range(2)]
            elif name[:2] in ("ga", "wb", "wo", "iq", "xb"):
                by = "dve" if name[:2] in ("wb", "wo") else "act"
                table += [(name, False, dc * P, half, 4 if name[:2] == "wb" else KC, by) for dc in range(4) for half in range(2)]
            else:
                table += [(name, True, tt, 0, KC, "act") for tt in range(5)]
            END[name] = len(table)
        starts = [0]
        for row in table:
            starts.append(starts[-1] + row[4])

        def taken_by(k):
            return "taken_" + table[k][5], sum(1 for row in table[:k + 1] if row[5] == table[k][5])

        def product(pe, k, c):
            name, natural, at, half, kn, _ = table[k]
            j = J[name]
            if c == 0:
                if k == 0 or table[k - 1][0] != name:
                    arrived(pe, j)
                    if name == "wo0":
                        pe.wait_ge(S("merged"), 48)
                if k >= 2:
                    sem, n = taken_by(k - 2)
                    pe.wait_ge(S(sem), n)
            bank = ps[6 + k % 2]
            if natural:
                t0, m = tiles[at]
                w = jobs[j][2]
                mm = pe.matmul(bank[0:m, 0:w], hT[:, c, t0:t0 + m], slot3(j)[:, c, 0:w], start=(c == 0), stop=(c == kn - 1))
            else:
                if name[:2] == "wb":
                    src = brT[:, 4 * jobs[j][1][0] + c, half * HALF:half * HALF + HALF]
                elif name[:2] == "wo":
                    src = mg[:, c, half * HALF:half * HALF + HALF]
                else:
                    src = hT[:, c, half * HALF:half * HALF + HALF]
                mm = pe.matmul(bank[:, 0:HALF], slot3(j)[:, c, at:at + P], src, start=(c == 0), stop=(c == kn - 1))
            if c == kn - 1:
                mm.then_inc(S("proj_ready"), 1)

        keep_at, spills = {}, [0]

        def take_act(act, k):
            name, natural, at, half, _, by = table[k]
            if by != "act":
                return
            act.wait_ge(S("proj_ready"), k + 1)
            bank = ps[6 + k % 2]
            t = slice(half * HALF, half * HALF + HALF)
            if natural:
                t0, m = tiles[at]
            if name == "aq":
                ins = act.activation(keep_at["qn"][0:m, at, :], bank[0:m, :], ACT.Copy)
            elif name == "akv":
                act.activation(keep_at["kn"][0:m, at, :], bank[0:m, 0:256], ACT.Copy)
                ins = act.activation(keep_at["vn"][0:m, at, :], bank[0:m, 256:512], ACT.Copy)
            elif name == "iq":
                ins = act.activation(keep_at["iqT"][:, at // P, t], bank[:, 0:HALF], ACT.Copy)
            elif name == "ikiw":
                for u in range(2):
                    act.activation(keep_at["ikd"][0:m, at, u, :], bank[0:m, 0:64], ACT.Copy)
                ins = act.activation(keep_at["iwn"][0:m, at, :], bank[0:m, 64:72], ACT.Copy, scale=8 ** -0.5)
            elif name[:4] == "gate":
                ins = act.activation(sg[:, at // P, t], bank[:, 0:HALF], ACT.Copy)
                if at == 3 * P and half == 1:
                    ach.link(act, ins)
                    ins = act.activation(sg[:, :, :], sg[:, :, :], ACT.Sigmoid)
            elif name[:2] == "gu":
                ins = act.activation(sg[:, at // P, t], bank[:, 0:HALF], ACT.Silu)
            else:
                i, n = spills[0] % 4, spills[0] // 4
                if n:
                    act.wait_ge(S(f"spilled{i}"), 16 * n)
                st = stage[:, i * 512:i * 512 + 512]
                if name[:3] == "xbc":
                    c = 4 * int(name[3]) + at // P
                    ins = act.activation(st[:, 0:HALF], bank[:, 0:HALF], ACT.Copy)
                    dst, src = (spill_x[c * P:c * P + P, t], st[:, 0:HALF])
                elif name == "dt":
                    ins = act.activation(st[0:m, 0:8], bank[0:m, 0:8], ACT.Copy)
                    dst, src = (spill_dt[t0:t0 + m, :], st[0:m, 0:8])
                else:
                    row = 8 if name == "z" else int(name[1]) + (4 if name[0] == "c" else 0)
                    ins = act.activation(st[0:m, :], bank[0:m, :], ACT.Copy)
                    dst, src = (spill[row, t0:t0 + m, :], st[0:m, :])
                spills[0] += 1
                ins.then_inc(S("taken_act"), 1)
                act.wait_ge(S("taken_act"), taken_by(k)[1])
                act.dma_start(dst, src).then_inc(S(f"spilled{i}"), 16)
                return
            ins.then_inc(S("taken_act"), 1)

        merges = [0]

        def take_dve(dve, k):
            name, natural, at, half, _, by = table[k]
            if by != "dve":
                return
            dve.wait_ge(S("proj_ready"), k + 1)
            bank = ps[6 + k % 2]
            t = slice(half * HALF, half * HALF + HALF)
            if name[:2] == "wb":
                n, db = jobs[J[name]][1]
                gate = max(i for i in range(k) if table[i][0][:4] == "gate")
                dve.wait_ge(S("taken_act"), taken_by(gate)[1])
                dst = mg[:, db * 4 + at // P, t]
                if n == 0:
                    dve.tensor_tensor(dst, bank[:, 0:HALF], sg[:, at // P, t], ALU.mult).then_inc(S("taken_dve"), 1)
                else:
                    tm = merge_tmp[:, k % 2, :]
                    dve.tensor_tensor(tm, bank[:, 0:HALF], sg[:, at // P, t], ALU.mult).then_inc(S("taken_dve"), 1)
                    dve.wait_ge(S("taken_dve"), taken_by(k)[1])
                    dve.tensor_tensor(dst, dst, tm, ALU.add).then_inc(S("merged"), 1)
                    merges[0] += 1
                    dve.wait_ge(S("merged"), merges[0])
            elif name[:2] == "wo":
                dst = xT[:, jobs[J[name]][1] * 4 + at // P, t]
                dve.tensor_tensor(dst, dst, bank[:, 0:HALF], ALU.add).then_inc(S("taken_dve"), 1)
            else:
                gate = k - 2
                dve.wait_ge(S("taken_act"), taken_by(gate)[1])
                n = 2 * jobs[J[name]][1] + (at - 256) // P
                dve.tensor_tensor(ff_ref[0][:, n, t], bank[:, 0:HALF], sg[:, (at - 256) // P, t], ALU.mult).then_inc(S("taken_dve"), 1)

        done = {"pe": 0, "act": 0, "dve": 0}
        ff_ref = [None]

        def fill_to(who, eng, upto):
            if who == "pe":
                for x in range(done["pe"], upto):
                    k = max(i for i in range(len(table)) if starts[i] <= x)
                    product(eng, k, x - starts[k])
                done["pe"] = max(done["pe"], upto)
                return
            k = max(i for i in range(len(table)) if starts[i] < max(upto, 1))
            take_to(who, eng, k - 1)

        def take_to(who, eng, upto):
            for k in range(done[who], upto):
                if who == "act" and (table[k][0][:4] == "gate" or table[k][0][:2] == "gu") and table[k][5] == "act":
                    last = [i for i in range(k) if table[i][5] == "dve" and
                            (table[k][0][:4] == "gate" or table[i][0][:2] == "wo" or table[i][2] - 256 == table[k][2])]
                    if last:
                        eng.wait_ge(S("taken_dve"), taken_by(last[-1])[1])
                (take_act if who == "act" else take_dve)(eng, k)
            done[who] = max(done[who], upto)

        def finish_to(who, eng, name):
            if who == "pe":
                fill_to("pe", eng, starts[END[name]])
            else:
                take_to(who, eng, END[name])

        class Share:
            def __init__(self, last, weights):
                self.a = {w: starts_at[0] for w in ("pe", "act", "dve")}
                self.a0, self.b = starts_at[0], starts[END[last]]
                self.cum = np.cumsum(weights) / np.sum(weights)
                self.p = {"pe": 0, "act": 0, "dve": 0}
                self.last = last
                starts_at[0] = self.b

            def point(self, who, eng):
                x = self.a0 + int(round((self.b - self.a0) * self.cum[self.p[who]]))
                self.p[who] += 1
                fill_to(who, eng, x)

            def end(self, who, eng):
                assert self.p[who] in (0, len(self.cum)) or who == "dve", (who, self.p[who], len(self.cum))
                finish_to(who, eng, self.last)
        starts_at = [0]

        def prologue():
            ar = Arena(arena, 0, AN)
            xnat = ar.take(5, DM)
            with nc.Block() as block:
                @block.sync
                def _(sp):
                    sp.dma_start(cst[:, :], inp["consts"]).then_inc(S("consts_in"), 16)
                    sp.dma_start(xnat[:, 0:4, :], inp["x_prompt"].rearrange("o (t p) d -> p (o t) d", p=P)).then_inc(S("x_in"), 16)
                    sp.dma_start(xnat[0:NS, 4, :], inp["x_sample"].rearrange("b t d -> (b t) d")).then_inc(S("x_in"), 16)
                    sp.dma_start(ptab[:, :], inp["page_table"].rearrange("(o b) g -> o (b g)", o=1)).then_inc(S("x_in"), 16)
                    sp.dma_start(lbt[:, :], inp["lb_param"].rearrange("(o l) n -> o (l n)", o=1).broadcast_to([P, 2 * 512])).then_inc(S("lb_in"), 16)
                    sp.wait_ge(S("x_in"), 48)

                @block.tensor
                def _(pe):
                    pe.wait_ge(S("consts_in"), 16)
                    pe.wait_ge(S("x_in"), 48)
                    for c in range(KC):
                        if c >= 2:
                            pe.wait_ge(S("x_taken"), c - 1)
                        for tt, (t0, m) in enumerate(tiles):
                            dst = ps[c % 2][:, t0:t0 + m] if m == P else ps[2 + c % 2][:, 0:m]
                            mm = pe.transpose(dst, xnat[0:m, tt, c * P:c * P + P], ident[0:m, 0:m])
                        mm.then_inc(S("x_turned"), 1)

                @block.scalar
                def _(act):
                    for c in range(KC):
                        act.wait_ge(S("x_turned"), c + 1)
                        act.activation(xT[:, c, 0:SEQ], ps[c % 2][:, :], ACT.Copy)
                        act.activation(xT[:, c, SEQ:T], ps[2 + c % 2][:, 0:NS], ACT.Copy).then_inc(S("x_taken"), 1)
                    act.wait_ge(S("lb_shifted"), 1)
                    act.activation(lbt[:, :], lbt[:, :], ACT.Exp).then_inc(S("lb_exp"), 1)

                @block.vector
                def _(dve):
                    tmp = ar.take(512)
                    l0, l1 = lbt[:, 0:512], lbt[:, 512:1024]
                    dve.wait_ge(S("lb_in"), 16)
                    vch.link(dve, dve.tensor_tensor(tmp, l0, l1, ALU.max))
                    vch.link(dve, dve.tensor_tensor(l0, l0, tmp, ALU.subtract))
                    dve.tensor_tensor(l1, l1, tmp, ALU.subtract).then_inc(S("lb_shifted"), 1)
                    dve.wait_ge(S("lb_exp"), 1)
                    vch.link(dve, dve.tensor_tensor(tmp, l0, l1, ALU.add))
                    vch.link(dve, dve.reciprocal(tmp, tmp))
                    vch.link(dve, dve.tensor_tensor(l0, l0, tmp, ALU.mult))
                    vch.link(dve, dve.tensor_tensor(l1, l1, tmp, ALU.mult))
                    vch.link(dve, dve.tensor_tensor(l1, l0, l1, ALU.add))
                    vch.link(dve, dve.tensor_tensor(l1, l1, l0, ALU.subtract))
                    vch.link(dve, dve.tensor_tensor(l0, l0, l0, ALU.subtract))

        part(prologue)
        with nc.Block() as block:
            @block.sync
            def _(sp):
                sp.sem_clear(S("dve_step"))
        vch.n = 0

        def rms_stage(gain, uses, l, prologue):
            ar = Arena(arena)
            rstd = ar.take(T)
            with nc.Block() as block:
                @block.sync
                def _(sp):
                    if prologue:
                        lay = bass.ds(l, 1)

                        def col(name):
                            return inp[name][lay].rearrange("o (c p) -> p (o c)", p=P)

                        def row(name):
                            a = inp[name][lay]
                            return a.broadcast_to([P, a.shape[1]])
                        with nc.allow_non_contiguous_dma(reason="small columns of parameters"):
                            sp.dma_start(g1, col("norm1_g")).then_inc(S("params_in"), 16)
                            sp.dma_start(g2, col("norm2_g")).then_inc(S("params_in"), 16)
                            sp.dma_start(cb, col("conv_b")).then_inc(S("params_in"), 16)
                            for j in range(4):
                                sp.dma_start(cw[:, j, :], inp["conv_w"][lay, j].rearrange("o (c p) -> p (o c)", p=P)).then_inc(S("params_in"), 16)
                        for dst, name in ((gq, "q_norm_g"), (gk, "k_norm_g"), (ghg, "hgrn_norm_g"), (dtb, "dt_bias"),
                                          (alog, "A_log"), (dskip, "D_skip"), (gssm, "ssm_norm_g")):
                            sp.dma_start(dst, row(name)).then_inc(S("params_in"), 16)
                        sp.wait_ge(S("params_in"), 16 * 14)
                    stream(sp, uses, l)

                @block.vector
                def _(dve):
                    dve.tensor_tensor(hT[:, :, :], xT[:, :, :], xT[:, :, :], ALU.mult).then_inc(S("sq_ready"), 1)
                    dve.wait_ge(S("rstd_ready"), 1)
                    if prologue:
                        dve.wait_ge(S("params_in"), 16 * 14)
                        vch.link(dve, dve.tensor_copy(lb, lbt[:, bass.ds(l * 512, 512)]))
                        vch.link(dve, dve.tensor_scalar(oml, lb, -1.0, 1.0, ALU.mult, ALU.add))
                    for c in range(KC):
                        dve.scalar_tensor_tensor(hT[:, c, :], xT[:, c, :], gain[:, c:c + 1], rstd[:, :], ALU.mult, ALU.mult)

                @block.tensor
                def _(pe):
                    pe.wait_ge(S("sq_ready"), 1)
                    for c in range(KC):
                        pe.matmul(ps[0][:, :], ones, hT[:, c, 0:SEQ], start=(c == 0), stop=(c == KC - 1))
                    for c in range(KC):
                        mm = pe.matmul(ps[1][:, 0:NS], ones, hT[:, c, SEQ:T], start=(c == 0), stop=(c == KC - 1))
                    mm.then_inc(S("sq_summed"), 1)

                @block.scalar
                def _(act):
                    act.wait_ge(S("sq_summed"), 1)
                    act.activation(rstd[:, 0:SEQ], ps[0][:, :], ACT.Ln, bias=eps, scale=1.0 / DM)
                    ach.link(act, act.activation(rstd[:, SEQ:T], ps[1][:, 0:NS], ACT.Ln, bias=eps, scale=1.0 / DM))
                    act.activation(rstd[:, :], rstd[:, :], ACT.Exp, scale=-0.5).then_inc(S("rstd_ready"), 1)

        def stage_a(l):
            lay = bass.ds(l, 1)
            ar = Arena(arena, 0, AN)
            vn = ar.take(5, 256)
            kTs = ar.take(2, NS)
            iwn = ar.take(5, 8)
            qT = ar.take(4, T)
            idx_at = ar.at
            ikT = ar.take(T)
            iqT = ar.take(4, T)
            keep = ar.at
            k2T = ar.take(4, T)
            kn = ar.take(5, 256)
            ikd = ar.take(5, 2, 64)
            qn = ar.take(5, 512)
            tmp = Arena(brT_, 4 * T, 16 * T).take(5, 512)
            kdup = ar.take(5, 4, 2, 64)
            ssq, ssk = ar.take(5 * 8), ar.take(5 * 4)
            with nc.Block() as block:
                @block.sync
                def _(sp):
                    stream(sp, J["ikiw"] + 3, l)

                @block.gpsimd
                def _(pool):
                    for a in (qn, kn, vn, iwn):
                        ins = pool.memset(a[:, 4, :], 1.0)
                    ins = pool.memset(ikd[:, 4, :, :], 1.0)
                    ins.then_inc(S("a_padded"), 1)

                @block.tensor
                def _(pe):
                    finish_to("pe", pe, "ikiw")

                @block.scalar
                def _(act):
                    act.wait_ge(S("a_padded"), 1)
                    keep_at.update(qn=qn, kn=kn, vn=vn, ikd=ikd, iwn=iwn, iqT=iqT)
                    finish_to("act", act, "ikiw")
            done["dve"] = END["ikiw"]
            starts_at[0] = starts[END["ikiw"]]
            share = Share("r0", [6, 12] + [1.2] * 10)
            with nc.Block() as block:
                @block.vector
                def _(dve):
                    for a, nh, ss, g, sem in ((qn, 8, ssq, gq, "q"), (kn, 4, ssk, gk, "k")):
                        a2 = a.rearrange("p t (h d) -> p (t h) d", d=64)
                        t2 = tmp.rearrange("p t n -> p (t n)")[:, 0:5 * nh * 64].rearrange("p (g d) -> p g d", d=64)
                        vch.link(dve, dve.tensor_tensor(t2, a2, a2, ALU.mult))
                        dve.tensor_reduce(ss, t2, AX, ALU.add).then_inc(S("qk_sq"), 1)
                        dve.wait_ge(S("qk_rstd"), 1 if sem == "q" else 2)
                        vch.link(dve, dve.tensor_tensor(a2, a2, bc(ss, 2, 64), ALU.mult))
                        dve.tensor_tensor(a2, a2, bc(g, 1, 5 * nh), ALU.mult).then_inc(S(sem + "_normed"), 1)
                    dve.wait_ge(S("k_normed"), 1)
                    for u in range(2):
                        ins = dve.tensor_copy(kdup[:, :, :, u, :], kn.rearrange("p t (h d) -> p t h d", d=64))
                        ins.then_inc(S("k_doubled"), 1)

                @block.scalar
                def _(act):
                    for i, ss in enumerate((ssq, ssk)):
                        act.wait_ge(S("qk_sq"), i + 1)
                        ach.link(act, act.activation(ss, ss, ACT.Ln, bias=eps, scale=1.0 / 64))
                        act.activation(ss, ss, ACT.Exp, scale=-0.5).then_inc(S("qk_rstd"), 1)
                        share.point("act", act)
                    for g in range(10):
                        act.wait_ge(S("a_turned"), g + 1)
                        if g < 9:
                            dst = qT[:, g] if g < 4 else k2T[:, g - 4] if g < 8 else ikT
                            act.activation(dst[:, 0:SEQ], ps[g % 2][:, :], ACT.Copy)
                            ins = act.activation(dst[:, SEQ:T], ps[2 + g % 2][:, 0:NS], ACT.Copy)
                        else:
                            ins = act.activation(kTs, ps[4][:, 0:2 * NS].rearrange("p (j t) -> p j t", j=2), ACT.Copy)
                        ins.then_inc(S("a_turn_taken"), 1)
                        share.point("act", act)
                    share.end("act", act)

                @block.tensor
                def _(pe):
                    share.point("pe", pe)
                    share.point("pe", pe)
                    pe.wait_ge(S("q_normed"), 1)
                    for g in range(10):
                        if g == 4:
                            pe.wait_ge(S("k_doubled"), 2)
                        if g >= 2:
                            pe.wait_ge(S("a_turn_taken"), g - 1)
                        if g == 9:
                            for j in range(2):
                                mm = pe.transpose(ps[4][:, j * NS:j * NS + NS], kn[0:NS, 4, j * P:j * P + P], ident[0:NS, 0:NS])
                            mm.then_inc(S("a_turned"), 1)
                            share.point("pe", pe)
                            continue
                        for i, (t0, m) in enumerate(tiles):
                            if g < 4:
                                src = qn[0:m, i, g * P:g * P + P]
                            elif g < 8:
                                src = kdup[0:m, i, g - 4].rearrange("p u d -> p (u d)")
                            else:
                                src = ikd[0:m, i].rearrange("p u d -> p (u d)")
                            dst = ps[g % 2][:, t0:t0 + m] if m == P else ps[2 + g % 2][:, 0:m]
                            mm = pe.transpose(dst, src, ident[0:m, 0:m])
                        mm.then_inc(S("a_turned"), 1)
                        share.point("pe", pe)
                    share.end("pe", pe)

                @block.sync
                def _(sp):
                    def rows(name):
                        return out[name][lay].rearrange("o b (t p) h d -> p (o b t) (h d)", p=P)
                    sp.wait_ge(S("k_normed"), 1)
                    sp.dma_start(rows("k_prompt"), kn[:, 0:4, :]).then_inc(S("a_stored"), 16)
                    sp.dma_start(rows("v_prompt"), vn[:, 0:4, :]).then_inc(S("a_stored"), 16)
                    sp.dma_start(out["kidx_prompt"][lay].rearrange("o b (t p) d -> p (o b t) d", p=P), ikd[:, 0:4, 0, :]).then_inc(S("a_stored"), 16)
                    sp.dma_start(out["k_sample"][lay].rearrange("o b t h d -> (o b t) (h d)"), kn[0:NS, 4, :]).then_inc(S("a_stored"), 16)
                    sp.dma_start(out["v_sample"][lay].rearrange("o b t h d -> (o b t) (h d)"), vn[0:NS, 4, :]).then_inc(S("a_stored"), 16)
                    sp.dma_start(out["kidx_sample"][lay].rearrange("o b t d -> (o b t) d"), ikd[0:NS, 4, 0, :]).then_inc(S("a_stored"), 16)
                    sp.wait_ge(S("a_stored"), 96)

            ar = Arena(arena, keep + 4 * T, AN)
            R = ar.take(2, 512)
            score, work, bias = ar.take(512), ar.take(512), ar.take(512)
            m8 = ar.take(2, 8)
            St, Pr = ar.take(2, 512), ar.take(2, 512)
            PT = ar.take(2, 512)
            on = ar.take(2, 512)
            mx, sm = ar.take(2, 8), ar.take(2, 8)
            weights = []
            for i in range(NT):
                weights += [1] * 8 + [(1, 18, 25, 34)[i]] + [1] * 18
            share = Share("r3", weights)
            with nc.Block() as block:
                @block.sync
                def _(sp):
                    stream(sp, J["r3"] + 3, l)

                @block.tensor
                def _(pe):
                    for i in range(NT):
                        L = (i + 1) * P
                        q0 = i * P
                        for h in range(8):
                            n = i * 8 + h
                            r = (h % 2) * 64
                            if n >= 2:
                                pe.wait_ge(S("idx_relu"), n - 1)
                            if h < 2 and i:
                                pe.wait_ge(S("att_biased"), 8 * i)
                            pe.matmul(ps[n % 2][:, 0:L], iqT[r:r + 64, h // 2, q0:q0 + P], ikT[r:r + 64, 0:L]).then_inc(S("idx_logits"), 1)
                            share.point("pe", pe)

                        def scores(h):
                            n = i * 8 + h
                            r = (h % 2) * 64
                            if h < 2:
                                pe.wait_ge(S("idx_relu"), 8 * i + 8)
                            if n >= 2:
                                pe.wait_ge(S("att_biased"), n - 1)
                            pe.matmul(ps[n % 2][:, 0:L], qT[r:r + 64, h // 2, q0:q0 + P], k2T[r:r + 64, h // 2, 0:L]).then_inc(S("att_scores"), 1)

                        def turn_probs(h):
                            n = i * 8 + h
                            if n >= 2:
                                pe.wait_ge(S("probT_taken"), n - 1)
                            pe.wait_ge(S("att_probs"), n + 1)
                            for s in range(i + 1):
                                mm = pe.transpose(ps[2 + n % 2][:, s * P:s * P + P], Pr[:, n % 2, s * P:s * P + P], ident)
                            mm.then_inc(S("probT_ready"), 1)

                        def values(h):
                            n = i * 8 + h
                            pe.wait_ge(S("probT_taken"), n + 1)
                            if n >= 2:
                                pe.wait_ge(S("att_out"), n - 1)
                            if h == 1 and i:
                                pe.wait_ge(S("att_turn_taken"), i)
                            for s in range(i + 1):
                                mm = pe.matmul(ps[4 + n % 2][:, h * 64:h * 64 + 64], PT[:, n % 2, s * P:s * P + P],
                                               vn[:, s, (h // 2) * 64:(h // 2) * 64 + 64], start=(s == 0), stop=(s == i))
                            mm.then_inc(S("att_values"), 1)
                        share.point("pe", pe)
                        scores(0)
                        for h in range(9):
                            if h < 7:
                                scores(h + 1)
                            share.point("pe", pe)
                            if h < 8:
                                turn_probs(h)
                            share.point("pe", pe)
                            if h >= 1:
                                values(h - 1)
                        pe.wait_ge(S("att_out"), 8 * i + 8)
                        if i >= 1:
                            pe.wait_ge(S("att_turn_taken"), i)
                        for c in range(4):
                            mm = pe.transpose(ps[5][:, c * P:c * P + P], on[:, i % 2, c * P:c * P + P], ident)
                        mm.then_inc(S("att_turned"), 1)
                    share.end("pe", pe)

                @block.scalar
                def _(act):
                    for i in range(NT):
                        L = (i + 1) * P
                        for h in range(8):
                            n = i * 8 + h
                            act.wait_ge(S("idx_logits"), n + 1)
                            if n >= 2:
                                act.wait_ge(S("idx_summed"), n - 1)
                            act.activation(R[:, n % 2, 0:L], ps[n % 2][:, 0:L], ACT.Relu, scale=0.125).then_inc(S("idx_relu"), 1)
                            share.point("act", act)
                        share.point("act", act)
                        for h in range(9):
                            n = i * 8 + h
                            if h < 8:
                                act.wait_ge(S("att_max"), n + 1)
                                if n >= 2:
                                    act.wait_ge(S("probT_ready"), n - 1)
                                act.activation(Pr[:, n % 2, 0:L], St[:, n % 2, 0:L], ACT.Exp, bias=mx[:, n % 2, 0:1],
                                               accum_out=sm[:, n % 2, 0:1]).then_inc(S("att_probs"), 1)
                            share.point("act", act)
                            if h >= 1:
                                act.wait_ge(S("probT_ready"), n)
                                if n >= 3:
                                    act.wait_ge(S("att_values"), n - 2)
                                act.activation(PT[:, (n - 1) % 2, 0:L], ps[2 + (n - 1) % 2][:, 0:L], ACT.Copy).then_inc(S("probT_taken"), 1)
                            share.point("act", act)
                        act.wait_ge(S("att_turned"), i + 1)
                        act.activation(brT[:, 0:4, i * P:i * P + P], ps[5][:, :].rearrange("p (c t) -> p c t", c=4), ACT.Copy).then_inc(S("att_turn_taken"), 1)
                    share.end("act", act)

                @block.vector
                def _(dve):
                    for i in range(NT):
                        L = (i + 1) * P
                        dve.wait_ge(S("idx_relu"), i * 8 + 1)
                        vch.link(dve, dve.memset(score[:, 0:L], 0.0))
                        for h in range(8):
                            n = i * 8 + h
                            dve.wait_ge(S("idx_relu"), n + 1)
                            ins = dve.scalar_tensor_tensor(score[:, 0:L], R[:, n % 2, 0:L], iwn[:, i, h:h + 1],
                                                           score[:, 0:L], ALU.mult, ALU.add)
                            ins.then_inc(S("idx_summed"), 1)
                            dve.wait_ge(S("idx_summed"), n + 1)
                        vch.link(dve, dve.tensor_tensor(score[:, L - P:L], score[:, L - P:L], K("neg"), ALU.add))
                        topk(dve, score[:, 0:L], work[:, 0:L], bias[:, 0:L], m8, TOPK_P if L > TOPK_P else L)
                        vch.link(dve, dve.tensor_tensor(bias[:, L - P:L], bias[:, L - P:L], K("neg"), ALU.add))
                        for h in range(10):
                            n = i * 8 + h
                            if h >= 2:
                                dve.wait_ge(S("att_probs"), n - 1)
                                vch.link(dve, dve.reciprocal(sm[:, n % 2, 1:2], sm[:, n % 2, 0:1]))
                            if h < 8:
                                dve.wait_ge(S("att_scores"), n + 1)
                                if n >= 2:
                                    dve.wait_ge(S("att_probs"), n - 1)
                                dve.scalar_tensor_tensor(St[:, n % 2, 0:L], ps[n % 2][:, 0:L], 0.125, bias[:, 0:L],
                                                         ALU.mult, ALU.add).then_inc(S("att_biased"), 1)
                                dve.wait_ge(S("att_biased"), n + 1)
                                dve.tensor_reduce(mx[:, n % 2, 0:1], St[:, n % 2, 0:L], AX, ALU.max, negate=True).then_inc(S("att_max"), 1)
                            if h >= 2:
                                dve.wait_ge(S("att_values"), n - 1)
                                if h == 2 and i >= 2:
                                    dve.wait_ge(S("att_turned"), i - 1)
                                dve.tensor_scalar(on[:, i % 2, (h - 2) * 64:(h - 2) * 64 + 64], ps[4 + n % 2][:, (h - 2) * 64:(h - 2) * 64 + 64],
                                                  sm[:, n % 2, 1:2], None, ALU.mult).then_inc(S("att_out"), 1)
            stage_a_sample(l, idx_at, keep, vn, kTs, iwn, qT, ikT, iqT)

        def topk(dve, score, work, bias, m8, k):
            if k >= score.shape[1]:
                vch.link(dve, dve.memset(bias, 0.0))
                return
            for r in range(k // 8):
                src = score if r == 0 else work
                m = m8[0:score.shape[0], r % 2, :]
                vch.link(dve, dve.max(m, src))
                vch.link(dve, dve.match_replace(work, m, src, TAKEN))
            vch.link(dve, dve.tensor_scalar(bias, work, TAKEN, NEG, ALU.not_equal, ALU.mult))

        def stage_a_sample(l, idx_at, keep, vn, kTs, iwn, qT, ikT, iqT):
            lay = bass.ds(l, 1)
            ar = Arena(arena, keep, AN)
            bias = ar.take(LK)
            keep2 = ar.at
            ba = Arena(brT_, 4 * T, 16 * T)
            QP = ba.take(8, 2, 4, 32)
            qz = ba.take(2, 8, 8, 4)
            score, work = ar.take(LK), ar.take(LK)
            iqh = ar.take(8, 8, 4)
            IQP = ar.take(8, 4, 32)
            kx = ar.take(4, 4, 64)
            ikc = ar.take(2, 512)
            R = ar.take(2, 512)
            WS = ar.take(2, NS)
            w8, wcol = ar.take(2, 8), ar.take(2)
            m8 = ar.take(2, 8)
            steps = [(g, c, bb) for g in range(2) for c in range(4) for bb in range(4)]
            share = Share("xbc0", [1] * 32 + [160])

            def load_pages(eng, pages, dst, name, b, c, sem):
                for pg in pages:
                    at = b * NPG + 4 * c + pg
                    page = eng.value_load(ptab[0:1, at:at + 1], min_val=0, max_val=inp[name].shape[1] - 1)
                    if name == "cache_kidx":
                        src = inp[name][lay, bass.ds(page, 1)].rearrange("o q t d -> (o q t) d")
                    else:
                        src = inp[name][lay, bass.ds(page, 1)].rearrange("o q t g d -> (o q t) (g d)")
                    eng.dma_start(dst[:, pg, :], src).then_inc(S(sem), 16)

            def load_kidx(eng, pages, s):
                g, c, bb = steps[s]
                load_pages(eng, pages, kx[:, s % 4], "cache_kidx", 4 * g + bb, c, f"kidx_in{s % 4}")
            with nc.Block() as block:
                @block.sync
                def _(sp):
                    for s, (g, c, bb) in enumerate(steps):
                        if s == 16:
                            stream(sp, J["c0"] + 2, l)
                        if s >= 4:
                            sp.wait_ge(S("kidx_turned"), s - 3)
                        load_kidx(sp, (0, 1), s)
                    stream(sp, J["xbc0"] + 3, l)

                @block.tensor
                def _(pe):
                    for g in range(2):
                        mm = pe.matmul(ps[4][:, g * 8:g * 8 + 8], K("rep")[0:NS, g * P:g * P + P], iwn[0:NS, 4, :])
                    mm.then_inc(S("w_spread"), 1)
                    pe.wait_ge(S("iq_padded"), 1)
                    pe.wait_ge(S("wsel_ready"), 1)

                    def turn(s):
                        pe.wait_ge(S(f"kidx_in{s % 4}"), 64 * (s // 4 + 1))
                        if s >= 2:
                            pe.wait_ge(S("ikc_ready"), s - 1)
                        for pg in range(4):
                            mm = pe.transpose(ps[s % 2][0:64, pg * P:pg * P + P], kx[:, s % 4, pg, :], ident)
                        mm.then_inc(S("kidx_turned"), 1)

                    def weigh(u, w):
                        pe.wait_ge(S("sidx_relu"), u + 1)
                        if u >= 2:
                            pe.wait_ge(S("sidx_taken"), u - 1)
                        pe.matmul(ps[4 + u % 2][0:NS, 0:w], WS[:, u // 5, :], R[:, u % 2, 0:w]).then_inc(S("sidx_weighed"), 1)

                    turn(0)
                    for g in range(2):
                        for c in range(5):
                            u = g * 5 + c
                            if u >= 2:
                                pe.wait_ge(S("sidx_relu"), u - 1)
                            for bb in range(4):
                                if c < 4:
                                    s = (g * 4 + c) * 4 + bb
                                    if s + 1 < len(steps):
                                        turn(s + 1)
                                    share.point("pe", pe)
                                    pe.wait_ge(S("ikc_ready"), s + 1)
                                    mm = pe.matmul(ps[2 + u % 2][:, :], IQP[0:64, 4 * g + bb].rearrange("p a n -> p (a n)"),
                                                   ikc[0:64, s % 2, :], start=(bb == 0), stop=(bb == 3))
                                    if bb < 3:
                                        mm.then_inc(S("ikc_used"), 1)
                                else:
                                    mm = pe.matmul(ps[2 + u % 2][:, 0:NS], IQP[0:64, 4 * g + bb].rearrange("p a n -> p (a n)"),
                                                   ikT[0:64, SEQ:T], start=(bb == 0), stop=(bb == 3))
                            mm.then_inc(S("sidx_logits"), 1)
                            if u >= 1:
                                weigh(u - 1, NS if (u - 1) % 5 == 4 else 512)
                    weigh(9, NS)
                    share.point("pe", pe)
                    share.end("pe", pe)

                @block.gpsimd
                def _(pool):
                    pool.memset(qz, 0.0).then_inc(S("qz_zero"), 1)

                @block.scalar
                def _(act):
                    for s in range(4):
                        load_kidx(act, (2, 3), s)
                    for g in range(2):
                        for c in range(5):
                            u = g * 5 + c
                            if c < 4:
                                for bb in range(4):
                                    s = u // 5 * 16 + c * 4 + bb
                                    act.wait_ge(S("kidx_turned"), s + 1)
                                    if s >= 2:
                                        q = s - 2
                                        act.wait_ge(S("ikc_used"), q // 4 * 3 + min(q % 4 + 1, 3))
                                        if q % 4 == 3:
                                            act.wait_ge(S("sidx_logits"), q // 16 * 5 + q % 16 // 4 + 1)
                                    act.activation(ikc[0:64, s % 2, :], ps[s % 2][0:64, :], ACT.Copy).then_inc(S("ikc_ready"), 1)
                                    if s + 4 < len(steps):
                                        load_kidx(act, (2, 3), s + 4)
                                    share.point("act", act)
                            w = 512 if c < 4 else NS
                            act.wait_ge(S("sidx_logits"), u + 1)
                            if u >= 2:
                                act.wait_ge(S("sidx_weighed"), u - 1)
                            act.activation(R[:, u % 2, 0:w], ps[2 + u % 2][:, 0:w], ACT.Relu, scale=0.125).then_inc(S("sidx_relu"), 1)
                    share.point("act", act)
                    share.end("act", act)

                @block.vector
                def _(dve):
                    for h in range(8):
                        r = (h % 2) * 64
                        ins = dve.tensor_copy(iqh[0:64, :, h, :], iqT[r:r + 64, h // 2, SEQ:T].rearrange("p (b t) -> p b t", b=NB))
                    vch.link(dve, ins)
                    bb = K("bb").rearrange("p (a b) -> p a b", a=4)
                    for b in range(NB):
                        ins = dve.tensor_tensor(IQP[0:64, b], bc(iqh[0:64, b].rearrange("p h t -> p (h t)"), 1, 4),
                                                bc(bb[0:64, b % 4], 2, 32), ALU.mult)
                    ins.then_inc(S("iq_padded"), 1)
                    dve.wait_ge(S("w_spread"), 1)
                    for g in range(2):
                        vch.link(dve, dve.tensor_tensor(w8[:, g, :], ps[4][:, g * 8:g * 8 + 8], K("hsel"), ALU.mult))
                        vch.link(dve, dve.tensor_reduce(wcol[:, g:g + 1], w8[:, g, :], AX, ALU.add))
                        ins = dve.tensor_scalar(WS[:, g, :], K("wsel")[:, g * NS:g * NS + NS], wcol[:, g:g + 1], None, ALU.mult)
                    ins.then_inc(S("wsel_ready"), 1)
                    dve.wait_ge(S("qz_zero"), 1)
                    for h in range(8):
                        r, j, g2 = (h % 2) * 64, h // 4, (h // 2) % 2
                        ins = dve.tensor_copy(qz[g2 * 64:g2 * 64 + 64, j, :, h, :], qT[r:r + 64, h // 2, SEQ:T].rearrange("p (b t) -> p b t", b=NB))
                    vch.link(dve, ins)
                    for u in range(10):
                        if u < NB:
                            for j in range(2):
                                dve.tensor_tensor(QP[:, u, j], bc(qz[:, j, u].rearrange("p h t -> p (h t)"), 1, 4),
                                                  bc(bb[:, u % 4], 2, 32), ALU.mult)
                        c, w = u % 5, (512 if u % 5 < 4 else NS)
                        dst = score[0:NS, c * 512:c * 512 + w]
                        dve.wait_ge(S("sidx_weighed"), u + 1)
                        if u < 5:
                            dve.tensor_copy(dst, ps[4 + u % 2][0:NS, 0:w]).then_inc(S("sidx_taken"), 1)
                        else:
                            dve.wait_ge(S("sidx_taken"), u - 4)
                            dve.tensor_tensor(dst, dst, ps[4 + u % 2][0:NS, 0:w], ALU.add).then_inc(S("sidx_taken"), 1)
                    dve.wait_ge(S("sidx_taken"), 10)
                    vch.link(dve, dve.tensor_tensor(score[0:NS, PAST:LK], score[0:NS, PAST:LK], K("neg_s")[0:NS], ALU.add))
                    topk(dve, score[0:NS], work[0:NS], bias[0:NS], m8, TOPK_S)
                    dve.tensor_tensor(bias[0:NS, PAST:LK], bias[0:NS, PAST:LK], K("neg_s")[0:NS], ALU.add)
            ar = Arena(arena, idx_at, keep)
            pages = [ar.take(4, 256) for _ in range(2)]
            KT = ba.take(2, 2, 512)
            pages += [ba.take(4, 256)]
            ar = Arena(arena, keep2, AN)
            St = ar.take(LK)
            Os = ar.take(NB, 256)
            PT = ar.take(17, P)
            mx, sm = ar.take(2), ar.take(4)
            pages += [ar.take(4, 256) for _ in range(3)]

            def k_at(s):
                return s // 16 * 32 + s % 16

            def v_at(s):
                return s // 16 * 32 + 16 + s % 16

            def load_step(eng, which, q):
                g, x = q // 32, q % 16
                if q % 32 < 16:
                    load_pages(eng, which, pages[q % 6], "cache_k", 4 * g + x % 4, x // 4, f"page_in{q % 6}")
                else:
                    load_pages(eng, which, pages[q % 6], "cache_v", 4 * g + x // 4, x % 4, f"page_in{q % 6}")

            def page_used(eng, q):
                s = 16 * (q // 32) + q % 16
                if q % 32 < 16:
                    eng.wait_ge(S("k_turned"), 2 * s + 2)
                else:
                    eng.wait_ge(S("v_used"), s + 1)

            share = Share("dt", [5] + ([0.1] * 16 + [10] + [1.2] * 16) * 2)
            with nc.Block() as block:
                @block.sync
                def _(sp):
                    for q in range(64):
                        if q >= 6:
                            page_used(sp, q - 6)
                        load_step(sp, (0, 1), q)
                    stream(sp, J["dt"] + 3, l)

                @block.tensor
                def _(pe):
                    share.point("pe", pe)

                    def turn(s):
                        q = k_at(s)
                        pe.wait_ge(S(f"page_in{q % 6}"), 64 * (q // 6 + 1))
                        for j in range(2):
                            n = 2 * s + j
                            if n >= 2:
                                pe.wait_ge(S("kt_ready"), n - 1)
                            for pg in range(4):
                                mm = pe.transpose(ps[j][:, pg * P:pg * P + P], pages[q % 6][:, pg, j * P:j * P + P], ident)
                            mm.then_inc(S("k_turned"), 1)

                    for g in range(2):
                        turn(16 * g)
                        for c in range(5):
                            u = g * 10 + c
                            w = 512 if c < 4 else NS
                            if u >= 2:
                                pe.wait_ge(S("sa_taken"), u - 1)
                            for bb in range(4):
                                b = 4 * g + bb
                                s = g * 16 + c * 4 + bb
                                if c < 4:
                                    if (s + 1) % 16:
                                        turn(s + 1)
                                    share.point("pe", pe)
                                    pe.wait_ge(S("kt_ready"), 2 * s + 2)
                                for j in range(2):
                                    rhs = KT[:, s % 2, j, :] if c < 4 else kTs[:, j, :]
                                    mm = pe.matmul(ps[4 + u % 2][:, 0:w], QP[:, b, j].rearrange("p a n -> p (a n)"), rhs,
                                                   start=(bb == 0 and j == 0), stop=False)
                                if c < 4:
                                    mm.then_inc(S("kt_used"), 1)
                            pe.matmul(ps[4 + u % 2][:, 0:w], K("rep")[0:NS, g * P:g * P + P], bias[0:NS, c * 512:c * 512 + w],
                                      start=False, stop=True).then_inc(S("sa_ready"), 1)
                        share.point("pe", pe)
                        for qd in range(5):
                            u = g * 10 + 5 + qd
                            pe.wait_ge(S("sa_taken"), u - 1)
                            pe.wait_ge(S("sprobs_ready"), g + 1)
                            for x in range(4 if qd < 4 else 1):
                                kt = qd * 4 + x
                                m = P if kt < 16 else NS
                                mm = pe.transpose(ps[4 + u % 2][0:m, x * P:x * P + P], St[:, kt * P:kt * P + m], ident)
                            mm.then_inc(S("sa_ready"), 1)
                        pe.wait_ge(S("sa_taken"), g * 10 + 10)
                        for bb in range(4):
                            b = 4 * g + bb
                            for c in range(4):
                                sv = b * 4 + c
                                q = v_at(sv)
                                pe.wait_ge(S(f"page_in{q % 6}"), 64 * (q // 6 + 1))
                                if c == 0 and b >= 2:
                                    pe.wait_ge(S("sv_taken"), b - 1)
                                for pg in range(4):
                                    mm = pe.matmul(ps[2 + b % 2][0:32, 0:256], PT[:, c * 4 + pg, bb * 32:bb * 32 + 32], pages[q % 6][:, pg, :],
                                                   start=(c == 0 and pg == 0), stop=False)
                                mm.then_inc(S("v_used"), 1)
                                share.point("pe", pe)
                            pe.matmul(ps[2 + b % 2][0:32, 0:256], PT[0:NS, 16, bb * 32:bb * 32 + 32], vn[0:NS, 4, :],
                                      start=False, stop=True).then_inc(S("sv_done"), 1)
                    pe.wait_ge(S("sv_taken"), NB)
                    for b in range(NB):
                        for j in range(2):
                            mm = pe.transpose(ps[0][:, j * 256 + b * 32:j * 256 + b * 32 + 32], Os[0:32, b, j * P:j * P + P], ident[0:32, 0:32])
                    mm.then_inc(S("sv_turned"), 1)
                    share.end("pe", pe)

                @block.scalar
                def _(act):
                    for q in range(6):
                        load_step(act, (2, 3), q)
                    share.point("act", act)
                    for g in range(2):
                        for c in range(5):
                            u = g * 10 + c
                            w = 512 if c < 4 else NS
                            if c < 4:
                                for bb in range(4):
                                    s = g * 16 + c * 4 + bb
                                    if s >= 2:
                                        act.wait_ge(S("kt_used"), s - 1)
                                    for j in range(2):
                                        act.wait_ge(S("k_turned"), 2 * s + j + 1)
                                        act.activation(KT[:, s % 2, j, :], ps[j][:, :], ACT.Copy).then_inc(S("kt_ready"), 1)
                                    load_step(act, (2, 3), k_at(s) + 6)
                                    share.point("act", act)
                            act.wait_ge(S("sa_ready"), u + 1)
                            act.activation(St[:, c * 512:c * 512 + w], ps[4 + u % 2][:, 0:w], ACT.Copy, scale=0.125).then_inc(S("sa_taken"), 1)
                        act.wait_ge(S("smax_ready"), g + 1)
                        act.activation(St[:, :], St[:, :], ACT.Exp, bias=mx[:, g:g + 1], accum_out=sm[:, g:g + 1]).then_inc(S("sexp_ready"), 1)
                        share.point("act", act)
                        if g == 1:
                            act.wait_ge(S("sv_done"), 4)
                        for qd in range(5):
                            u = g * 10 + 5 + qd
                            act.wait_ge(S("sa_ready"), u + 1)
                            if qd < 4:
                                ins = act.activation(PT[:, qd * 4:qd * 4 + 4, :], ps[4 + u % 2][:, :].rearrange("p (a n) -> p a n", a=4), ACT.Copy)
                            else:
                                ins = act.activation(PT[0:NS, 16, :], ps[4 + u % 2][0:NS, 0:P], ACT.Copy)
                            ins.then_inc(S("sa_taken"), 1)
                        for bb in range(4):
                            b = 4 * g + bb
                            for c in range(4):
                                share.point("act", act)
                                q = v_at(4 * b + c)
                                if q + 6 < 64:
                                    page_used(act, q)
                                    load_step(act, (2, 3), q + 6)
                            act.wait_ge(S("sv_done"), b + 1)
                            act.activation(Os[0:32, b, :], ps[2 + b % 2][0:32, 0:256], ACT.Copy).then_inc(S("sv_taken"), 1)
                    share.end("act", act)

                @block.vector
                def _(dve):
                    for g in range(2):
                        dve.wait_ge(S("sa_taken"), g * 10 + 5)
                        dve.tensor_reduce(mx[:, g:g + 1], St[:, :], AX, ALU.max, negate=True).then_inc(S("smax_ready"), 1)
                        dve.wait_ge(S("sexp_ready"), g + 1)
                        vch.link(dve, dve.reciprocal(sm[:, 2 + g:3 + g], sm[:, g:g + 1]))
                        dve.tensor_scalar(St[:, :], St[:, :], sm[:, 2 + g:3 + g], None, ALU.mult).then_inc(S("sprobs_ready"), 1)
                    dve.wait_ge(S("sv_turned"), 1)
                    for h in range(8):
                        r, j, g2 = (h % 2) * 64, h // 4, (h // 2) % 2
                        src = ps[0][g2 * 64:g2 * 64 + 64, :].rearrange("p (j b h t) -> p j b h t", j=2, b=NB, h=8)[:, j, :, h, :]
                        dve.tensor_copy(brT[r:r + 64, h // 2, SEQ:T].rearrange("p (b t) -> p b t", b=NB), src)

        GAMMA = [1.0 - 2.0 ** (-5 - h) for h in range(4)]

        def stage_linear(l, kind):
            lay = bass.ds(l, 1)
            ret = kind == "r"
            br0 = 4 if ret else 8

            def Z(name):
                return S(kind + "_" + name)

            ar = Arena(arena, 0, ANB)
            sc = Arena(brT_, (8 if ret else 12) * T, 16 * T)
            inputs = ar.take(2, 4, 512)
            q, k, v, g = ((lambda i, n=n: inputs[:, i % 2, n]) for n in range(4))
            S0 = ar.take(NB, 4, P)
            Sp = ar.take(4, P)
            qT, kT, A = sc.take(4 * P), sc.take(4 * P), sc.take(4 * P)
            kd = sc.take(512)
            t1, t2 = ar.take(512), ar.take(512)
            sm = ar.take(3, 4)
            dec = ar.take(NB, 4)
            if ret:
                qr, kr = sc.take(512), sc.take(512)
                E = None
            else:
                sf = ar.take(512)
                sc = Arena(brT_, 0, 4 * T)
                E = sc.take(512)
            Vx, qm = sc.take(NB, P), ar.take(NB, NS)
            nlv = [7, 7, 7, 7, 2]
            lv0 = [0, 7, 14, 21, 28]
            per_tile = [4 + (0 if ret else 3 * nlv[i]) for i in range(5)]
            share = Share("wb01" if ret else "wb11", [1] * sum(per_tile))
            row0 = 0 if ret else 4
            job0 = J["gate01" if ret else "gate11"]
            with nc.Block() as block:
                @block.tensor
                def _(pe):
                    for i, (t0, m) in enumerate(tiles):
                        last = i == 4
                        triu, aft = (K("tri_s")[0:NS], K("after_s")[0:NS]) if last else (tri, after)
                        if i >= 1:
                            pe.wait_ge(Z("y_taken"), i)
                        if not ret:
                            pe.wait_ge(Z("logf"), i + 1)
                            pe.matmul(ps[3][0:m, :], triu, sf[0:m, :])
                            mm = pe.matmul(ps[4][0:m, :], aft, sf[0:m, :])
                            for h in range(4):
                                w = sf[0:m, h * P:h * P + P]
                                if last:
                                    mm = pe.matmul(ps[5][:, h * NB:h * NB + NB], w, K("seqhot")[0:NS])
                                else:
                                    mm = pe.matmul(ps[5][:, h:h + 1], w, ones[:, 0:1])
                            mm.then_inc(Z("cum"), 1)
                            for x in range(nlv[i]):
                                n = lv0[i] + x
                                pe.matmul(ps[0][0:m, :], K("lv_sum").rearrange("p (l t) -> p l t", l=7)[0:m, x, 0:m], sf[0:m, :]).then_inc(Z("lv_z"), 1)
                                share.point("pe", pe)
                                pe.wait_ge(Z("lv_x"), n + 1)
                                for h in range(4):
                                    mm = pe.transpose(ps[1][:, h * m:h * m + m], t2[0:m, h * P:h * P + P], ident[0:m, 0:m])
                                mm.then_inc(Z("lv_turned"), 1)
                                share.point("pe", pe)
                                pe.wait_ge(Z("lv_turn_taken"), n + 1)
                                if n >= 1:
                                    pe.wait_ge(Z("lv_added"), n)
                                for h in range(4):
                                    xT_h = kT[:, h * m:h * m + m]
                                    mm = pe.matmul(ps[2][0:m, h * m:h * m + m], xT_h, xT_h)
                                mm.then_inc(Z("lv_product"), 1)
                                share.point("pe", pe)
                        pe.wait_ge(Z("qk_ready" if ret else "weights"), i + 1)
                        for h in range(4):
                            mm = pe.transpose(ps[0][:, h * m:h * m + m], (qr if ret else t1)[0:m, h * P:h * P + P], ident[0:m, 0:m])
                        if ret:
                            for h in range(4):
                                mm = pe.transpose(ps[1][:, h * m:h * m + m], kr[0:m, h * P:h * P + P], ident[0:m, 0:m])
                        mm.then_inc(Z("turned"), 1)
                        share.point("pe", pe)
                        pe.wait_ge(Z("turn_taken"), i + 1)
                        if ret:
                            for h in range(4):
                                mm = pe.matmul(ps[2][0:m, h * m:h * m + m], kT[:, h * m:h * m + m], qT[:, h * m:h * m + m])
                            mm.then_inc(Z("scores"), 1)
                        share.point("pe", pe)
                        pe.wait_ge(Z("weights"), i + 1)
                        if last:
                            pe.wait_ge(Z("state_in"), 64)
                        for h in range(4):
                            o = ps[3][0:m, h * P:h * P + P]
                            mm = pe.matmul(o, A[0:m, h * m:h * m + m], v(i)[0:m, h * P:h * P + P], start=True, stop=(i == 0))
                            if last:
                                pe.wait_ge(Z("q_masked"), h + 1)
                                for b in range(NB):
                                    mm = pe.matmul(o, qm[:, b, :], S0[:, b, h, :], start=False, stop=(b == NB - 1))
                                mm.then_inc(Z("q_mask_used"), 1)
                            elif i > 0:
                                mm = pe.matmul(o, qT[:, h * m:h * m + m], Sp[:, h, :], start=False, stop=True)
                        if not last:
                            for h in range(4):
                                mm = pe.matmul(ps[4][:, h * P:h * P + P], kd[0:m, h * P:h * P + P], v(i)[0:m, h * P:h * P + P])
                            mm.then_inc(Z("out"), 1)
                        else:
                            for h in range(4):
                                pe.wait_ge(Z("v_masked"), h + 1)
                                for half in range(2):
                                    n = 2 * h + half
                                    if n >= 2:
                                        pe.wait_ge(Z("state_new"), n - 1)
                                    pe.matmul(ps[n % 2][:, :], kd[0:NS, h * P:h * P + P],
                                              Vx[0:NS, half * 4:half * 4 + 4, :].rearrange("p b e -> p (b e)")).then_inc(Z("state_add"), 1)
                        share.point("pe", pe)
                        pe.wait_ge(Z("y"), i + 1)
                        for h in range(4):
                            mm = pe.transpose(ps[5][:, h * m:h * m + m], t2[0:m, h * P:h * P + P], ident[0:m, 0:m])
                        mm.then_inc(Z("y_turned"), 1)
                        share.point("pe", pe)
                    share.end("pe", pe)

                @block.scalar
                def _(act):
                    for i, (t0, m) in enumerate(tiles):
                        last = i == 4
                        act.wait_ge(Z(f"tile_in{i % 2}"), 16 * (i // 2 + 1))
                        if not ret:
                            act.activation(sf[0:m, :], k(i)[0:m, :], ACT.Sigmoid)
                            ach.link(act, act.activation(q(i)[0:m, :], q(i)[0:m, :], ACT.Silu))
                            act.activation(k(i)[0:m, :], k(i)[0:m, :], ACT.Sigmoid, scale=-1.0)
                        act.activation(g(i)[0:m, :], g(i)[0:m, :], ACT.Silu).then_inc(Z("inputs"), 1)
                        if not ret:
                            act.wait_ge(Z("forget"), i + 1)
                            act.activation(t1[0:m, :], t1[0:m, :], ACT.Ln)
                            act.activation(t2[0:m, :], t2[0:m, :], ACT.Ln).then_inc(Z("logs"), 1)
                            act.wait_ge(Z("cum"), i + 1)
                            act.activation(E[0:m, :], ps[3][0:m, :], ACT.Exp)
                            act.activation(t1[0:m, :], ps[4][0:m, :], ACT.Exp)
                            if last:
                                ins = act.activation(dec, ps[5][:, 0:4 * NB].rearrange("p (h b) -> p b h", h=4), ACT.Exp)
                            else:
                                ins = act.activation(dec[:, 0, :], ps[5][:, 0:4], ACT.Exp)
                            ins.then_inc(Z("decays"), 1)
                            for x in range(nlv[i]):
                                n = lv0[i] + x
                                act.wait_ge(Z("lv_z"), n + 1)
                                act.wait_ge(Z("lv_e_free"), n + 1)
                                act.activation(E[0:m, :], ps[0][0:m, :], ACT.Exp).then_inc(Z("lv_e"), 1)
                                share.point("act", act)
                                act.wait_ge(Z("lv_turned"), n + 1)
                                act.activation(kT[:, 0:4 * m], ps[1][:, 0:4 * m], ACT.Copy).then_inc(Z("lv_turn_taken"), 1)
                                share.point("act", act)
                                share.point("act", act)
                        act.wait_ge(Z("turned"), i + 1)
                        if ret:
                            act.activation(kT[:, 0:4 * m], ps[1][:, 0:4 * m], ACT.Copy)
                        act.activation(qT[:, 0:4 * m], ps[0][:, 0:4 * m], ACT.Copy).then_inc(Z("turn_taken"), 1)
                        share.point("act", act)
                        share.point("act", act)
                        share.point("act", act)
                        act.wait_ge(Z("sq"), i + 1)
                        ach.link(act, act.activation(sm[0:m, 1, :], sm[0:m, 1, :], ACT.Ln, bias=eps[0:m], scale=1.0 / P))
                        act.activation(sm[0:m, 1, :], sm[0:m, 1, :], ACT.Exp, scale=-0.5).then_inc(Z("rstd"), 1)
                        act.wait_ge(Z("y_turned"), i + 1)
                        act.activation(brT[:, br0:br0 + 4, t0:t0 + m], ps[5][:, 0:4 * m].rearrange("p (h t) -> p h t", h=4), ACT.Copy).then_inc(Z("y_taken"), 1)
                        share.point("act", act)
                    share.end("act", act)

                @block.vector
                def _(dve):
                    hv = lambda a, m: a[0:m, :].rearrange("p (h d) -> p h d", h=4)
                    L = vch.link
                    for i, (t0, m) in enumerate(tiles):
                        last = i == 4
                        dve.wait_ge(Z("inputs"), i + 1)
                        if ret:
                            cs = bc(K("cos").rearrange("p (t f) -> p t f", t=5)[0:m, i, :], 1, 4)
                            sn = bc(K("sin").rearrange("p (t f) -> p t f", t=5)[0:m, i, :], 1, 4)
                            a1, a2 = hv(t1, m)[:, :, 0:64], hv(t1, m)[:, :, 64:128]
                            if i >= 1:
                                dve.wait_ge(Z("y_turned"), i)
                            for src, dst in ((q, qr), (k, kr)):
                                x1, x2 = hv(src(i), m)[:, :, 0:64], hv(src(i), m)[:, :, 64:128]
                                y1, y2 = hv(dst, m)[:, :, 0:64], hv(dst, m)[:, :, 64:128]
                                dve.tensor_tensor(y1, x1, cs, ALU.mult)
                                dve.tensor_tensor(a1, x2, sn, ALU.mult)
                                dve.tensor_tensor(y2, x1, sn, ALU.mult)
                                L(dve, dve.tensor_tensor(a2, x2, cs, ALU.mult))
                                dve.tensor_tensor(y1, y1, a1, ALU.subtract)
                                L(dve, dve.tensor_tensor(y2, y2, a2, ALU.add))
                            L(dve, dve.tensor_tensor(hv(qr, m), hv(qr, m), bc(K("rq_s" if last else "rq")[0:m], 2, P), ALU.mult))
                            dve.tensor_tensor(hv(kd, m), hv(kr, m), bc(K("rk_s" if last else "rk")[0:m], 2, P), ALU.mult).then_inc(Z("qk_ready"), 1)
                            share.point("dve", dve)
                            dve.wait_ge(Z("scores"), i + 1)
                            dve.tensor_tensor(A[0:m, 0:4 * m], ps[2][0:m, 0:4 * m], K("rdec_s" if last else "rdec")[0:m], ALU.mult).then_inc(Z("weights"), 1)
                        else:
                            qi, ki, fi = q(i)[0:m, :], k(i)[0:m, :], sf[0:m, :]
                            if i >= 1:
                                dve.wait_ge(Z("y_turned"), i)
                            L(dve, dve.tensor_tensor(fi, fi, oml[0:m], ALU.mult))
                            L(dve, dve.tensor_tensor(fi, fi, lb[0:m], ALU.add))
                            dve.tensor_scalar(t1[0:m, :], fi, 2.0 ** -60, None, ALU.max)
                            L(dve, dve.tensor_scalar(t2[0:m, :], fi, 1e-30, 2.0 ** -60, ALU.max, ALU.min))
                            dve.tensor_scalar(t2[0:m, :], t2[0:m, :], 2.0 ** 60, None, ALU.mult).then_inc(Z("forget"), 1)
                            dve.tensor_tensor(ki, ki, oml[0:m], ALU.mult)
                            L(dve, dve.tensor_scalar(qi, qi, P ** -0.5, None, ALU.mult))
                            dve.wait_ge(Z("logs"), i + 1)
                            L(dve, dve.tensor_tensor(fi, t1[0:m, :], t2[0:m, :], ALU.add))
                            dve.tensor_tensor(t2[0:m, :], qi, ki, ALU.mult).then_inc(Z("logf"), 1)
                            dve.wait_ge(Z("logf"), i + 1)
                            L(dve, dve.tensor_reduce(sm[0:m, 2, :], hv(t2, m), AX, ALU.add))
                            dve.wait_ge(Z("decays"), i + 1)
                            L(dve, dve.tensor_tensor(kd[0:m, :], ki, t1[0:m, :], ALU.mult))
                            L(dve, dve.tensor_tensor(t1[0:m, :], qi, E[0:m, :], ALU.mult))
                            L(dve, dve.tensor_tensor(qi, qi, ki, ALU.subtract))
                            dve.memset(A[0:m, 0:4 * m], 0.0).then_inc(Z("lv_e_free"), 1)
                            dve.wait_ge(Z("lv_e_free"), lv0[i] + 1)
                            for x in range(nlv[i]):
                                n = lv0[i] + x
                                L(dve, dve.scalar_tensor_tensor(t2[0:m, :], qi, K("lv_side")[0:m, x:x + 1], ki, ALU.mult, ALU.add))
                                dve.wait_ge(Z("lv_e"), n + 1)
                                dve.tensor_tensor(t2[0:m, :], t2[0:m, :], E[0:m, :], ALU.mult).then_inc(Z("lv_x"), 1)
                                share.point("dve", dve)
                                share.point("dve", dve)
                                dve.wait_ge(Z("lv_product"), n + 1)
                                msk = bc(K("lv_mask").rearrange("p (l t) -> p l t", l=7)[0:m, x, 0:m], 1, 4)
                                dm = t2[0:m, 0:4 * m].rearrange("p (h n) -> p h n", h=4)
                                dve.tensor_tensor(dm, ps[2][0:m, 0:4 * m].rearrange("p (h n) -> p h n", h=4), msk, ALU.mult).then_inc(Z("lv_added"), 1)
                                dve.wait_ge(Z("lv_added"), n + 1)
                                ins = dve.tensor_tensor(A[0:m, 0:4 * m], A[0:m, 0:4 * m], t2[0:m, 0:4 * m], ALU.add)
                                if x < nlv[i] - 1:
                                    ins.then_inc(Z("lv_e_free"), 1)
                                    dve.wait_ge(Z("lv_e_free"), n + 2)
                                else:
                                    ins.then_inc(Z("weights"), 1)
                                share.point("dve", dve)
                        share.point("dve", dve)
                        if not ret:
                            share.point("dve", dve)
                        if last:
                            dve.wait_ge(Z("turn_taken"), i + 1)
                            msk = K("qmask").rearrange("p (b t) -> p b t", b=NB)
                            for h in range(4):
                                if h >= 1:
                                    dve.wait_ge(Z("q_mask_used"), h)
                                dve.tensor_tensor(qm, bc(qT[:, h * NS:h * NS + NS], 1, NB), msk, ALU.mult).then_inc(Z("q_masked"), 1)
                            for h in range(4):
                                if h >= 1:
                                    dve.wait_ge(Z("state_add"), 2 * h)
                                dve.tensor_tensor(Vx[0:NS], bc(v(4)[0:NS, h * P:h * P + P], 1, NB), bc(K("seqhot")[0:NS], 2, P), ALU.mult).then_inc(Z("v_masked"), 1)
                                for half in range(2):
                                    n = 2 * h + half
                                    dve.wait_ge(Z("state_add"), n + 1)
                                    if h == 0 and half == 0:
                                        dve.wait_ge(Z("q_mask_used"), 4)
                                    st = S0[:, half * 4:half * 4 + 4, h, :]
                                    add = ps[n % 2][:, :].rearrange("p (b e) -> p b e", b=4)
                                    if ret:
                                        dve.scalar_tensor_tensor(st, st, GAMMA[h] ** TS, add, ALU.mult, ALU.add).then_inc(Z("state_new"), 1)
                                    else:
                                        L(dve, dve.tensor_tensor(st, st, bc(dec[:, half * 4:half * 4 + 4, h], 2, P), ALU.mult))
                                        dve.tensor_tensor(st, st, add, ALU.add).then_inc(Z("state_new"), 1)
                        else:
                            dve.wait_ge(Z("out"), i + 1)
                            for h in range(4):
                                add = ps[4][:, h * P:h * P + P]
                                if i == 0:
                                    ins = dve.tensor_copy(Sp[:, h, :], add)
                                else:
                                    ins = dve.scalar_tensor_tensor(Sp[:, h, :], Sp[:, h, :], GAMMA[h] ** P if ret else dec[:, 0, h:h + 1], add, ALU.mult, ALU.add)
                            if i == 3:
                                ins.then_inc(Z("prompt_state"), 1)
                            else:
                                L(dve, ins)
                        share.point("dve", dve)
                        o = hv(ps[3], m)
                        y, w = hv(t2, m), hv(t1, m)
                        if ret:
                            L(dve, dve.tensor_reduce(sm[0:m, 0, :], o, AX, ALU.add))
                            L(dve, dve.tensor_scalar(sm[0:m, 0, :], sm[0:m, 0, :], 1.0 / P, None, ALU.mult))
                            L(dve, dve.tensor_tensor(y, o, bc(sm[0:m, 0, :], 2, P), ALU.subtract))
                        else:
                            for h in range(4):
                                ins = dve.scalar_tensor_tensor(y[:, h], hv(v(i), m)[:, h], sm[0:m, 2, h:h + 1], o[:, h], ALU.mult, ALU.add)
                            L(dve, ins)
                        if not ret:
                            dve.wait_ge(Z("turned"), i + 1)
                        L(dve, dve.tensor_tensor(w, y, y, ALU.mult))
                        dve.tensor_reduce(sm[0:m, 1, :], w, AX, ALU.add).then_inc(Z("sq"), 1)
                        dve.wait_ge(Z("rstd"), i + 1)
                        L(dve, dve.tensor_tensor(y, y, bc(sm[0:m, 1, :], 2, P), ALU.mult))
                        if not ret:
                            L(dve, dve.tensor_tensor(y, y, bc(ghg[0:m], 1, 4), ALU.mult))
                        dve.tensor_tensor(t2[0:m, :], t2[0:m, :], g(i)[0:m, :], ALU.mult).then_inc(Z("y"), 1)
                        share.point("dve", dve)
                    share.end("dve", dve)

                @block.sync
                def _(sp):
                    for w in range(4):
                        sp.wait_ge(S(f"spilled{w}"), 16 * (5 if ret else 10))
                    for i, (t0, m) in enumerate(tiles):
                        if i >= 2:
                            sp.wait_ge(Z("y"), i - 1)
                        sp.dma_start(inputs[0:m, i % 2], spill[row0:row0 + 4, t0:t0 + m, :].rearrange("j t n -> t j n")).then_inc(Z(f"tile_in{i % 2}"), 16)
                        if i == 1:
                            name = "state_ret" if ret else "state_hgrn"
                            for b in range(0, NB, 2):
                                sp.dma_start(S0[:, b:b + 2].rearrange("p b h e -> p (b h) e"),
                                             inp[name][lay, b:b + 2].rearrange("o b h d e -> d (o b h) e")).then_inc(Z("state_in"), 16)
                        if i >= 2:
                            stream(sp, min(job0 + i - 1, job0 + 2), l)
                    name = "ret" if ret else "hgrn"
                    sp.wait_ge(Z("prompt_state"), 1)
                    sp.dma_start(out[name + "_prompt"][lay].rearrange("o b h d e -> d (o b h) e"), Sp).then_inc(S("ret_stored"), 16)
                    stream(sp, job0 + 4, l)
                    sp.wait_ge(Z("state_new"), 8)
                    sp.dma_start(out[name + "_sample"][lay].rearrange("o b h d e -> d (o b h) e"), S0.rearrange("p b h e -> p (b h) e")).then_inc(S("ret_stored"), 16)

        def stage_hgrn(l):
            lay = bass.ds(l, 1)
            ar = Arena(arena, 0, ANB)
            inputs = ar.take(2, 4, 512)
            q, k, v, g = ((lambda i, n=n: inputs[:, i % 2, n]) for n in range(4))
            S0 = ar.take(NB, 4, P)
            Sp = ar.take(4, P)
            t1, t2 = ar.take(512), ar.take(512)
            sm = ar.take(3, 4)
            dec = ar.take(NB, 4)
            sf = ar.take(512)
            qm = ar.take(NB, NS)
            sc = Arena(brT_, 12 * T, 16 * T)
            qT, kT0, A, kd = sc.take(4 * P), sc.take(4 * P), sc.take(4 * P), sc.take(512)
            sc = Arena(brT_, 0, 4 * T)
            E = sc.take(2, 512)
            Vx = sc.take(NB, P)
            vx = Vx.rearrange("p b e -> p (b e)")
            D, kT = vx[:, 0:512], (kT0, vx[:, 512:1024])
            F1, F2 = vx[:, 0:512], vx[:, 512:1024]
            nlv = [7, 7, 7, 7, 2]
            lv0 = [0, 7, 14, 21, 28]
            weights = [4]
            for i in range(5):
                weights += [1] * (2 * nlv[i] + 2) + [2, 2, 2]
            share = Share("wb11", weights)
            job0 = J["gate11"]
            zbank = (0, 5)
            with nc.Block() as block:
                @block.tensor
                def _(pe):
                    def z_sums(i, x):
                        m = tiles[i][1]
                        if x < nlv[i]:
                            pe.matmul(ps[zbank[x % 2]][0:m, :], K("lv_sum").rearrange("p (l t) -> p l t", l=7)[0:m, x, 0:m], sf[0:m, :]).then_inc(S("c_lv_z"), 1)

                    def start_tile(i):
                        m = tiles[i][1]
                        last = i == 4
                        triu, aft = (K("tri_s")[0:NS], K("after_s")[0:NS]) if last else (tri, after)
                        pe.wait_ge(S("c_logf"), i + 1)
                        pe.matmul(ps[3][0:m, :], triu, sf[0:m, :])
                        pe.matmul(ps[4][0:m, :], aft, sf[0:m, :])
                        for h in range(4):
                            w = sf[0:m, h * P:h * P + P]
                            if last:
                                mm = pe.matmul(ps[5][:, h * NB:h * NB + NB], w, K("seqhot")[0:NS])
                            else:
                                mm = pe.matmul(ps[5][:, h:h + 1], w, ones[:, 0:1])
                        mm.then_inc(S("c_cum"), 1)
                        z_sums(i, 0)
                        pe.wait_ge(S("c_decays"), i + 1)
                        z_sums(i, 1)

                    share.point("pe", pe)
                    start_tile(0)
                    for i, (t0, m) in enumerate(tiles):
                        last = i == 4
                        pe.wait_ge(S("c_q_decayed"), i + 1)
                        for h in range(4):
                            mm = pe.transpose(ps[2][:, h * m:h * m + m], t1[0:m, h * P:h * P + P], ident[0:m, 0:m])
                        mm.then_inc(S("c_turned"), 1)
                        if i >= 1:
                            pe.wait_ge(S("c_y_taken"), i)
                        for x in range(nlv[i] + 1):
                            n = lv0[i] + x
                            if x < nlv[i]:
                                pe.wait_ge(S("c_lv_x"), n + 1)
                                if n >= 1:
                                    pe.wait_ge(S("c_lv_turn_taken"), n)
                                for h in range(4):
                                    mm = pe.transpose(ps[1][:, h * m:h * m + m], t2[0:m, h * P:h * P + P], ident[0:m, 0:m])
                                mm.then_inc(S("c_lv_turned"), 1)
                                z_sums(i, x + 2)
                            share.point("pe", pe)
                            if x >= 1:
                                pe.wait_ge(S("c_lv_turn_taken"), n)
                                if x == 1:
                                    pe.wait_ge(S("c_turn_taken"), i + 1)
                                if n >= 2:
                                    pe.wait_ge(S("c_lv_masked"), n - 1)
                                for h in range(4):
                                    xT_h = kT[(x - 1) % 2][:, h * m:h * m + m]
                                    mm = pe.matmul(ps[2][0:m, h * m:h * m + m], xT_h, xT_h)
                                mm.then_inc(S("c_lv_product"), 1)
                            share.point("pe", pe)
                        pe.wait_ge(S("c_weights"), i + 1)
                        if last:
                            pe.wait_ge(S("c_state_in"), 64)
                        for h in range(4):
                            o = ps[3][0:m, h * P:h * P + P]
                            mm = pe.matmul(o, A[0:m, h * m:h * m + m], v(i)[0:m, h * P:h * P + P], start=True, stop=(i == 0))
                            if last:
                                pe.wait_ge(S("c_q_masked"), h + 1)
                                for b in range(NB):
                                    mm = pe.matmul(o, qm[:, b, :], S0[:, b, h, :], start=False, stop=(b == NB - 1))
                                mm.then_inc(S("c_q_mask_used"), 1)
                            elif i > 0:
                                mm = pe.matmul(o, qT[:, h * m:h * m + m], Sp[:, h, :], start=False, stop=True)
                        if not last:
                            for h in range(4):
                                mm = pe.matmul(ps[4][:, h * P:h * P + P], kd[0:m, h * P:h * P + P], v(i)[0:m, h * P:h * P + P])
                            mm.then_inc(S("c_out"), 1)
                        else:
                            for h in range(4):
                                pe.wait_ge(S("c_v_masked"), h + 1)
                                for half in range(2):
                                    n = 2 * h + half
                                    if n >= 2:
                                        pe.wait_ge(S("c_state_new"), n - 1)
                                    pe.matmul(ps[(0, 5)[n % 2]][:, :], kd[0:NS, h * P:h * P + P],
                                              Vx[0:NS, half * 4:half * 4 + 4, :].rearrange("p b e -> p (b e)")).then_inc(S("c_state_add"), 1)
                        share.point("pe", pe)
                        if not last:
                            start_tile(i + 1)
                        share.point("pe", pe)
                        pe.wait_ge(S("c_y"), i + 1)
                        for h in range(4):
                            mm = pe.transpose(ps[1][:, h * m:h * m + m], t2[0:m, h * P:h * P + P], ident[0:m, 0:m])
                        mm.then_inc(S("c_y_turned"), 1)
                        share.point("pe", pe)
                    share.end("pe", pe)

                @block.scalar
                def _(act):
                    def gates(i):
                        m = tiles[i][1]
                        act.wait_ge(S(f"c_tile_in{i % 2}"), 16 * (i // 2 + 1))
                        act.activation(sf[0:m, :], k(i)[0:m, :], ACT.Sigmoid)
                        ach.link(act, act.activation(q(i)[0:m, :], q(i)[0:m, :], ACT.Silu))
                        act.activation(k(i)[0:m, :], k(i)[0:m, :], ACT.Sigmoid, scale=-1.0)
                        act.activation(g(i)[0:m, :], g(i)[0:m, :], ACT.Silu).then_inc(S("c_inputs"), 1)
                        act.wait_ge(S("c_forget"), i + 1)
                        act.activation(F1[0:m, :], F1[0:m, :], ACT.Ln)
                        act.activation(F2[0:m, :], F2[0:m, :], ACT.Ln).then_inc(S("c_logs"), 1)

                    def decays(i):
                        m = tiles[i][1]
                        act.wait_ge(S("c_cum"), i + 1)
                        act.activation(E[0:m, 1, :], ps[3][0:m, :], ACT.Exp)
                        act.activation(t1[0:m, :], ps[4][0:m, :], ACT.Exp)
                        if i == 4:
                            ins = act.activation(dec, ps[5][:, 0:4 * NB].rearrange("p (h b) -> p b h", h=4), ACT.Exp)
                        else:
                            ins = act.activation(dec[:, 0, :], ps[5][:, 0:4], ACT.Exp)
                        ins.then_inc(S("c_decays"), 1)
                        level_decay(i, 0)

                    def level_decay(i, x):
                        m = tiles[i][1]
                        if x < nlv[i]:
                            act.wait_ge(S("c_lv_z"), lv0[i] + x + 1)
                            if x == 1:
                                act.wait_ge(S("c_q_decayed"), i + 1)
                            if x >= 2:
                                act.wait_ge(S("c_lv_x"), lv0[i] + x - 1)
                            act.activation(E[0:m, x % 2, :], ps[zbank[x % 2]][0:m, :], ACT.Exp).then_inc(S("c_lv_e"), 1)

                    gates(0)
                    share.point("act", act)
                    decays(0)
                    for i, (t0, m) in enumerate(tiles):
                        level_decay(i, 1)
                        act.wait_ge(S("c_turned"), i + 1)
                        act.activation(qT[:, 0:4 * m], ps[2][:, 0:4 * m], ACT.Copy).then_inc(S("c_turn_taken"), 1)
                        for x in range(nlv[i] + 1):
                            n = lv0[i] + x
                            if x < nlv[i]:
                                act.wait_ge(S("c_lv_turned"), n + 1)
                                if n >= 2:
                                    act.wait_ge(S("c_lv_product"), n - 1)
                                act.activation(kT[x % 2][:, 0:4 * m], ps[1][:, 0:4 * m], ACT.Copy).then_inc(S("c_lv_turn_taken"), 1)
                                level_decay(i, x + 2)
                            share.point("act", act)
                            share.point("act", act)
                        if i < 4:
                            gates(i + 1)
                        act.wait_ge(S("c_sq"), i + 1)
                        ach.link(act, act.activation(sm[0:m, 1, :], sm[0:m, 1, :], ACT.Ln, bias=eps[0:m], scale=1.0 / P))
                        act.activation(sm[0:m, 1, :], sm[0:m, 1, :], ACT.Exp, scale=-0.5).then_inc(S("c_rstd"), 1)
                        share.point("act", act)
                        if i < 4:
                            decays(i + 1)
                        share.point("act", act)
                        act.wait_ge(S("c_y_turned"), i + 1)
                        act.activation(brT[:, 8:12, t0:t0 + m], ps[1][:, 0:4 * m].rearrange("p (h t) -> p h t", h=4), ACT.Copy).then_inc(S("c_y_taken"), 1)
                        share.point("act", act)
                    share.end("act", act)

                @block.vector
                def _(dve):
                    hv = lambda a, m: a[0:m, :].rearrange("p (h d) -> p h d", h=4)
                    L = vch.link

                    def forget(i):
                        m = tiles[i][1]
                        qi, ki, fi = q(i)[0:m, :], k(i)[0:m, :], sf[0:m, :]
                        dve.wait_ge(S("c_inputs"), i + 1)
                        L(dve, dve.tensor_tensor(fi, fi, oml[0:m], ALU.mult))
                        L(dve, dve.tensor_tensor(fi, fi, lb[0:m], ALU.add))
                        dve.tensor_scalar(F1[0:m, :], fi, 2.0 ** -60, None, ALU.max)
                        L(dve, dve.tensor_scalar(F2[0:m, :], fi, 1e-30, 2.0 ** -60, ALU.max, ALU.min))
                        dve.tensor_scalar(F2[0:m, :], F2[0:m, :], 2.0 ** 60, None, ALU.mult).then_inc(S("c_forget"), 1)
                        dve.tensor_tensor(ki, ki, oml[0:m], ALU.mult)
                        L(dve, dve.tensor_scalar(qi, qi, P ** -0.5, None, ALU.mult))

                    def log_forget(i):
                        m = tiles[i][1]
                        dve.wait_ge(S("c_logs"), i + 1)
                        L(dve, dve.tensor_tensor(sf[0:m, :], F1[0:m, :], F2[0:m, :], ALU.add))
                        dve.tensor_tensor(F2[0:m, :], q(i)[0:m, :], k(i)[0:m, :], ALU.mult).then_inc(S("c_logf"), 1)
                        dve.wait_ge(S("c_logf"), i + 1)
                        L(dve, dve.tensor_reduce(sm[0:m, 2, :], hv(F2, m), AX, ALU.add))

                    share.point("dve", dve)
                    forget(0)
                    log_forget(0)
                    for i, (t0, m) in enumerate(tiles):
                        last = i == 4
                        qi, ki, fi = q(i)[0:m, :], k(i)[0:m, :], sf[0:m, :]
                        dve.wait_ge(S("c_decays"), i + 1)
                        L(dve, dve.tensor_tensor(kd[0:m, :], ki, t1[0:m, :], ALU.mult))
                        dve.tensor_tensor(t1[0:m, :], qi, E[0:m, 1, :], ALU.mult).then_inc(S("c_q_decayed"), 1)
                        dve.wait_ge(S("c_q_decayed"), i + 1)
                        L(dve, dve.tensor_tensor(qi, qi, ki, ALU.subtract))
                        if i >= 1:
                            dve.wait_ge(S("c_y_turned"), i)

                        def level_x(x):
                            n = lv0[i] + x
                            if x >= 1:
                                dve.wait_ge(S("c_lv_turned"), n)
                            L(dve, dve.scalar_tensor_tensor(t2[0:m, :], qi, K("lv_side")[0:m, x:x + 1], ki, ALU.mult, ALU.add))
                            dve.wait_ge(S("c_lv_e"), n + 1)
                            dve.tensor_tensor(t2[0:m, :], t2[0:m, :], E[0:m, x % 2, :], ALU.mult).then_inc(S("c_lv_x"), 1)

                        def level_add(x):
                            n = lv0[i] + x
                            dve.wait_ge(S("c_lv_product"), n + 1)
                            msk = bc(K("lv_mask").rearrange("p (l t) -> p l t", l=7)[0:m, x, 0:m], 1, 4)
                            dst = A if x == 0 else D
                            dve.tensor_tensor(dst[0:m, 0:4 * m].rearrange("p (h n) -> p h n", h=4),
                                              ps[2][0:m, 0:4 * m].rearrange("p (h n) -> p h n", h=4), msk, ALU.mult).then_inc(S("c_lv_masked"), 1)
                            dve.wait_ge(S("c_lv_masked"), n + 1)
                            if x:
                                ins = dve.tensor_tensor(A[0:m, 0:4 * m], A[0:m, 0:4 * m], D[0:m, 0:4 * m], ALU.add)
                                if x == nlv[i] - 1:
                                    ins.then_inc(S("c_weights"), 1)
                                else:
                                    L(dve, ins)

                        for x in range(nlv[i] + 2):
                            if x < nlv[i]:
                                level_x(x)
                            if x >= 1:
                                share.point("dve", dve)
                            if x >= 2:
                                level_add(x - 2)
                            if x <= nlv[i]:
                                share.point("dve", dve)
                        dve.wait_ge(S("c_weights"), i + 1)
                        if last:
                            dve.wait_ge(S("c_turn_taken"), i + 1)
                            msk = K("qmask").rearrange("p (b t) -> p b t", b=NB)
                            for h in range(4):
                                if h >= 1:
                                    dve.wait_ge(S("c_q_mask_used"), h)
                                dve.tensor_tensor(qm, bc(qT[:, h * NS:h * NS + NS], 1, NB), msk, ALU.mult).then_inc(S("c_q_masked"), 1)
                            for h in range(4):
                                if h >= 1:
                                    dve.wait_ge(S("c_state_add"), 2 * h)
                                dve.tensor_tensor(Vx[0:NS], bc(v(4)[0:NS, h * P:h * P + P], 1, NB), bc(K("seqhot")[0:NS], 2, P), ALU.mult).then_inc(S("c_v_masked"), 1)
                                for half in range(2):
                                    n = 2 * h + half
                                    dve.wait_ge(S("c_state_add"), n + 1)
                                    if h == 0 and half == 0:
                                        dve.wait_ge(S("c_q_mask_used"), 4)
                                    st = S0[:, half * 4:half * 4 + 4, h, :]
                                    add = ps[(0, 5)[n % 2]][:, :].rearrange("p (b e) -> p b e", b=4)
                                    L(dve, dve.tensor_tensor(st, st, bc(dec[:, half * 4:half * 4 + 4, h], 2, P), ALU.mult))
                                    dve.tensor_tensor(st, st, add, ALU.add).then_inc(S("c_state_new"), 1)
                        else:
                            forget(i + 1)
                            dve.wait_ge(S("c_out"), i + 1)
                            if i == 0:
                                dve.wait_ge(S("ret_stored"), 32)
                            for h in range(4):
                                add = ps[4][:, h * P:h * P + P]
                                if i == 0:
                                    ins = dve.tensor_copy(Sp[:, h, :], add)
                                else:
                                    ins = dve.scalar_tensor_tensor(Sp[:, h, :], Sp[:, h, :], dec[:, 0, h:h + 1], add, ALU.mult, ALU.add)
                            if i == 3:
                                ins.then_inc(S("c_prompt_state"), 1)
                            else:
                                L(dve, ins)
                        o = hv(ps[3], m)
                        y, w = hv(t2, m), hv(t1, m)
                        for h in range(4):
                            ins = dve.scalar_tensor_tensor(y[:, h], hv(v(i), m)[:, h], sm[0:m, 2, h:h + 1], o[:, h], ALU.mult, ALU.add)
                        L(dve, ins)
                        dve.wait_ge(S("c_turned"), i + 1)
                        L(dve, dve.tensor_tensor(w, y, y, ALU.mult))
                        dve.tensor_reduce(sm[0:m, 1, :], w, AX, ALU.add).then_inc(S("c_sq"), 1)
                        if not last:
                            log_forget(i + 1)
                        share.point("dve", dve)
                        dve.wait_ge(S("c_rstd"), i + 1)
                        L(dve, dve.tensor_tensor(y, y, bc(sm[0:m, 1, :], 2, P), ALU.mult))
                        L(dve, dve.tensor_tensor(y, y, bc(ghg[0:m], 1, 4), ALU.mult))
                        dve.tensor_tensor(t2[0:m, :], t2[0:m, :], g(i)[0:m, :], ALU.mult).then_inc(S("c_y"), 1)
                        share.point("dve", dve)
                        share.point("dve", dve)
                    share.end("dve", dve)

                @block.sync
                def _(sp):
                    for w in range(4):
                        sp.wait_ge(S(f"spilled{w}"), 16 * 10)
                    for i, (t0, m) in enumerate(tiles):
                        if i >= 2:
                            sp.wait_ge(S("c_y"), i - 1)
                        sp.dma_start(inputs[0:m, i % 2], spill[4:8, t0:t0 + m, :].rearrange("j t n -> t j n")).then_inc(S(f"c_tile_in{i % 2}"), 16)
                        if i == 1:
                            sp.wait_ge(S("ret_stored"), 32)
                            for b in range(0, NB, 2):
                                sp.dma_start(S0[:, b:b + 2].rearrange("p b h e -> p (b h) e"),
                                             inp["state_hgrn"][lay, b:b + 2].rearrange("o b h d e -> d (o b h) e")).then_inc(S("c_state_in"), 16)
                        if i >= 2:
                            stream(sp, min(job0 + i - 1, job0 + 2), l)
                    sp.wait_ge(S("c_prompt_state"), 1)
                    sp.dma_start(out["hgrn_prompt"][lay].rearrange("o b h d e -> d (o b h) e"), Sp).then_inc(S("hgrn_stored"), 16)
                    stream(sp, job0 + 4, l)
                    sp.wait_ge(S("c_state_new"), 8)
                    sp.dma_start(out["hgrn_sample"][lay].rearrange("o b h d e -> d (o b h) e"), S0.rearrange("p b h e -> p (b h) e")).then_inc(S("hgrn_stored"), 16)

        def stage_ssm(l):
            lay = bass.ds(l, 1)
            ar = Arena(arena, 0, ANB)
            dt, a = ar.take(5, 8), ar.take(5, 8)
            xc = ar.take(8, T)
            keep = ar.at
            raw = Arena(brT_, 0, 8 * T).take(8, SEQ + 3)
            raws = ar.take(8, NB, 7)
            xs_in = ar.take(8, NS)
            cst_in = ar.take(DM)
            cv = Arena(brT_, 12 * T, 16 * T)
            cp, cs = cv.take(DM), cv.take(DM)
            tail = ar.take(8, NB * 3)
            acc, accs = ar.take(2, SEQ), ar.take(2, NS)
            ut, au = ar.take(5, 8), ar.take(5, 8)
            ea = ar.take(8)
            share = Share("gate20", [2] + [1] * 8)
            with nc.Block() as block:
                @block.gpsimd
                def _(pool):
                    pool.memset(raw[:, :, 0:3], 0.0)
                    pool.memset(dt[:, 4, :], 0.0).then_inc(S("d_padded"), 1)

                @block.vector
                def _(dve):
                    L = vch.link
                    dve.wait_ge(S("conv_in_taken"), 1)
                    dve.wait_ge(S("d_in"), 16 * 5)
                    L(dve, dve.tensor_copy(raws[:, :, :, 3:7], xs_in.rearrange("p c (b t) -> p c b t", b=NB)))
                    dve.tensor_copy(tail.rearrange("p c (b j) -> p c b j", b=NB), raws[:, :, :, 4:7]).then_inc(S("tail_ready"), 1)
                    L(dve, dve.tensor_tensor(ut, dt, bc(dtb, 1, 5), ALU.add))
                    L(dve, dve.tensor_scalar(au, ut, -1.0, None, ALU.mult))
                    dve.tensor_tensor(au, au, ut, ALU.max).then_inc(S("dt_abs"), 1)
                    dve.wait_ge(S("dt_log"), 1)
                    L(dve, dve.scalar_tensor_tensor(dt, ut, 0.0, au, ALU.max, ALU.add))
                    dve.scalar_tensor_tensor(a, dt, -1.0, bc(ea, 1, 5), ALU.mult, ALU.mult)
                    for c in range(8):
                        if c >= 2:
                            dve.wait_ge(S("conv_taken"), c - 1)
                        ap_, as_ = acc[:, c % 2, :], accs[:, c % 2, :].rearrange("p (b t) -> p b t", b=NB)
                        dve.tensor_scalar(ap_, raw[:, c, 0:SEQ], cw[:, 0, c:c + 1], cb[:, c:c + 1], ALU.mult, ALU.add)
                        L(dve, dve.tensor_scalar(as_, raws[:, c, :, 0:4], cw[:, 0, c:c + 1], cb[:, c:c + 1], ALU.mult, ALU.add))
                        for j in range(1, 4):
                            dve.scalar_tensor_tensor(ap_, raw[:, c, j:j + SEQ], cw[:, j, c:c + 1], ap_, ALU.mult, ALU.add)
                            ins = dve.scalar_tensor_tensor(as_, raws[:, c, :, j:j + 4], cw[:, j, c:c + 1], as_, ALU.mult, ALU.add)
                            if j < 3:
                                L(dve, ins)
                        ins.then_inc(S("conv_ready"), 1)

                @block.scalar
                def _(act):
                    share.point("act", act)
                    act.wait_ge(S("conv_in_turned"), 1)
                    for c in range(8):
                        ins = act.activation(raws[:, c, :, 0:3], ps[4][:, c * 24:c * 24 + 24].rearrange("p (b j) -> p b j", b=NB), ACT.Copy)
                    ins.then_inc(S("conv_in_taken"), 1)
                    act.wait_ge(S("dt_abs"), 1)
                    act.activation(ea, alog, ACT.Exp)
                    ach.link(act, act.activation(au, au, ACT.Exp, scale=-1.0))
                    act.activation(au, au, ACT.Ln, bias=ones[:, 0:1]).then_inc(S("dt_log"), 1)
                    for c in range(8):
                        act.wait_ge(S("conv_ready"), c + 1)
                        act.activation(xc[:, c, 0:SEQ], acc[:, c % 2, :], ACT.Silu)
                        act.activation(xc[:, c, SEQ:T], accs[:, c % 2, :], ACT.Silu).then_inc(S("conv_taken"), 1)
                        share.point("act", act)
                    share.end("act", act)
                    act.wait_ge(S("conv_state_turned"), 1)
                    for half in range(2):
                        act.activation(cp[0:3, half * 512:half * 512 + 512], ps[half][0:3, :], ACT.Copy)
                        ins = act.activation(cs[0:24, half * 512:half * 512 + 512], ps[2 + half][0:24, :], ACT.Copy)
                    ins.then_inc(S("conv_state_ready"), 1)

                @block.tensor
                def _(pe):
                    share.point("pe", pe)
                    pe.wait_ge(S("conv_in"), 16)
                    for c in range(8):
                        mm = pe.transpose(ps[4][:, c * 24:c * 24 + 24], cst_in[0:24, c * P:c * P + P], ident[0:24, 0:24])
                    mm.then_inc(S("conv_in_turned"), 1)
                    for c in range(8):
                        share.point("pe", pe)
                    share.end("pe", pe)
                    pe.wait_ge(S("tail_ready"), 1)
                    pe.wait_ge(S("d_in"), 16 * 5)
                    for c in range(8):
                        at = c % 4 * P
                        pe.transpose(ps[c // 4][0:3, at:at + P], raw[:, c, SEQ:SEQ + 3], ident)
                        mm = pe.transpose(ps[2 + c // 4][0:24, at:at + P], tail[:, c, :], ident)
                    mm.then_inc(S("conv_state_turned"), 1)

                @block.sync
                def _(sp):
                    for w in range(4):
                        sp.wait_ge(S(f"spilled{w}"), 16 * (17 if w < 2 else 16))
                    sp.wait_ge(S("d_padded"), 1)
                    sp.dma_start(dt[:, 0:4, :], spill_dt[0:SEQ].rearrange("(t p) h -> p t h", p=P)).then_inc(S("d_in"), 16)
                    sp.dma_start(dt[0:NS, 4, :], spill_dt[SEQ:T]).then_inc(S("d_in"), 16)
                    for half in range(2):
                        sp.dma_start(raw[:, half * 4:half * 4 + 4, 3:SEQ + 3],
                                     spill_x[half * 512:half * 512 + 512, 0:SEQ].rearrange("(c p) t -> p c t", p=P)).then_inc(S("d_in"), 16)
                    sp.wait_ge(S("hgrn_stored"), 32)
                    sp.dma_start(cst_in[0:24, :], inp["state_conv"][lay].rearrange("o b j n -> (o b j) n")).then_inc(S("conv_in"), 16)
                    sp.dma_start(xs_in, spill_x[:, SEQ:T].rearrange("(c p) t -> p c t", p=P)).then_inc(S("d_in"), 16)
                    stream(sp, J["gate21"] + 1, l)
                    sp.wait_ge(S("conv_state_ready"), 1)
                    sp.dma_start(out["conv_prompt"][lay].rearrange("o b j n -> (o b j) n"), cp[0:3, :]).then_inc(S("conv_stored"), 16)
                    sp.dma_start(out["conv_sample"][lay].rearrange("o b j n -> (o b j) n"), cs[0:24, :]).then_inc(S("conv_stored"), 16)
            ar = Arena(arena, keep, ANB)
            z = ar.take(2, 512)
            h0 = Arena(brT_, 0, 8 * T).take(NB, 4, P)
            AW, W = ar.take(8 * P), ar.take(8 * P)
            xn, xw, hp, y = ar.take(512), ar.take(512), ar.take(512), ar.take(512)
            t_x = AW[:, 512:1024]
            Bn = ar.take(256)
            ec = ar.take(3, 8)
            wt = ar.take(8)
            ss = ar.take(2)
            dec = ar.take(4, NB)
            t = AW[:, 0:512]
            hs = (W[:, 0:512], AW[:, 0:512])
            CM = W[:, 512:1024].rearrange("p (g b t) -> p g b t", g=2, b=NB)
            Bx = AW.rearrange("p (b s) -> p b s", b=NB)
            def load_state(sp):
                for b in range(0, NB, 2):
                    sp.dma_start(h0[:, b:b + 2].rearrange("p b q s -> p (b q) s"),
                                 inp["state_ssm"][lay, b:b + 2].rearrange("o b (q x) p s -> (x p) (o b q) s", x=2)).then_inc(S("ssm_in"), 16)

            share = Share("wb21", [2] + [1] * 25)
            job0 = J["gate21"]
            with nc.Block() as block:
                @block.sync
                def _(sp):
                    for i, (t0, m) in enumerate(tiles):
                        if i >= 2:
                            sp.wait_ge(S("d_y"), i - 1)
                        sp.dma_start(z[0:m, i % 2, :], spill[8, t0:t0 + m, :]).then_inc(S(f"z_in{i % 2}"), 16)
                        if i == 1:
                            load_state(sp)
                        if i >= 2:
                            stream(sp, min(job0 + i - 1, job0 + 2), l)
                    stream(sp, job0 + 4, l)
                    sp.wait_ge(S("ssm_new"), 8)
                    sp.dma_start(out["ssm_sample"][lay].rearrange("o b (q x) p s -> (x p) (o b q) s", x=2), h0.rearrange("p b q s -> p (b q) s")).then_inc(S("ssm_stored"), 16)
                    sp.wait_ge(S("ssm_prompt_ready"), 1)
                    sp.dma_start(out["ssm_prompt"][lay].rearrange("o b (q x) p s -> (x p) (o b q) s", x=2), hp.rearrange("p (q s) -> p q s", q=4)).then_inc(S("ssm_stored"), 16)

                @block.tensor
                def _(pe):
                    share.point("pe", pe)
                    for i, (t0, m) in enumerate(tiles):
                        last = i == 4
                        triu, aft = (K("tri_s")[0:NS], K("after_s")[0:NS]) if last else (tri, after)
                        if i >= 1:
                            pe.wait_ge(S("d_y_taken"), i)
                        if last:
                            pe.wait_ge(S("ssm_prompt_ready"), 1)
                        for c in range(4):
                            pe.transpose(ps[0][0:m, c * P:c * P + P], xc[:, c, t0:t0 + m], ident)
                        for c in range(2):
                            pe.transpose(ps[1][0:m, c * P:c * P + P], xc[:, 4 + c, t0:t0 + m], ident)
                        for c in range(2):
                            pe.matmul(ps[2][0:m, c * m:c * m + m], xc[:, 4 + c, t0:t0 + m], xc[:, 6 + c, t0:t0 + m])
                        pe.matmul(ps[2][0:m, 256:264], triu, a[0:m, i, :])
                        mm = pe.matmul(ps[2][0:m, 264:272], aft, a[0:m, i, :])
                        if not last:
                            mm = pe.matmul(ps[2][:, 272:280], ones, a[:, i, :])
                        mm.then_inc(S("d_turned"), 1)
                        share.point("pe", pe)
                        pe.wait_ge(S("d_segs"), i + 1)
                        for h in range(8):
                            mm = pe.matmul(ps[3 + h // 4][0:m, h % 4 * m:h % 4 * m + m], AW[0:m, h * m:h * m + m], triu)
                        mm.then_inc(S("d_seg_sums"), 1)
                        share.point("pe", pe)
                        share.point("pe", pe)
                        pe.wait_ge(S("d_weights"), i + 1)
                        for h in range(8):
                            mm = pe.matmul(ps[5][0:m, h * 64:h * 64 + 64], W[0:m, h * m:h * m + m], t_x[0:m, h * 64:h * 64 + 64])
                        if not last:
                            for gg in range(2):
                                if i > 0:
                                    pe.matmul(ps[3][0:m, gg * 256:gg * 256 + 256], xc[:, 6 + gg, t0:t0 + m], hp[:, gg * 256:gg * 256 + 256])
                                mm = pe.matmul(ps[4][:, gg * 256:gg * 256 + 256], Bn[0:m, gg * P:gg * P + P], xw[0:m, gg * 256:gg * 256 + 256])
                            mm.then_inc(S("d_out"), 1)
                        else:
                            mm.then_inc(S("d_out"), 1)
                            pe.wait_ge(S("ssm_in"), 64)

                            def turn_state(b):
                                if b >= 2:
                                    pe.wait_ge(S("hs_taken"), b - 1)
                                for qq in range(4):
                                    mm = pe.transpose(ps[1 + b % 2 * 3][:, qq * P:qq * P + P], h0[:, b, qq, :], ident)
                                mm.then_inc(S("hs_turned"), 1)
                            turn_state(0)
                            pe.wait_ge(S("c_masked"), 1)
                            for b in range(NB):
                                if b < NB - 1:
                                    turn_state(b + 1)
                                pe.wait_ge(S("hs_taken"), b + 1)
                                for gg in range(2):
                                    mm = pe.matmul(ps[3][0:NS, gg * 256:gg * 256 + 256], CM[:, gg, b, :], hs[b % 2][:, gg * 256:gg * 256 + 256],
                                                   start=(b == 0 and gg == 0), stop=(b == NB - 1 and gg == 1), skip_group_check=True)
                                mm.then_inc(S("hs_used"), 1)
                            pe.wait_ge(S("a_spread"), 1)
                            for qq in range(4):
                                mm = pe.matmul(ps[1][:, qq * NB:qq * NB + NB], y[0:NS, qq * P:qq * P + P], K("seqhot")[0:NS])
                            mm.then_inc(S("ssm_decay_sums"), 1)
                            for n in range(8):
                                qq, half = n // 2, n % 2
                                pe.wait_ge(S("b_masked"), qq // 2 + 1)
                                if n >= 2:
                                    pe.wait_ge(S("ssm_new"), n - 1)
                                pe.matmul(ps[(4, 2)[n % 2]][:, :], xw[0:NS, qq * P:qq * P + P],
                                          Bx[0:NS, half * 4:half * 4 + 4, :].rearrange("p b s -> p (b s)")).then_inc(S("ssm_add"), 1)
                        share.point("pe", pe)
                        pe.wait_ge(S("d_y"), i + 1)
                        for c in range(4):
                            mm = pe.transpose(ps[0][:, c * m:c * m + m], y[0:m, c * P:c * P + P], ident[0:m, 0:m])
                        mm.then_inc(S("d_y_turned"), 1)
                        share.point("pe", pe)
                        if i == 3:
                            for qq in range(4):
                                mm = pe.transpose(ps[1][:, qq * P:qq * P + P], hp[:, qq * P:qq * P + P], ident)
                            mm.then_inc(S("hp_turned"), 1)
                    share.end("pe", pe)

                @block.scalar
                def _(act):
                    share.point("act", act)
                    for i, (t0, m) in enumerate(tiles):
                        last = i == 4
                        act.wait_ge(S(f"z_in{i % 2}"), 16 * (i // 2 + 1))
                        act.activation(z[0:m, i % 2, :], z[0:m, i % 2, :], ACT.Silu).then_inc(S("z_gate"), 1)
                        act.wait_ge(S("d_turned"), i + 1)
                        act.activation(xn[0:m, :], ps[0][0:m, :], ACT.Copy)
                        act.activation(Bn[0:m, :], ps[1][0:m, 0:256], ACT.Copy)
                        k = 2 if last else 3
                        act.activation(ec[0:m, 0:k, :], ps[2][0:m, 256:256 + 8 * k].rearrange("p (k h) -> p k h", k=k), ACT.Exp).then_inc(S("d_taken"), 1)
                        share.point("act", act)
                        act.wait_ge(S("d_seg_sums"), i + 1)
                        for half in range(2):
                            ins = act.activation(W[0:m, half * 4 * m:half * 4 * m + 4 * m], ps[3 + half][0:m, 0:4 * m], ACT.Exp)
                        ins.then_inc(S("d_seg_exp"), 1)
                        share.point("act", act)
                        share.point("act", act)
                        if last:
                            act.wait_ge(S("d_out"), 5)
                            for b in range(NB):
                                act.wait_ge(S("hs_turned"), b + 1)
                                if b >= 2:
                                    act.wait_ge(S("hs_used"), b - 1)
                                act.activation(hs[b % 2][:, :], ps[1 + b % 2 * 3][:, :], ACT.Copy).then_inc(S("hs_taken"), 1)
                            act.wait_ge(S("ssm_decay_sums"), 1)
                            act.activation(dec.rearrange("p q b -> p (q b)"), ps[1][:, 0:32], ACT.Exp).then_inc(S("ssm_decays"), 1)
                        share.point("act", act)
                        act.wait_ge(S("d_sq"), i + 1)
                        ach.link(act, act.activation(ss[0:m, :], ss[0:m, :], ACT.Ln, bias=eps[0:m], scale=1.0 / 256))
                        act.activation(ss[0:m, :], ss[0:m, :], ACT.Exp, scale=-0.5).then_inc(S("d_rstd"), 1)
                        act.wait_ge(S("d_y_turned"), i + 1)
                        if i == 0:
                            act.wait_ge(S("conv_stored"), 32)
                        act.activation(brT[:, 12:16, t0:t0 + m], ps[0][:, 0:4 * m].rearrange("p (c t) -> p c t", c=4), ACT.Copy).then_inc(S("d_y_taken"), 1)
                        share.point("act", act)
                        if i == 3:
                            act.wait_ge(S("hp_turned"), 1)
                            act.activation(hp[:, :], ps[1][:, :], ACT.Copy).then_inc(S("ssm_prompt_ready"), 1)
                    share.end("act", act)

                @block.vector
                def _(dve):
                    L = vch.link

                    def v3(x, m, k):
                        return x[0:m].rearrange("p (k d) -> p k d", k=k)
                    share.point("dve", dve)
                    for i, (t0, m) in enumerate(tiles):
                        last = i == 4
                        triu, aft = (K("tri_s")[0:NS], K("after_s")[0:NS]) if last else (tri, after)
                        dve.tensor_tensor(AW[0:m, 0:8 * m].rearrange("p (h n) -> p h n", h=8), bc(aft, 1, 8), bc(a[0:m, i, :], 2, m), ALU.mult).then_inc(S("d_segs"), 1)
                        dve.wait_ge(S("d_taken"), i + 1)
                        cbm = ps[2][0:m, 0:2 * m].rearrange("p (g n) -> p g n", g=2)
                        L(dve, dve.tensor_tensor(v3(y, m, 1)[:, 0, 0:2 * m].rearrange("p (g n) -> p g n", g=2), cbm, bc(triu, 1, 2), ALU.mult))
                        L(dve, dve.tensor_tensor(wt[0:m, :], ec[0:m, 1, :], dt[0:m, i, :], ALU.mult))
                        L(dve, dve.tensor_tensor(v3(xw, m, 8), v3(xn, m, 8), bc(wt[0:m, :], 2, 64), ALU.mult))
                        share.point("dve", dve)
                        dve.wait_ge(S("d_seg_exp"), i + 1)
                        L(dve, dve.tensor_tensor(v3(t_x, m, 8), v3(xn, m, 8), bc(dt[0:m, i, :], 2, 64), ALU.mult))
                        dve.tensor_tensor(W[0:m, 0:8 * m].rearrange("p (g h n) -> p g h n", g=2, h=4), W[0:m, 0:8 * m].rearrange("p (g h n) -> p g h n", g=2, h=4),
                                          bc(y[0:m, 0:2 * m].rearrange("p (g n) -> p g n", g=2), 2, 4), ALU.mult).then_inc(S("d_weights"), 1)
                        share.point("dve", dve)
                        share.point("dve", dve)
                        dve.wait_ge(S("d_out"), i + 1)
                        if last:
                            msk = K("qmask").rearrange("p (b t) -> p b t", b=NB)
                            dve.tensor_copy(v3(y, NS, 8), bc(a[0:NS, 4, :], 2, 64)).then_inc(S("a_spread"), 1)
                            for gg in range(2):
                                ins = dve.tensor_tensor(CM[:, gg], bc(xc[:, 6 + gg, SEQ:T], 1, NB), msk, ALU.mult)
                            ins.then_inc(S("c_masked"), 1)
                            dve.wait_ge(S("ssm_decays"), 1)
                            dve.wait_ge(S("hs_used"), 8)
                            for n in range(8):
                                qq, half = n // 2, n % 2
                                if n % 4 == 0:
                                    if n:
                                        dve.wait_ge(S("ssm_add"), 4)
                                    dve.tensor_tensor(Bx[0:NS], bc(Bn[0:NS, qq // 2 * P:qq // 2 * P + P], 1, NB), bc(K("seqhot")[0:NS], 2, P), ALU.mult).then_inc(S("b_masked"), 1)
                                dve.wait_ge(S("ssm_add"), n + 1)
                                st = h0[:, half * 4:half * 4 + 4, qq, :]
                                L(dve, dve.tensor_tensor(st, st, bc(dec[:, qq, half * 4:half * 4 + 4], 2, P), ALU.mult))
                                dve.tensor_tensor(st, st, ps[(4, 2)[n % 2]][:, :].rearrange("p (b s) -> p b s", b=4), ALU.add).then_inc(S("ssm_new"), 1)
                            dve.wait_ge(S("ssm_new"), 8)
                        else:
                            if i == 0:
                                L(dve, dve.tensor_copy(hp[:, :], ps[4][:, :]))
                            else:
                                L(dve, dve.tensor_tensor(v3(hp, P, 8), v3(hp, P, 8), bc(ec[:, 2, :], 2, 64), ALU.mult))
                                L(dve, dve.tensor_tensor(hp[:, :], hp[:, :], ps[4][:, :], ALU.add))
                        dve.wait_ge(S("z_gate"), i + 1)
                        L(dve, dve.tensor_tensor(v3(t, m, 8), v3(xn, m, 8), bc(dskip[0:m, :], 2, 64), ALU.mult))
                        L(dve, dve.tensor_tensor(t[0:m, :], t[0:m, :], ps[5][0:m, :], ALU.add))
                        if i > 0:
                            L(dve, dve.tensor_tensor(v3(y, m, 8), ps[3][0:m, :].rearrange("p (k d) -> p k d", k=8), bc(ec[0:m, 0, :], 2, 64), ALU.mult))
                            L(dve, dve.tensor_tensor(t[0:m, :], t[0:m, :], y[0:m, :], ALU.add))
                        L(dve, dve.tensor_tensor(y[0:m, :], t[0:m, :], z[0:m, i % 2, :], ALU.mult))
                        L(dve, dve.tensor_tensor(t[0:m, :], y[0:m, :], y[0:m, :], ALU.mult))
                        dve.tensor_reduce(ss[0:m, :], v3(t, m, 2), AX, ALU.add).then_inc(S("d_sq"), 1)
                        share.point("dve", dve)
                        dve.wait_ge(S("d_rstd"), i + 1)
                        L(dve, dve.tensor_tensor(v3(y, m, 2), v3(y, m, 2), bc(ss[0:m, :], 2, 256), ALU.mult))
                        dve.tensor_tensor(y[0:m, :], y[0:m, :], gssm[0:m, :], ALU.mult).then_inc(S("d_y"), 1)
                        dve.wait_ge(S("d_y_turned"), i + 1)
                        share.point("dve", dve)
                    share.end("dve", dve)

        def stage_merge(l):
            with nc.Block() as block:
                @block.sync
                def _(sp):
                    stream(sp, J["wo1"] + 3, l)
                    sp.wait_ge(S("ssm_stored"), 32)

                @block.tensor
                def _(pe):
                    finish_to("pe", pe, "wo1")

                @block.scalar
                def _(act):
                    finish_to("act", act, "wo1")

                @block.vector
                def _(dve):
                    finish_to("dve", dve, "wo1")

        def stage_ff(l):
            ar = Arena(arena, 0, AN - 4 * T)
            ff = ar.take(FC, T)
            ff_ref[0] = ff
            with nc.Block() as block:
                @block.sync
                def _(sp):
                    stream(sp, len(jobs), l)

                @block.tensor
                def _(pe):
                    finish_to("pe", pe, "gu10")
                    sem, n = taken_by(len(table) - 1)
                    pe.wait_ge(S(sem), n)
                    for db in range(2):
                        for r in range(3):
                            j = J[f"dn{db}{r}"]
                            arrived(pe, j)
                            for c in range(min(8, FC - 8 * r)):
                                fc = 8 * r + c
                                for dc in range(4):
                                    w = slot3(j)[:, c, dc * P:dc * P + P]
                                    if db and fc == 0:
                                        pe.wait_ge(S("down_taken"), dc + 1)
                                    for half in range(2):
                                        mm = pe.matmul(ps[2 * dc + half][:, 0:HALF], w, ff[:, fc, half * HALF:half * HALF + HALF],
                                                       start=(fc == 0), stop=(fc == FC - 1))
                            mm.then_inc(S("down_job_done"), 1)

                @block.scalar
                def _(act):
                    finish_to("act", act, "gu10")

                @block.vector
                def _(dve):
                    finish_to("dve", dve, "gu10")
                    for db in range(2):
                        dve.wait_ge(S("down_job_done"), 3 * (db + 1))
                        for dc in range(4):
                            for half in range(2):
                                x = xT[:, db * 4 + dc, half * HALF:half * HALF + HALF]
                                ins = dve.tensor_tensor(x, x, ps[2 * dc + half][:, 0:HALF], ALU.add)
                            ins.then_inc(S("down_taken"), 1)

        with nc.Fori(0, DEPTH) as l:
            part(rms_stage, g1, 2, l, True)
            part(stage_a, l)
            part(stage_linear, l, "r")
            part(stage_hgrn, l)
            part(stage_ssm, l)
            part(stage_merge, l)
            part(rms_stage, g2, 0, l, False)
            part(stage_ff, l)
            with nc.Block() as block:
                @block.sync
                def _(sp):
                    for name in LAYER_SEMS:
                        sp.sem_clear(S(name))

        def epilogue():
            ar = Arena(arena, 0, AN)
            yn = ar.take(5, DM)
            with nc.Block() as block:
                @block.tensor
                def _(pe):
                    for u in range(10):
                        i, half = u // 2, u % 2
                        t0, m = tiles[i]
                        if u >= 2:
                            pe.wait_ge(S("end_taken"), u - 1)
                        for c in range(4):
                            mm = pe.transpose(ps[u % 2][0:m, c * P:c * P + P], xT[:, half * 4 + c, t0:t0 + m], ident)
                        mm.then_inc(S("end_turned"), 1)

                @block.scalar
                def _(act):
                    for u in range(10):
                        i, half = u // 2, u % 2
                        m = tiles[i][1]
                        act.wait_ge(S("end_turned"), u + 1)
                        act.activation(yn[0:m, i, half * 512:half * 512 + 512], ps[u % 2][0:m, :], ACT.Copy).then_inc(S("end_taken"), 1)

                @block.sync
                def _(sp):
                    sp.wait_ge(S("end_taken"), 10)
                    sp.dma_start(out["y_prompt"].rearrange("o (t p) d -> p (o t) d", p=P), yn[:, 0:4, :]).then_inc(S("end_stored"), 16)
                    sp.dma_start(out["y_sample"].rearrange("b t d -> (b t) d"), yn[0:NS, 4, :]).then_inc(S("end_stored"), 16)
                    sp.wait_ge(S("end_stored"), 32)

        part(epilogue)


OUTS = [("y_prompt", (1, SEQ, DM)), ("y_sample", (NB, TS, DM)),
        ("k_prompt", (DEPTH, 1, SEQ, 4, 64)), ("v_prompt", (DEPTH, 1, SEQ, 4, 64)), ("kidx_prompt", (DEPTH, 1, SEQ, 64)),
        ("ret_prompt", (DEPTH, 1, 4, P, P)), ("hgrn_prompt", (DEPTH, 1, 4, P, P)), ("ssm_prompt", (DEPTH, 1, 8, 64, P)),
        ("conv_prompt", (DEPTH, 1, 3, DM)),
        ("k_sample", (DEPTH, NB, TS, 4, 64)), ("v_sample", (DEPTH, NB, TS, 4, 64)), ("kidx_sample", (DEPTH, NB, TS, 64)),
        ("ret_sample", (DEPTH, NB, 4, P, P)), ("hgrn_sample", (DEPTH, NB, 4, P, P)), ("ssm_sample", (DEPTH, NB, 8, 64, P)),
        ("conv_sample", (DEPTH, NB, 3, DM))]


def build(nc, arrays):
    inp = {n: nc.dram_tensor(f"in_{n}", a.shape, mybir.dt.from_np(a.dtype), kind="ExternalInput").ap() for n, a in arrays.items()}
    out = {n: nc.dram_tensor(f"out_{n}", s, F32, kind="ExternalOutput").ap() for n, s in OUTS}
    trunk(nc, inp, out)


def kernel(**inputs):
    import concourse.bacc as bacc
    from concourse.bass_utils import run_bass_kernel_spmd

    arrays = {n: np.ascontiguousarray(a) for n, a in inputs.items()}
    arrays["consts"] = constants()
    nc = bacc.Bacc("TRN2", target_bir_lowering=False, num_devices=1)
    build(nc, arrays)
    r = run_bass_kernel_spmd(nc, [{f"in_{n}": a for n, a in arrays.items()}], core_ids=[0])
    return tuple(r.results[0][f"out_{n}"] for n, _ in OUTS)
```

```python
from contextlib import ExitStack

import numpy as np

import concourse.bass as bass
from concourse import mybir

ALU = mybir.AluOpType
ACT = mybir.ActivationFunctionType
F32 = mybir.dt.float32
I32 = mybir.dt.int32
AX = mybir.AxisListType.X

P = 128
DM = 1024
SEQ = 512
DEPTH = 2
NB = 8
TS = 4
NS = NB * TS
NT = SEQ // P
T = SEQ + NS
PAST = 2048
PAGE = 128
NPG = PAST // PAGE
LK = PAST + NS
KC = DM // P
DFF = 2816
FC = DFF // P
EPS = 1e-6
NEG = -1e30
TAKEN = -3.0e38
TOPK_P = min(256, SEQ // 4)
TOPK_S = min(256, (PAST + TS) // 4)

A_Q, A_K, A_V, A_IQ, A_IK, A_IW = 0, 512, 768, 1024, 1536, 1600
R_Q, C_Q, M_Z, M_X, M_DT, GATES = 1608, 3656, 5704, 6216, 7240, 7248
D_IN = 11344

C = {}
_at = 0
for _n, _w in (("ident", 128), ("ones", 128), ("tri", 128), ("after", 128), ("tri_s", 32), ("after_s", 32),
               ("seqhot", 8), ("qmask", 256), ("bb", 16), ("lv_sum", 7 * 128), ("lv_mask", 7 * 128),
               ("lv_side", 7), ("rdec", 4 * 128), ("rq", 4), ("rk", 4), ("rdec_s", 4 * 32), ("rq_s", 4),
               ("rk_s", 4), ("cos", 5 * 64), ("sin", 5 * 64), ("neg", 128), ("neg_s", 32), ("eps", 1),
               ("rep", 2 * 128), ("wsel", 2 * NS), ("hsel", 8)):
    C[_n] = (_at, _w)
    _at += _w
NCONST = _at
AN = 17840


def constants():
    c = np.zeros((P, NCONST), np.float64)

    def put(name, a):
        a = np.asarray(a, np.float64)
        a = a.reshape(a.shape[0], -1)
        c[:a.shape[0], C[name][0]:C[name][0] + a.shape[1]] = a

    i = np.arange(P)
    k, n = i[:, None], i[None, :]
    put("ident", np.eye(P))
    put("ones", np.ones((P, P)))
    put("tri", k <= n)
    put("after", k > n)
    t = np.arange(NS)
    same = (t[:, None] // TS) == (t[None, :] // TS)
    put("tri_s", (t[:, None] <= t[None, :]) & same)
    put("after_s", (t[:, None] > t[None, :]) & same)
    put("seqhot", (t[:, None] // TS) == np.arange(NB)[None])
    put("qmask", np.broadcast_to((np.arange(NB)[:, None] == t[None, :] // TS)[None], (P, NB, NS)))
    put("bb", np.broadcast_to(np.eye(4)[None], (P, 4, 4)))
    sums, masks, sides = [], [], []
    for lv in range(7):
        w = 1 << lv
        block = i // (2 * w)
        right = (i // w) % 2 == 1
        ref = block * 2 * w + w - 1
        s = np.where(right[None, :], (k > ref[None, :]) & (k <= n), (k > n) & (k <= ref[None, :]))
        sums.append(s)
        masks.append((block[:, None] == block[None, :]) & ~right[:, None] & right[None, :])
        sides.append(right)
    put("lv_sum", np.stack(sums, 1))
    put("lv_mask", np.stack(masks, 1))
    put("lv_side", np.stack(sides, 1))
    lg = np.log1p(-np.exp2(-5.0 - np.arange(4)))
    sc = 128 ** -0.5
    put("rdec", np.stack([np.where(k <= n, np.exp(-g * (k + 1.0)) * sc, 0.0) for g in lg], 1))
    put("rq", np.exp(lg[None] * (i[:, None] + 1.0)))
    put("rk", np.exp(lg[None] * (127.0 - i[:, None])) * sc)
    ts = t % TS
    put("rdec_s", np.stack([np.where((t[:, None] <= t[None, :]) & same, np.exp(-g * (ts[:, None] + 1.0)) * sc, 0.0)
                            for g in lg], 1))
    put("rq_s", np.exp(lg[None] * (ts[:, None] + 1.0)))
    put("rk_s", np.exp(lg[None] * (TS - 1.0 - ts[:, None])) * sc)
    freq = (np.float32(10000.0) ** (-np.arange(64, dtype=np.float32) / np.float32(64))).astype(np.float32)
    pos = np.zeros((P, 5), np.float32)
    for tt in range(4):
        pos[:, tt] = tt * P + i
    pos[:NS, 4] = PAST + ts
    ang = (pos[:, :, None] * freq[None, None]).astype(np.float32).astype(np.float64)
    put("cos", np.cos(ang))
    put("sin", np.sin(ang))
    put("neg", np.where(n <= k, 0.0, NEG))
    put("neg_s", np.where((t[None, :] <= t[:, None]) & same, 0.0, NEG))
    put("eps", np.full((P, 1), EPS))
    rep = np.zeros((NS, 2, 4, 8, TS))
    for b in range(NB):
        for tq in range(TS):
            rep[b * TS + tq, b // 4, b % 4, :, tq] = 1
    put("rep", rep)
    r = np.arange(P)
    wsel = np.zeros((P, 2, NB, TS))
    for g in range(2):
        wsel[r, g, 4 * g + r // 32, r % TS] = 1
    put("wsel", wsel)
    put("hsel", (r[:, None] // TS) % 8 == np.arange(8)[None])
    return c.astype(np.float32)


HALF = T // 2
LAYER_SEMS = ("proj_ready", "taken_act", "taken_dve", "weights_in0", "weights_in1", "down_job_done", "dve_step", "act_step",
              "merged", "spilled0", "spilled1", "spilled2", "spilled3", "h_ready", "next_tile_in", "ret_stored", "hgrn_stored", "ssm_stored")


def trunk(nc, inp, out):
    es = ExitStack()
    with es:
        sems, stage_sems, stage_stack = {}, {}, [None]

        def S(name):
            if name in LAYER_SEMS:
                if name not in sems:
                    sems[name] = es.enter_context(nc.semaphore(name))
                return sems[name]
            if name not in stage_sems:
                stage_sems[name] = stage_stack[0].enter_context(nc.semaphore(name))
            return stage_sems[name]

        def part(run, *args):
            with ExitStack() as stack:
                stage_stack[0] = stack
                run(*args)
                with nc.Block() as block:
                    @block.sync
                    def _(sp):
                        for sem in stage_sems.values():
                            sp.sem_clear(sem)
                stage_sems.clear()

        def sb(name, n):
            return es.enter_context(nc.sbuf_tensor(name, [P, n], F32))

        def bc(ap, axis, n):
            u = ap.unsqueeze(axis)
            shape = list(u.shape)
            shape[axis] = n
            return u.broadcast_to(shape)

        xT_ = sb("xT", KC * T)
        hT_ = sb("hT", KC * T)
        brT_ = sb("branchT", 16 * T)
        ring_ = sb("ring", 2 * KC * 512)
        cst = sb("cst", NCONST)
        lbt = sb("lb_both", 2 * 512)
        par = sb("layer_params", 2112)
        ptab = es.enter_context(nc.sbuf_tensor("ptab", [1, NB * NPG], I32))
        stage = sb("stage", 4 * 512)
        arena = sb("arena", AN)
        spill = nc.dram_tensor("spill", [9, T, 512], F32).ap()
        spill_x = nc.dram_tensor("spill_x", [DM, T], F32).ap()
        spill_dt = nc.dram_tensor("spill_dt", [T, 8], F32).ap()
        ps = [es.enter_context(nc.psum_tensor(f"ps{i}", [P, 512], F32)) for i in range(8)]
        xT = xT_[:, :].rearrange("p (c t) -> p c t", c=KC)
        hT = hT_[:, :].rearrange("p (c t) -> p c t", c=KC)
        brT = brT_[:, :].rearrange("p (c t) -> p c t", c=16)
        slot = [ring_[:, i * 4096:(i + 1) * 4096] for i in range(2)]

        def K(name):
            return cst[:, C[name][0]:C[name][0] + C[name][1]]

        ident, ones, tri, after = K("ident"), K("ones"), K("tri"), K("after")
        eps = K("eps")

        sg = arena[:, AN - 4 * T:AN].rearrange("p (c t) -> p c t", c=4)
        merge_tmp = arena[:, AN - 5 * T:AN - 4 * T].rearrange("p (i t) -> p i t", i=2)
        mg = arena[:, AN - 13 * T:AN - 5 * T].rearrange("p (c t) -> p c t", c=8)
        ANB = AN - 13 * T

        class Arena:
            def __init__(self, t, at=0, end=None):
                self.t, self.at, self.end = t, at, end

            def take(self, *dims):
                n = int(np.prod(dims))
                a = self.t[:, self.at:self.at + n]
                self.at += n
                assert self.end is None or self.at <= self.end, self.at
                if len(dims) == 1:
                    return a
                names = "abcd"[:len(dims)]
                return a.rearrange(f"p ({' '.join(names)}) -> p {' '.join(names)}",
                                   **{x: d for x, d in zip(names, dims)})

        pa = Arena(par, 0, 2112)
        g1, g2 = pa.take(KC), pa.take(KC)
        gq, gk = pa.take(64), pa.take(64)
        ghg, dtb, alog, dskip = pa.take(128), pa.take(8), pa.take(8), pa.take(8)
        gssm = pa.take(512)
        cw, cb = pa.take(4, 8), pa.take(8)
        lb, oml = pa.take(512), pa.take(512)

        class Chain:
            def __init__(self, name):
                self.sem, self.n = S(name), 0

            def link(self, eng, ins):
                ins.then_inc(self.sem, 1)
                self.n += 1
                eng.wait_ge(self.sem, self.n)

        vch, ach = Chain("dve_step"), Chain("act_step")

        jobs = [("aq", A_Q, 512), ("akv", A_K, 512), ("iq", A_IQ, 512), ("ikiw", A_IK, 72)]
        jobs += [(f"r{i}", R_Q + 512 * i, 512) for i in range(4)]
        jobs += [(f"c{i}", C_Q + 512 * i, 512) for i in range(4)]
        jobs += [("z", M_Z, 512), ("xbc0", M_X, 512), ("xbc1", M_X + 512, 512), ("dt", M_DT, 8)]
        for n in range(4):
            for db in range(2):
                jobs += [(f"gate{n}{db}", GATES + n * DM + db * 512, 512), (f"wb{n}{db}", (n, db), 512)]
        jobs += [(f"wo{db}", db, 512) for db in range(2)]
        jobs += [(f"gu{i}", i, 512) for i in range(11)]
        jobs += [(f"dn{db}{r}", (db, r), 512) for db in range(2) for r in range(3)]
        J = {name: i for i, (name, _, _) in enumerate(jobs)}
        issued = [0]

        def slot3(j):
            return slot[j % 2].rearrange("p (c n) -> p c n", c=KC)

        def stream(sp, upto, l):
            for j in range(issued[0], min(upto, len(jobs))):
                name, at, w = jobs[j]
                if j >= 2:
                    if jobs[j - 2][0][:2] == "dn":
                        sp.wait_ge(S("down_job_done"), j - 2 - J["dn00"] + 1)
                    else:
                        sp.wait_ge(S("proj_ready"), END[jobs[j - 2][0]])
                dst = slot3(j)
                lay = bass.ds(l, 1)
                if name[:2] == "wb":
                    src = inp["w_branch"][lay, at[0]].rearrange("o (c p) n -> p (o c) n", p=P)[:, :, at[1] * 512:at[1] * 512 + 512]
                    sp.dma_start(dst[:, 0:4, :], src).then_inc(S(f"weights_in{j % 2}"), 16)
                elif name[:2] == "wo":
                    src = inp["w_out"][lay].rearrange("o (c p) n -> p (o c) n", p=P)[:, :, at * 512:at * 512 + 512]
                    sp.dma_start(dst, src).then_inc(S(f"weights_in{j % 2}"), 16)
                elif name[:2] == "gu":
                    src = inp["w_gu"][lay].rearrange("o (c p) (u n) -> p u (o c) n", p=P, u=2)
                    for u in range(2):
                        sp.dma_start(dst[:, :, u * 256:u * 256 + 256],
                                     src[:, u, :, at * 256:at * 256 + 256]).then_inc(S(f"weights_in{j % 2}"), 16)
                elif name[:2] == "dn":
                    n = min(8, FC - 8 * at[1])
                    src = inp["w_down"][lay].rearrange("o (c p) n -> p (o c) n", p=P)[:, at[1] * 8:at[1] * 8 + n, at[0] * 512:at[0] * 512 + 512]
                    sp.dma_start(dst[:, 0:n, :], src).then_inc(S(f"weights_in{j % 2}"), 16)
                else:
                    src = inp["w_in"][lay].rearrange("o (c p) n -> p (o c) n", p=P)[:, :, at:at + w]
                    sp.dma_start(dst[:, :, 0:w], src).then_inc(S(f"weights_in{j % 2}"), 16)
            issued[0] = max(issued[0], upto)

        def arrived(pe, j):
            n = sum(32 if jobs[i][0][:2] == "gu" else 16 for i in range(j % 2, j + 1, 2))
            pe.wait_ge(S(f"weights_in{j % 2}"), n)

        tiles = [(tt * P, P) for tt in range(NT)] + [(SEQ, NS)]
        kpe, kact = [0], [0]

        table = []
        END = {}
        for name, _, _ in jobs:
            if name[:2] == "dn":
                continue
            if name[:2] == "gu":
                for col in (0, 256, 128, 384):
                    table += [(name, False, col, half, KC, "dve" if col >= 256 else "act") for half in range(2)]
            elif name[:2] in ("ga", "wb", "wo", "iq", "xb"):
                by = "dve" if name[:2] in ("wb", "wo") else "act"
                table += [(name, False, dc * P, half, 4 if name[:2] == "wb" else KC, by) for dc in range(4) for half in range(2)]
            else:
                table += [(name, True, tt, 0, KC, "act") for tt in range(5)]
            END[name] = len(table)
        starts = [0]
        for row in table:
            starts.append(starts[-1] + row[4])

        def taken_by(k):
            return "taken_" + table[k][5], sum(1 for row in table[:k + 1] if row[5] == table[k][5])

        def product(pe, k, c):
            name, natural, at, half, kn, _ = table[k]
            j = J[name]
            if c == 0:
                if k == 0 or table[k - 1][0] != name:
                    arrived(pe, j)
                    if name == "wo0":
                        pe.wait_ge(S("merged"), 48)
                if k >= 2:
                    sem, n = taken_by(k - 2)
                    pe.wait_ge(S(sem), n)
            if k == 0:
                pe.wait_ge(S("h_ready"), c + 1)
            if name == "gu0" and table[k - 1][0] != name:
                pe.wait_ge(S("h_ready"), KC + c + 1)
            bank = ps[6 + k % 2]
            if natural:
                t0, m = tiles[at]
                w = jobs[j][2]
                mm = pe.matmul(bank[0:m, 0:w], hT[:, c, t0:t0 + m], slot3(j)[:, c, 0:w], start=(c == 0), stop=(c == kn - 1))
            else:
                if name[:2] == "wb":
                    src = brT[:, 4 * jobs[j][1][0] + c, half * HALF:half * HALF + HALF]
                elif name[:2] == "wo":
                    src = mg[:, c, half * HALF:half * HALF + HALF]
                else:
                    src = hT[:, c, half * HALF:half * HALF + HALF]
                mm = pe.matmul(bank[:, 0:HALF], slot3(j)[:, c, at:at + P], src, start=(c == 0), stop=(c == kn - 1))
            if c == kn - 1:
                mm.then_inc(S("proj_ready"), 1)

        keep_at, spills = {}, [0]

        def take_act(act, k):
            name, natural, at, half, _, by = table[k]
            if by != "act":
                return
            act.wait_ge(S("proj_ready"), k + 1)
            bank = ps[6 + k % 2]
            t = slice(half * HALF, half * HALF + HALF)
            if natural:
                t0, m = tiles[at]
            if name == "aq":
                ins = act.activation(keep_at["qn"][0:m, at, :], bank[0:m, :], ACT.Copy)
            elif name == "akv":
                act.activation(keep_at["kn"][0:m, at, :], bank[0:m, 0:256], ACT.Copy)
                ins = act.activation(keep_at["vn"][0:m, at, :], bank[0:m, 256:512], ACT.Copy)
            elif name == "iq":
                ins = act.activation(keep_at["iqT"][:, at // P, t], bank[:, 0:HALF], ACT.Copy)
            elif name == "ikiw":
                for u in range(2):
                    act.activation(keep_at["ikd"][0:m, at, u, :], bank[0:m, 0:64], ACT.Copy)
                ins = act.activation(keep_at["iwn"][0:m, at, :], bank[0:m, 64:72], ACT.Copy, scale=8 ** -0.5)
            elif name[:4] == "gate":
                ins = act.activation(sg[:, at // P, t], bank[:, 0:HALF], ACT.Copy)
                if at == 3 * P and half == 1:
                    ach.link(act, ins)
                    ins = act.activation(sg[:, :, :], sg[:, :, :], ACT.Sigmoid)
            elif name[:2] == "gu":
                ins = act.activation(sg[:, at // P, t], bank[:, 0:HALF], ACT.Silu)
            else:
                i, n = spills[0] % 4, spills[0] // 4
                if n:
                    act.wait_ge(S(f"spilled{i}"), 16 * n)
                st = stage[:, i * 512:i * 512 + 512]
                if name[:3] == "xbc":
                    c = 4 * int(name[3]) + at // P
                    ins = act.activation(st[:, 0:HALF], bank[:, 0:HALF], ACT.Copy)
                    dst, src = (spill_x[c * P:c * P + P, t], st[:, 0:HALF])
                elif name == "dt":
                    ins = act.activation(st[0:m, 0:8], bank[0:m, 0:8], ACT.Copy)
                    dst, src = (spill_dt[t0:t0 + m, :], st[0:m, 0:8])
                else:
                    row = 8 if name == "z" else int(name[1]) + (4 if name[0] == "c" else 0)
                    ins = act.activation(st[0:m, :], bank[0:m, :], ACT.Copy)
                    dst, src = (spill[row, t0:t0 + m, :], st[0:m, :])
                spills[0] += 1
                ins.then_inc(S("taken_act"), 1)
                act.wait_ge(S("taken_act"), taken_by(k)[1])
                act.dma_start(dst, src).then_inc(S(f"spilled{i}"), 16)
                return
            ins.then_inc(S("taken_act"), 1)

        merges = [0]

        def take_dve(dve, k):
            name, natural, at, half, _, by = table[k]
            if by != "dve":
                return
            dve.wait_ge(S("proj_ready"), k + 1)
            bank = ps[6 + k % 2]
            t = slice(half * HALF, half * HALF + HALF)
            if name[:2] == "wb":
                n, db = jobs[J[name]][1]
                gate = max(i for i in range(k) if table[i][0][:4] == "gate")
                dve.wait_ge(S("taken_act"), taken_by(gate)[1])
                dst = mg[:, db * 4 + at // P, t]
                if n == 0:
                    dve.tensor_tensor(dst, bank[:, 0:HALF], sg[:, at // P, t], ALU.mult).then_inc(S("taken_dve"), 1)
                else:
                    tm = merge_tmp[:, k % 2, :]
                    dve.tensor_tensor(tm, bank[:, 0:HALF], sg[:, at // P, t], ALU.mult).then_inc(S("taken_dve"), 1)
                    dve.wait_ge(S("taken_dve"), taken_by(k)[1])
                    dve.tensor_tensor(dst, dst, tm, ALU.add).then_inc(S("merged"), 1)
                    merges[0] += 1
                    dve.wait_ge(S("merged"), merges[0])
            elif name[:2] == "wo":
                dst = xT[:, jobs[J[name]][1] * 4 + at // P, t]
                dve.tensor_tensor(dst, dst, bank[:, 0:HALF], ALU.add).then_inc(S("taken_dve"), 1)
            else:
                gate = k - 2
                dve.wait_ge(S("taken_act"), taken_by(gate)[1])
                n = 2 * jobs[J[name]][1] + (at - 256) // P
                dve.tensor_tensor(ff_ref[0][:, n, t], bank[:, 0:HALF], sg[:, (at - 256) // P, t], ALU.mult).then_inc(S("taken_dve"), 1)

        done = {"pe": 0, "act": 0, "dve": 0}
        ff_ref = [None]

        def fill_to(who, eng, upto):
            if who == "pe":
                for x in range(done["pe"], upto):
                    k = max(i for i in range(len(table)) if starts[i] <= x)
                    product(eng, k, x - starts[k])
                done["pe"] = max(done["pe"], upto)
                return
            k = max(i for i in range(len(table)) if starts[i] < max(upto, 1))
            take_to(who, eng, k - 1)

        def take_to(who, eng, upto):
            for k in range(done[who], upto):
                if who == "act" and (table[k][0][:4] == "gate" or table[k][0][:2] == "gu") and table[k][5] == "act":
                    last = [i for i in range(k) if table[i][5] == "dve" and
                            (table[k][0][:4] == "gate" or table[i][0][:2] == "wo" or table[i][2] - 256 == table[k][2])]
                    if last:
                        eng.wait_ge(S("taken_dve"), taken_by(last[-1])[1])
                (take_act if who == "act" else take_dve)(eng, k)
            done[who] = max(done[who], upto)

        def finish_to(who, eng, name):
            if who == "pe":
                fill_to("pe", eng, starts[END[name]])
            else:
                take_to(who, eng, END[name])

        class Share:
            def __init__(self, last, weights):
                self.a = {w: starts_at[0] for w in ("pe", "act", "dve")}
                self.a0, self.b = starts_at[0], starts[END[last]]
                self.cum = np.cumsum(weights) / np.sum(weights)
                self.p = {"pe": 0, "act": 0, "dve": 0}
                self.last = last
                starts_at[0] = self.b

            def point(self, who, eng):
                x = self.a0 + int(round((self.b - self.a0) * self.cum[self.p[who]]))
                self.p[who] += 1
                fill_to(who, eng, x)

            def end(self, who, eng):
                assert self.p[who] in (0, len(self.cum)) or who == "dve", (who, self.p[who], len(self.cum))
                finish_to(who, eng, self.last)
        starts_at = [0]

        def prologue():
            ar = Arena(arena, 0, AN)
            xnat = ar.take(5, DM)
            with nc.Block() as block:
                @block.sync
                def _(sp):
                    sp.dma_start(cst[:, :], inp["consts"]).then_inc(S("consts_in"), 16)
                    sp.dma_start(xnat[:, 0:4, :], inp["x_prompt"].rearrange("o (t p) d -> p (o t) d", p=P)).then_inc(S("x_in"), 16)
                    sp.dma_start(xnat[0:NS, 4, :], inp["x_sample"].rearrange("b t d -> (b t) d")).then_inc(S("x_in"), 16)
                    sp.dma_start(ptab[:, :], inp["page_table"].rearrange("(o b) g -> o (b g)", o=1)).then_inc(S("x_in"), 16)
                    sp.dma_start(lbt[:, :], inp["lb_param"].rearrange("(o l) n -> o (l n)", o=1).broadcast_to([P, 2 * 512])).then_inc(S("lb_in"), 16)
                    sp.wait_ge(S("x_in"), 48)

                @block.tensor
                def _(pe):
                    pe.wait_ge(S("consts_in"), 16)
                    pe.wait_ge(S("x_in"), 48)
                    for c in range(KC):
                        if c >= 2:
                            pe.wait_ge(S("x_taken"), c - 1)
                        for tt, (t0, m) in enumerate(tiles):
                            dst = ps[c % 2][:, t0:t0 + m] if m == P else ps[2 + c % 2][:, 0:m]
                            mm = pe.transpose(dst, xnat[0:m, tt, c * P:c * P + P], ident[0:m, 0:m])
                        mm.then_inc(S("x_turned"), 1)

                @block.scalar
                def _(act):
                    for c in range(KC):
                        act.wait_ge(S("x_turned"), c + 1)
                        act.activation(xT[:, c, 0:SEQ], ps[c % 2][:, :], ACT.Copy)
                        act.activation(xT[:, c, SEQ:T], ps[2 + c % 2][:, 0:NS], ACT.Copy).then_inc(S("x_taken"), 1)
                    act.wait_ge(S("lb_shifted"), 1)
                    act.activation(lbt[:, :], lbt[:, :], ACT.Exp).then_inc(S("lb_exp"), 1)

                @block.vector
                def _(dve):
                    tmp = ar.take(512)
                    l0, l1 = lbt[:, 0:512], lbt[:, 512:1024]
                    dve.wait_ge(S("lb_in"), 16)
                    vch.link(dve, dve.tensor_tensor(tmp, l0, l1, ALU.max))
                    vch.link(dve, dve.tensor_tensor(l0, l0, tmp, ALU.subtract))
                    dve.tensor_tensor(l1, l1, tmp, ALU.subtract).then_inc(S("lb_shifted"), 1)
                    dve.wait_ge(S("lb_exp"), 1)
                    vch.link(dve, dve.tensor_tensor(tmp, l0, l1, ALU.add))
                    vch.link(dve, dve.reciprocal(tmp, tmp))
                    vch.link(dve, dve.tensor_tensor(l0, l0, tmp, ALU.mult))
                    vch.link(dve, dve.tensor_tensor(l1, l1, tmp, ALU.mult))
                    vch.link(dve, dve.tensor_tensor(l1, l0, l1, ALU.add))
                    vch.link(dve, dve.tensor_tensor(l1, l1, l0, ALU.subtract))
                    vch.link(dve, dve.tensor_tensor(l0, l0, l0, ALU.subtract))

        part(prologue)
        with nc.Block() as block:
            @block.sync
            def _(sp):
                sp.sem_clear(S("dve_step"))
        vch.n = 0

        rstd = brT_[:, 0:T]

        def rms_dve(dve, gain, with_params, l):
            for c in range(KC):
                dve.tensor_tensor(hT[:, c, :], xT[:, c, :], xT[:, c, :], ALU.mult).then_inc(S("sq_ready"), 1)
            if with_params:
                dve.wait_ge(S("params_in"), 16 * 14)
                vch.link(dve, dve.tensor_copy(lb, lbt[:, bass.ds(l * 512, 512)]))
                vch.link(dve, dve.tensor_scalar(oml, lb, -1.0, 1.0, ALU.mult, ALU.add))
            dve.wait_ge(S("rstd_ready"), 1)
            for c in range(KC):
                dve.scalar_tensor_tensor(hT[:, c, :], xT[:, c, :], gain[:, c:c + 1], rstd, ALU.mult, ALU.mult).then_inc(S("h_ready"), 1)

        def rms_pe(pe):
            for c in range(KC):
                pe.wait_ge(S("sq_ready"), c + 1)
                for half in range(2):
                    mm = pe.matmul(ps[half][:, 0:HALF], ones, hT[:, c, half * HALF:half * HALF + HALF], start=(c == 0), stop=(c == KC - 1))
            mm.then_inc(S("sq_summed"), 1)

        def rms_act(act):
            act.wait_ge(S("sq_summed"), 1)
            act.activation(rstd[:, 0:HALF], ps[0][:, 0:HALF], ACT.Ln, bias=eps, scale=1.0 / DM)
            ach.link(act, act.activation(rstd[:, HALF:T], ps[1][:, 0:HALF], ACT.Ln, bias=eps, scale=1.0 / DM))
            act.activation(rstd, rstd, ACT.Exp, scale=-0.5).then_inc(S("rstd_ready"), 1)

        def load_params(sp, l):
            lay = bass.ds(l, 1)

            def col(name):
                return inp[name][lay].rearrange("o (c p) -> p (o c)", p=P)

            def row(name):
                a = inp[name][lay]
                return a.broadcast_to([P, a.shape[1]])
            with nc.allow_non_contiguous_dma(reason="small columns of parameters"):
                sp.dma_start(g1, col("norm1_g")).then_inc(S("params_in"), 16)
                sp.dma_start(g2, col("norm2_g")).then_inc(S("params_in"), 16)
                sp.dma_start(cb, col("conv_b")).then_inc(S("params_in"), 16)
                for j in range(4):
                    sp.dma_start(cw[:, j, :], inp["conv_w"][lay, j].rearrange("o (c p) -> p (o c)", p=P)).then_inc(S("params_in"), 16)
            for dst, name in ((gq, "q_norm_g"), (gk, "k_norm_g"), (ghg, "hgrn_norm_g"), (dtb, "dt_bias"),
                              (alog, "A_log"), (dskip, "D_skip"), (gssm, "ssm_norm_g")):
                sp.dma_start(dst, row(name)).then_inc(S("params_in"), 16)

        def stage_a(l):
            lay = bass.ds(l, 1)
            ar = Arena(arena, 0, AN)
            vn = ar.take(5, 256)
            kTs = ar.take(2, NS)
            iwn = ar.take(5, 8)
            qT = ar.take(4, T)
            idx_at = ar.at
            ikT = ar.take(T)
            iqT = ar.take(4, T)
            keep = ar.at
            k2T = ar.take(4, T)
            kn = ar.take(5, 256)
            ikd = ar.take(5, 2, 64)
            qn = ar.take(5, 512)
            tmp = Arena(brT_, 4 * T, 16 * T).take(5, 512)
            kdup = ar.take(5, 4, 2, 64)
            ssq, ssk = ar.take(5 * 8), ar.take(5 * 4)
            with nc.Block() as block:
                @block.sync
                def _(sp):
                    stream(sp, 1, l)
                    load_params(sp, l)
                    stream(sp, J["ikiw"] + 3, l)

                @block.vector
                def _(dve):
                    rms_dve(dve, g1, True, l)

                @block.gpsimd
                def _(pool):
                    for a in (qn, kn, vn, iwn):
                        ins = pool.memset(a[:, 4, :], 1.0)
                    ins = pool.memset(ikd[:, 4, :, :], 1.0)
                    ins.then_inc(S("a_padded"), 1)

                @block.tensor
                def _(pe):
                    rms_pe(pe)
                    finish_to("pe", pe, "ikiw")

                @block.scalar
                def _(act):
                    rms_act(act)
                    act.wait_ge(S("a_padded"), 1)
                    keep_at.update(qn=qn, kn=kn, vn=vn, ikd=ikd, iwn=iwn, iqT=iqT)
                    finish_to("act", act, "ikiw")
            done["dve"] = END["ikiw"]
            starts_at[0] = starts[END["ikiw"]]
            share = Share("r0", [6, 12] + [1.2] * 10)
            with nc.Block() as block:
                @block.vector
                def _(dve):
                    for a, nh, ss, g, sem in ((qn, 8, ssq, gq, "q"), (kn, 4, ssk, gk, "k")):
                        a2 = a.rearrange("p t (h d) -> p (t h) d", d=64)
                        t2 = tmp.rearrange("p t n -> p (t n)")[:, 0:5 * nh * 64].rearrange("p (g d) -> p g d", d=64)
                        vch.link(dve, dve.tensor_tensor(t2, a2, a2, ALU.mult))
                        dve.tensor_reduce(ss, t2, AX, ALU.add).then_inc(S("qk_sq"), 1)
                        dve.wait_ge(S("qk_rstd"), 1 if sem == "q" else 2)
                        vch.link(dve, dve.tensor_tensor(a2, a2, bc(ss, 2, 64), ALU.mult))
                        dve.tensor_tensor(a2, a2, bc(g, 1, 5 * nh), ALU.mult).then_inc(S(sem + "_normed"), 1)
                    dve.wait_ge(S("k_normed"), 1)
                    for u in range(2):
                        ins = dve.tensor_copy(kdup[:, :, :, u, :], kn.rearrange("p t (h d) -> p t h d", d=64))
                        ins.then_inc(S("k_doubled"), 1)

                @block.scalar
                def _(act):
                    for i, ss in enumerate((ssq, ssk)):
                        act.wait_ge(S("qk_sq"), i + 1)
                        ach.link(act, act.activation(ss, ss, ACT.Ln, bias=eps, scale=1.0 / 64))
                        act.activation(ss, ss, ACT.Exp, scale=-0.5).then_inc(S("qk_rstd"), 1)
                        share.point("act", act)
                    for g in range(10):
                        act.wait_ge(S("a_turned"), g + 1)
                        if g < 9:
                            dst = qT[:, g] if g < 4 else k2T[:, g - 4] if g < 8 else ikT
                            act.activation(dst[:, 0:SEQ], ps[g % 2][:, :], ACT.Copy)
                            ins = act.activation(dst[:, SEQ:T], ps[2 + g % 2][:, 0:NS], ACT.Copy)
                        else:
                            ins = act.activation(kTs, ps[4][:, 0:2 * NS].rearrange("p (j t) -> p j t", j=2), ACT.Copy)
                        ins.then_inc(S("a_turn_taken"), 1)
                        share.point("act", act)
                    share.end("act", act)

                @block.tensor
                def _(pe):
                    share.point("pe", pe)
                    share.point("pe", pe)
                    pe.wait_ge(S("q_normed"), 1)
                    for g in range(10):
                        if g == 4:
                            pe.wait_ge(S("k_doubled"), 2)
                        if g >= 2:
                            pe.wait_ge(S("a_turn_taken"), g - 1)
                        if g == 9:
                            for j in range(2):
                                mm = pe.transpose(ps[4][:, j * NS:j * NS + NS], kn[0:NS, 4, j * P:j * P + P], ident[0:NS, 0:NS])
                            mm.then_inc(S("a_turned"), 1)
                            share.point("pe", pe)
                            continue
                        for i, (t0, m) in enumerate(tiles):
                            if g < 4:
                                src = qn[0:m, i, g * P:g * P + P]
                            elif g < 8:
                                src = kdup[0:m, i, g - 4].rearrange("p u d -> p (u d)")
                            else:
                                src = ikd[0:m, i].rearrange("p u d -> p (u d)")
                            dst = ps[g % 2][:, t0:t0 + m] if m == P else ps[2 + g % 2][:, 0:m]
                            mm = pe.transpose(dst, src, ident[0:m, 0:m])
                        mm.then_inc(S("a_turned"), 1)
                        share.point("pe", pe)
                    share.end("pe", pe)

                @block.sync
                def _(sp):
                    def rows(name):
                        return out[name][lay].rearrange("o b (t p) h d -> p (o b t) (h d)", p=P)
                    sp.wait_ge(S("k_normed"), 1)
                    sp.dma_start(rows("k_prompt"), kn[:, 0:4, :]).then_inc(S("a_stored"), 16)
                    sp.dma_start(rows("v_prompt"), vn[:, 0:4, :]).then_inc(S("a_stored"), 16)
                    sp.dma_start(out["kidx_prompt"][lay].rearrange("o b (t p) d -> p (o b t) d", p=P), ikd[:, 0:4, 0, :]).then_inc(S("a_stored"), 16)
                    sp.dma_start(out["k_sample"][lay].rearrange("o b t h d -> (o b t) (h d)"), kn[0:NS, 4, :]).then_inc(S("a_stored"), 16)
                    sp.dma_start(out["v_sample"][lay].rearrange("o b t h d -> (o b t) (h d)"), vn[0:NS, 4, :]).then_inc(S("a_stored"), 16)
                    sp.dma_start(out["kidx_sample"][lay].rearrange("o b t d -> (o b t) d"), ikd[0:NS, 4, 0, :]).then_inc(S("a_stored"), 16)
                    sp.wait_ge(S("a_stored"), 96)

            ar = Arena(arena, keep + 4 * T, AN)
            R = ar.take(2, 512)
            score, work, bias = ar.take(512), ar.take(512), ar.take(512)
            m8 = ar.take(2, 8)
            St, Pr = ar.take(2, 512), ar.take(2, 512)
            PT = ar.take(2, 512)
            on = ar.take(2, 512)
            mx, sm = ar.take(2, 8), ar.take(2, 8)
            weights = []
            for i in range(NT):
                weights += [1] * 8 + [(1, 18, 25, 34)[i]] + [1] * 18
            share = Share("r3", weights)
            with nc.Block() as block:
                @block.sync
                def _(sp):
                    stream(sp, J["r3"] + 3, l)

                @block.tensor
                def _(pe):
                    for i in range(NT):
                        L = (i + 1) * P
                        q0 = i * P
                        for h in range(8):
                            n = i * 8 + h
                            r = (h % 2) * 64
                            if n >= 2:
                                pe.wait_ge(S("idx_relu"), n - 1)
                            if h < 2 and i:
                                pe.wait_ge(S("att_biased"), 8 * i)
                            pe.matmul(ps[n % 2][:, 0:L], iqT[r:r + 64, h // 2, q0:q0 + P], ikT[r:r + 64, 0:L]).then_inc(S("idx_logits"), 1)
                            share.point("pe", pe)

                        def scores(h):
                            n = i * 8 + h
                            r = (h % 2) * 64
                            if h < 2:
                                pe.wait_ge(S("idx_relu"), 8 * i + 8)
                            if n >= 2:
                                pe.wait_ge(S("att_biased"), n - 1)
                            pe.matmul(ps[n % 2][:, 0:L], qT[r:r + 64, h // 2, q0:q0 + P], k2T[r:r + 64, h // 2, 0:L]).then_inc(S("att_scores"), 1)

                        def turn_probs(h):
                            n = i * 8 + h
                            if n >= 2:
                                pe.wait_ge(S("probT_taken"), n - 1)
                            pe.wait_ge(S("att_probs"), n + 1)
                            for s in range(i + 1):
                                mm = pe.transpose(ps[2 + n % 2][:, s * P:s * P + P], Pr[:, n % 2, s * P:s * P + P], ident)
                            mm.then_inc(S("probT_ready"), 1)

                        def values(h):
                            n = i * 8 + h
                            pe.wait_ge(S("probT_taken"), n + 1)
                            if n >= 2:
                                pe.wait_ge(S("att_out"), n - 1)
                            if h == 1 and i:
                                pe.wait_ge(S("att_turn_taken"), i)
                            for s in range(i + 1):
                                mm = pe.matmul(ps[4 + n % 2][:, h * 64:h * 64 + 64], PT[:, n % 2, s * P:s * P + P],
                                               vn[:, s, (h // 2) * 64:(h // 2) * 64 + 64], start=(s == 0), stop=(s == i))
                            mm.then_inc(S("att_values"), 1)
                        share.point("pe", pe)
                        scores(0)
                        for h in range(9):
                            if h < 7:
                                scores(h + 1)
                            share.point("pe", pe)
                            if h < 8:
                                turn_probs(h)
                            share.point("pe", pe)
                            if h >= 1:
                                values(h - 1)
                        pe.wait_ge(S("att_out"), 8 * i + 8)
                        if i >= 1:
                            pe.wait_ge(S("att_turn_taken"), i)
                        for c in range(4):
                            mm = pe.transpose(ps[5][:, c * P:c * P + P], on[:, i % 2, c * P:c * P + P], ident)
                        mm.then_inc(S("att_turned"), 1)
                    share.end("pe", pe)

                @block.scalar
                def _(act):
                    for i in range(NT):
                        L = (i + 1) * P
                        for h in range(8):
                            n = i * 8 + h
                            act.wait_ge(S("idx_logits"), n + 1)
                            if n >= 2:
                                act.wait_ge(S("idx_summed"), n - 1)
                            act.activation(R[:, n % 2, 0:L], ps[n % 2][:, 0:L], ACT.Relu, scale=0.125).then_inc(S("idx_relu"), 1)
                            share.point("act", act)
                        share.point("act", act)
                        for h in range(9):
                            n = i * 8 + h
                            if h < 8:
                                act.wait_ge(S("att_max"), n + 1)
                                if n >= 2:
                                    act.wait_ge(S("probT_ready"), n - 1)
                                act.activation(Pr[:, n % 2, 0:L], St[:, n % 2, 0:L], ACT.Exp, bias=mx[:, n % 2, 0:1],
                                               accum_out=sm[:, n % 2, 0:1]).then_inc(S("att_probs"), 1)
                            share.point("act", act)
                            if h >= 1:
                                act.wait_ge(S("probT_ready"), n)
                                if n >= 3:
                                    act.wait_ge(S("att_values"), n - 2)
                                act.activation(PT[:, (n - 1) % 2, 0:L], ps[2 + (n - 1) % 2][:, 0:L], ACT.Copy).then_inc(S("probT_taken"), 1)
                            share.point("act", act)
                        act.wait_ge(S("att_turned"), i + 1)
                        act.activation(brT[:, 0:4, i * P:i * P + P], ps[5][:, :].rearrange("p (c t) -> p c t", c=4), ACT.Copy).then_inc(S("att_turn_taken"), 1)
                    share.end("act", act)

                @block.vector
                def _(dve):
                    for i in range(NT):
                        L = (i + 1) * P
                        dve.wait_ge(S("idx_relu"), i * 8 + 1)
                        vch.link(dve, dve.memset(score[:, 0:L], 0.0))
                        for h in range(8):
                            n = i * 8 + h
                            dve.wait_ge(S("idx_relu"), n + 1)
                            ins = dve.scalar_tensor_tensor(score[:, 0:L], R[:, n % 2, 0:L], iwn[:, i, h:h + 1],
                                                           score[:, 0:L], ALU.mult, ALU.add)
                            ins.then_inc(S("idx_summed"), 1)
                            dve.wait_ge(S("idx_summed"), n + 1)
                        vch.link(dve, dve.tensor_tensor(score[:, L - P:L], score[:, L - P:L], K("neg"), ALU.add))
                        topk(dve, score[:, 0:L], work[:, 0:L], bias[:, 0:L], m8, TOPK_P if L > TOPK_P else L)
                        vch.link(dve, dve.tensor_tensor(bias[:, L - P:L], bias[:, L - P:L], K("neg"), ALU.add))
                        for h in range(10):
                            n = i * 8 + h
                            if h >= 2:
                                dve.wait_ge(S("att_probs"), n - 1)
                                vch.link(dve, dve.reciprocal(sm[:, n % 2, 1:2], sm[:, n % 2, 0:1]))
                            if h < 8:
                                dve.wait_ge(S("att_scores"), n + 1)
                                if n >= 2:
                                    dve.wait_ge(S("att_probs"), n - 1)
                                dve.scalar_tensor_tensor(St[:, n % 2, 0:L], ps[n % 2][:, 0:L], 0.125, bias[:, 0:L],
                                                         ALU.mult, ALU.add).then_inc(S("att_biased"), 1)
                                dve.wait_ge(S("att_biased"), n + 1)
                                dve.tensor_reduce(mx[:, n % 2, 0:1], St[:, n % 2, 0:L], AX, ALU.max, negate=True).then_inc(S("att_max"), 1)
                            if h >= 2:
                                dve.wait_ge(S("att_values"), n - 1)
                                if h == 2 and i >= 2:
                                    dve.wait_ge(S("att_turned"), i - 1)
                                dve.tensor_scalar(on[:, i % 2, (h - 2) * 64:(h - 2) * 64 + 64], ps[4 + n % 2][:, (h - 2) * 64:(h - 2) * 64 + 64],
                                                  sm[:, n % 2, 1:2], None, ALU.mult).then_inc(S("att_out"), 1)
            stage_a_sample(l, idx_at, keep, vn, kTs, iwn, qT, ikT, iqT)

        def topk(dve, score, work, bias, m8, k):
            if k >= score.shape[1]:
                vch.link(dve, dve.memset(bias, 0.0))
                return
            for r in range(k // 8):
                src = score if r == 0 else work
                m = m8[0:score.shape[0], r % 2, :]
                vch.link(dve, dve.max(m, src))
                vch.link(dve, dve.match_replace(work, m, src, TAKEN))
            vch.link(dve, dve.tensor_scalar(bias, work, TAKEN, NEG, ALU.not_equal, ALU.mult))

        def stage_a_sample(l, idx_at, keep, vn, kTs, iwn, qT, ikT, iqT):
            lay = bass.ds(l, 1)
            ar = Arena(arena, keep, AN)
            bias = ar.take(LK)
            keep2 = ar.at
            ba = Arena(brT_, 4 * T, 16 * T)
            QP = ba.take(8, 2, 4, 32)
            qz = ba.take(2, 8, 8, 4)
            score, work = ar.take(LK), ar.take(LK)
            iqh = ar.take(8, 8, 4)
            IQP = ar.take(8, 4, 32)
            kx = ar.take(4, 4, 64)
            ikc = ar.take(2, 512)
            R = ar.take(2, 512)
            WS = ar.take(2, NS)
            w8, wcol = ar.take(2, 8), ar.take(2)
            m8 = ar.take(2, 8)
            steps = [(g, c, bb) for g in range(2) for c in range(4) for bb in range(4)]
            share = Share("xbc0", [1] * 32 + [160])

            def load_pages(eng, pages, dst, name, b, c, sem):
                for pg in pages:
                    at = b * NPG + 4 * c + pg
                    page = eng.value_load(ptab[0:1, at:at + 1], min_val=0, max_val=inp[name].shape[1] - 1)
                    if name == "cache_kidx":
                        src = inp[name][lay, bass.ds(page, 1)].rearrange("o q t d -> (o q t) d")
                    else:
                        src = inp[name][lay, bass.ds(page, 1)].rearrange("o q t g d -> (o q t) (g d)")
                    eng.dma_start(dst[:, pg, :], src).then_inc(S(sem), 16)

            def load_kidx(eng, pages, s):
                g, c, bb = steps[s]
                load_pages(eng, pages, kx[:, s % 4], "cache_kidx", 4 * g + bb, c, f"kidx_in{s % 4}")
            ia = Arena(arena, idx_at, keep)
            pages = [ia.take(4, 256) for _ in range(2)]
            KT = ba.take(2, 2, 512)
            pages += [ba.take(4, 256)]

            def k_at(s):
                return s // 16 * 32 + s % 16

            def v_at(s):
                return s // 16 * 32 + 16 + s % 16

            def load_step(eng, which, q):
                g, x = q // 32, q % 16
                if q % 32 < 16:
                    load_pages(eng, which, pages[q % 6], "cache_k", 4 * g + x % 4, x // 4, f"page_in{q % 6}")
                else:
                    load_pages(eng, which, pages[q % 6], "cache_v", 4 * g + x // 4, x % 4, f"page_in{q % 6}")

            def page_used(eng, q):
                s = 16 * (q // 32) + q % 16
                if q % 32 < 16:
                    eng.wait_ge(S("k_turned"), 2 * s + 2)
                else:
                    eng.wait_ge(S("v_used"), s + 1)

            with nc.Block() as block:
                @block.sync
                def _(sp):
                    for s, (g, c, bb) in enumerate(steps):
                        if s == 16:
                            stream(sp, J["c0"] + 2, l)
                        if s >= 4:
                            sp.wait_ge(S("kidx_turned"), s - 3)
                        load_kidx(sp, (0, 1), s)
                    sp.wait_ge(S("sidx_logits"), 10)
                    for q in range(3):
                        load_step(sp, (0, 1), q)
                    stream(sp, J["xbc0"] + 3, l)

                @block.tensor
                def _(pe):
                    for g in range(2):
                        mm = pe.matmul(ps[4][:, g * 8:g * 8 + 8], K("rep")[0:NS, g * P:g * P + P], iwn[0:NS, 4, :])
                    mm.then_inc(S("w_spread"), 1)
                    pe.wait_ge(S("iq_padded"), 1)
                    pe.wait_ge(S("wsel_ready"), 1)

                    def turn(s):
                        pe.wait_ge(S(f"kidx_in{s % 4}"), 64 * (s // 4 + 1))
                        if s >= 2:
                            pe.wait_ge(S("ikc_ready"), s - 1)
                        for pg in range(4):
                            mm = pe.transpose(ps[s % 2][0:64, pg * P:pg * P + P], kx[:, s % 4, pg, :], ident)
                        mm.then_inc(S("kidx_turned"), 1)

                    def weigh(u, w):
                        pe.wait_ge(S("sidx_relu"), u + 1)
                        if u >= 2:
                            pe.wait_ge(S("sidx_taken"), u - 1)
                        pe.matmul(ps[4 + u % 2][0:NS, 0:w], WS[:, u // 5, :], R[:, u % 2, 0:w]).then_inc(S("sidx_weighed"), 1)

                    turn(0)
                    for g in range(2):
                        for c in range(5):
                            u = g * 5 + c
                            if u >= 2:
                                pe.wait_ge(S("sidx_relu"), u - 1)
                            for bb in range(4):
                                if c < 4:
                                    s = (g * 4 + c) * 4 + bb
                                    if s + 1 < len(steps):
                                        turn(s + 1)
                                    share.point("pe", pe)
                                    pe.wait_ge(S("ikc_ready"), s + 1)
                                    mm = pe.matmul(ps[2 + u % 2][:, :], IQP[0:64, 4 * g + bb].rearrange("p a n -> p (a n)"),
                                                   ikc[0:64, s % 2, :], start=(bb == 0), stop=(bb == 3))
                                    if bb < 3:
                                        mm.then_inc(S("ikc_used"), 1)
                                else:
                                    mm = pe.matmul(ps[2 + u % 2][:, 0:NS], IQP[0:64, 4 * g + bb].rearrange("p a n -> p (a n)"),
                                                   ikT[0:64, SEQ:T], start=(bb == 0), stop=(bb == 3))
                            mm.then_inc(S("sidx_logits"), 1)
                            if u >= 1:
                                weigh(u - 1, NS if (u - 1) % 5 == 4 else 512)
                    weigh(9, NS)
                    share.point("pe", pe)
                    share.end("pe", pe)

                @block.gpsimd
                def _(pool):
                    pool.memset(qz, 0.0).then_inc(S("qz_zero"), 1)

                @block.scalar
                def _(act):
                    for s in range(4):
                        load_kidx(act, (2, 3), s)
                    for g in range(2):
                        for c in range(5):
                            u = g * 5 + c
                            if c < 4:
                                for bb in range(4):
                                    s = u // 5 * 16 + c * 4 + bb
                                    act.wait_ge(S("kidx_turned"), s + 1)
                                    if s >= 2:
                                        q = s - 2
                                        act.wait_ge(S("ikc_used"), q // 4 * 3 + min(q % 4 + 1, 3))
                                        if q % 4 == 3:
                                            act.wait_ge(S("sidx_logits"), q // 16 * 5 + q % 16 // 4 + 1)
                                    act.activation(ikc[0:64, s % 2, :], ps[s % 2][0:64, :], ACT.Copy).then_inc(S("ikc_ready"), 1)
                                    if s + 4 < len(steps):
                                        load_kidx(act, (2, 3), s + 4)
                                    share.point("act", act)
                            w = 512 if c < 4 else NS
                            act.wait_ge(S("sidx_logits"), u + 1)
                            if u >= 2:
                                act.wait_ge(S("sidx_weighed"), u - 1)
                            act.activation(R[:, u % 2, 0:w], ps[2 + u % 2][:, 0:w], ACT.Relu, scale=0.125).then_inc(S("sidx_relu"), 1)
                    for q in range(3):
                        load_step(act, (2, 3), q)
                    share.point("act", act)
                    share.end("act", act)

                @block.vector
                def _(dve):
                    for h in range(8):
                        r = (h % 2) * 64
                        ins = dve.tensor_copy(iqh[0:64, :, h, :], iqT[r:r + 64, h // 2, SEQ:T].rearrange("p (b t) -> p b t", b=NB))
                    vch.link(dve, ins)
                    bb = K("bb").rearrange("p (a b) -> p a b", a=4)
                    for b in range(NB):
                        ins = dve.tensor_tensor(IQP[0:64, b], bc(iqh[0:64, b].rearrange("p h t -> p (h t)"), 1, 4),
                                                bc(bb[0:64, b % 4], 2, 32), ALU.mult)
                    ins.then_inc(S("iq_padded"), 1)
                    dve.wait_ge(S("w_spread"), 1)
                    for g in range(2):
                        vch.link(dve, dve.tensor_tensor(w8[:, g, :], ps[4][:, g * 8:g * 8 + 8], K("hsel"), ALU.mult))
                        vch.link(dve, dve.tensor_reduce(wcol[:, g:g + 1], w8[:, g, :], AX, ALU.add))
                        ins = dve.tensor_scalar(WS[:, g, :], K("wsel")[:, g * NS:g * NS + NS], wcol[:, g:g + 1], None, ALU.mult)
                    ins.then_inc(S("wsel_ready"), 1)
                    dve.wait_ge(S("qz_zero"), 1)
                    for h in range(8):
                        r, j, g2 = (h % 2) * 64, h // 4, (h // 2) % 2
                        ins = dve.tensor_copy(qz[g2 * 64:g2 * 64 + 64, j, :, h, :], qT[r:r + 64, h // 2, SEQ:T].rearrange("p (b t) -> p b t", b=NB))
                    vch.link(dve, ins)
                    for u in range(10):
                        if u < NB:
                            for j in range(2):
                                dve.tensor_tensor(QP[:, u, j], bc(qz[:, j, u].rearrange("p h t -> p (h t)"), 1, 4),
                                                  bc(bb[:, u % 4], 2, 32), ALU.mult)
                        c, w = u % 5, (512 if u % 5 < 4 else NS)
                        dst = score[0:NS, c * 512:c * 512 + w]
                        dve.wait_ge(S("sidx_weighed"), u + 1)
                        if u < 5:
                            dve.tensor_copy(dst, ps[4 + u % 2][0:NS, 0:w]).then_inc(S("sidx_taken"), 1)
                        else:
                            dve.wait_ge(S("sidx_taken"), u - 4)
                            dve.tensor_tensor(dst, dst, ps[4 + u % 2][0:NS, 0:w], ALU.add).then_inc(S("sidx_taken"), 1)
                    dve.wait_ge(S("sidx_taken"), 10)
                    vch.link(dve, dve.tensor_tensor(score[0:NS, PAST:LK], score[0:NS, PAST:LK], K("neg_s")[0:NS], ALU.add))
                    topk(dve, score[0:NS], work[0:NS], bias[0:NS], m8, TOPK_S)
                    dve.tensor_tensor(bias[0:NS, PAST:LK], bias[0:NS, PAST:LK], K("neg_s")[0:NS], ALU.add)
            ar = Arena(arena, keep2, AN)
            St = ar.take(LK)
            Os = ar.take(NB, 256)
            PT = ar.take(17, P)
            mx, sm = ar.take(2), ar.take(4)
            pages += [ar.take(4, 256) for _ in range(3)]

            share = Share("dt", [1] + ([0.1] * 16 + [10] + [1] * 16) * 2)
            with nc.Block() as block:
                @block.sync
                def _(sp):
                    for q in range(3, 64):
                        if q >= 6:
                            page_used(sp, q - 6)
                        load_step(sp, (0, 1), q)
                    stream(sp, J["dt"] + 3, l)

                @block.tensor
                def _(pe):
                    share.point("pe", pe)

                    def turn(s):
                        q = k_at(s)
                        pe.wait_ge(S(f"page_in{q % 6}"), 64 * (q // 6 + 1))
                        for j in range(2):
                            n = 2 * s + j
                            if n >= 2:
                                pe.wait_ge(S("kt_ready"), n - 1)
                            for pg in range(4):
                                mm = pe.transpose(ps[j][:, pg * P:pg * P + P], pages[q % 6][:, pg, j * P:j * P + P], ident)
                            mm.then_inc(S("k_turned"), 1)

                    for g in range(2):
                        turn(16 * g)
                        for c in range(5):
                            u = g * 10 + c
                            w = 512 if c < 4 else NS
                            if u >= 2:
                                pe.wait_ge(S("sa_taken"), u - 1)
                            for bb in range(4):
                                b = 4 * g + bb
                                s = g * 16 + c * 4 + bb
                                if c < 4:
                                    if (s + 1) % 16:
                                        turn(s + 1)
                                    share.point("pe", pe)
                                    pe.wait_ge(S("kt_ready"), 2 * s + 2)
                                for j in range(2):
                                    rhs = KT[:, s % 2, j, :] if c < 4 else kTs[:, j, :]
                                    mm = pe.matmul(ps[4 + u % 2][:, 0:w], QP[:, b, j].rearrange("p a n -> p (a n)"), rhs,
                                                   start=(bb == 0 and j == 0), stop=False)
                                if c < 4:
                                    mm.then_inc(S("kt_used"), 1)
                            pe.matmul(ps[4 + u % 2][:, 0:w], K("rep")[0:NS, g * P:g * P + P], bias[0:NS, c * 512:c * 512 + w],
                                      start=False, stop=True).then_inc(S("sa_ready"), 1)
                        share.point("pe", pe)
                        for qd in range(5):
                            u = g * 10 + 5 + qd
                            pe.wait_ge(S("sa_taken"), u - 1)
                            pe.wait_ge(S("sprobs_ready"), g + 1)
                            for x in range(4 if qd < 4 else 1):
                                kt = qd * 4 + x
                                m = P if kt < 16 else NS
                                mm = pe.transpose(ps[4 + u % 2][0:m, x * P:x * P + P], St[:, kt * P:kt * P + m], ident)
                            mm.then_inc(S("sa_ready"), 1)
                        pe.wait_ge(S("sa_taken"), g * 10 + 10)
                        for bb in range(4):
                            b = 4 * g + bb
                            for c in range(4):
                                sv = b * 4 + c
                                q = v_at(sv)
                                pe.wait_ge(S(f"page_in{q % 6}"), 64 * (q // 6 + 1))
                                if c == 0 and b >= 2:
                                    pe.wait_ge(S("sv_taken"), b - 1)
                                for pg in range(4):
                                    mm = pe.matmul(ps[2 + b % 2][0:32, 0:256], PT[:, c * 4 + pg, bb * 32:bb * 32 + 32], pages[q % 6][:, pg, :],
                                                   start=(c == 0 and pg == 0), stop=False)
                                mm.then_inc(S("v_used"), 1)
                                share.point("pe", pe)
                            pe.matmul(ps[2 + b % 2][0:32, 0:256], PT[0:NS, 16, bb * 32:bb * 32 + 32], vn[0:NS, 4, :],
                                      start=False, stop=True).then_inc(S("sv_done"), 1)
                    pe.wait_ge(S("sv_taken"), NB)
                    for b in range(NB):
                        for j in range(2):
                            mm = pe.transpose(ps[0][:, j * 256 + b * 32:j * 256 + b * 32 + 32], Os[0:32, b, j * P:j * P + P], ident[0:32, 0:32])
                    mm.then_inc(S("sv_turned"), 1)
                    share.end("pe", pe)

                @block.scalar
                def _(act):
                    for q in range(3, 6):
                        load_step(act, (2, 3), q)
                    share.point("act", act)
                    for g in range(2):
                        for c in range(5):
                            u = g * 10 + c
                            w = 512 if c < 4 else NS
                            if c < 4:
                                for bb in range(4):
                                    s = g * 16 + c * 4 + bb
                                    if s >= 2:
                                        act.wait_ge(S("kt_used"), s - 1)
                                    for j in range(2):
                                        act.wait_ge(S("k_turned"), 2 * s + j + 1)
                                        act.activation(KT[:, s % 2, j, :], ps[j][:, :], ACT.Copy).then_inc(S("kt_ready"), 1)
                                    load_step(act, (2, 3), k_at(s) + 6)
                                    share.point("act", act)
                            act.wait_ge(S("sa_ready"), u + 1)
                            act.activation(St[:, c * 512:c * 512 + w], ps[4 + u % 2][:, 0:w], ACT.Copy, scale=0.125).then_inc(S("sa_taken"), 1)
                        act.wait_ge(S("smax_ready"), g + 1)
                        act.activation(St[:, :], St[:, :], ACT.Exp, bias=mx[:, g:g + 1], accum_out=sm[:, g:g + 1]).then_inc(S("sexp_ready"), 1)
                        share.point("act", act)
                        if g == 1:
                            act.wait_ge(S("sv_done"), 4)
                        for qd in range(5):
                            u = g * 10 + 5 + qd
                            act.wait_ge(S("sa_ready"), u + 1)
                            if qd < 4:
                                ins = act.activation(PT[:, qd * 4:qd * 4 + 4, :], ps[4 + u % 2][:, :].rearrange("p (a n) -> p a n", a=4), ACT.Copy)
                            else:
                                ins = act.activation(PT[0:NS, 16, :], ps[4 + u % 2][0:NS, 0:P], ACT.Copy)
                            ins.then_inc(S("sa_taken"), 1)
                        for bb in range(4):
                            b = 4 * g + bb
                            for c in range(4):
                                share.point("act", act)
                                q = v_at(4 * b + c)
                                if q + 6 < 64:
                                    page_used(act, q)
                                    load_step(act, (2, 3), q + 6)
                            act.wait_ge(S("sv_done"), b + 1)
                            act.activation(Os[0:32, b, :], ps[2 + b % 2][0:32, 0:256], ACT.Copy).then_inc(S("sv_taken"), 1)
                    share.end("act", act)

                @block.vector
                def _(dve):
                    for g in range(2):
                        dve.wait_ge(S("sa_taken"), g * 10 + 5)
                        dve.tensor_reduce(mx[:, g:g + 1], St[:, :], AX, ALU.max, negate=True).then_inc(S("smax_ready"), 1)
                        dve.wait_ge(S("sexp_ready"), g + 1)
                        vch.link(dve, dve.reciprocal(sm[:, 2 + g:3 + g], sm[:, g:g + 1]))
                        dve.tensor_scalar(St[:, :], St[:, :], sm[:, 2 + g:3 + g], None, ALU.mult).then_inc(S("sprobs_ready"), 1)
                    dve.wait_ge(S("sv_turned"), 1)
                    for h in range(8):
                        r, j, g2 = (h % 2) * 64, h // 4, (h // 2) % 2
                        src = ps[0][g2 * 64:g2 * 64 + 64, :].rearrange("p (j b h t) -> p j b h t", j=2, b=NB, h=8)[:, j, :, h, :]
                        dve.tensor_copy(brT[r:r + 64, h // 2, SEQ:T].rearrange("p (b t) -> p b t", b=NB), src)

        GAMMA = [1.0 - 2.0 ** (-5 - h) for h in range(4)]

        def stage_retention(l):
            lay = bass.ds(l, 1)
            ar = Arena(arena, 0, ANB)
            inputs = ar.take(2, 4, 512)
            q, k, v, g = ((lambda i, n=n: inputs[:, i % 2, n]) for n in range(4))
            S0 = ar.take(NB, 4, P)
            Sp = ar.take(4, P)
            t1, t2 = ar.take(512), ar.take(512)
            sm = ar.take(2, 4)
            qm = ar.take(NB, NS)
            sc = Arena(brT_, 8 * T, 16 * T)
            qT, kT, A = sc.take(4 * P), sc.take(4 * P), sc.take(4 * P)
            kd = (sc.take(512), ar.take(512))
            qr, kr = sc.take(512), sc.take(512)
            Vx = sc.take(NB, P)
            share = Share("wb01", [6] + [1] * 25)
            job0 = J["gate01"]
            with nc.Block() as block:
                @block.tensor
                def _(pe):
                    def turn(i):
                        m = tiles[i][1]
                        pe.wait_ge(S("b_qk_ready"), i + 1)
                        for bank, src in ((ps[0], qr), (ps[1], kr)):
                            for h in range(4):
                                mm = pe.transpose(bank[:, h * m:h * m + m], src[0:m, h * P:h * P + P], ident[0:m, 0:m])
                        mm.then_inc(S("b_turned"), 1)

                    share.point("pe", pe)
                    turn(0)
                    for i, (t0, m) in enumerate(tiles):
                        last = i == 4
                        share.point("pe", pe)
                        pe.wait_ge(S("b_turn_taken"), i + 1)
                        for h in range(4):
                            mm = pe.matmul(ps[2][0:m, h * m:h * m + m], kT[:, h * m:h * m + m], qT[:, h * m:h * m + m])
                        mm.then_inc(S("b_scores"), 1)
                        share.point("pe", pe)
                        pe.wait_ge(S("b_weights"), i + 1)
                        if last:
                            pe.wait_ge(S("b_state_in"), 64)
                        for h in range(4):
                            o = ps[3][0:m, h * P:h * P + P]
                            mm = pe.matmul(o, A[0:m, h * m:h * m + m], v(i)[0:m, h * P:h * P + P], start=True, stop=(i == 0))
                            if last:
                                pe.wait_ge(S("b_q_masked"), h + 1)
                                for b in range(NB):
                                    mm = pe.matmul(o, qm[:, b, :], S0[:, b, h, :], start=False, stop=(b == NB - 1))
                                mm.then_inc(S("b_q_mask_used"), 1)
                            elif i > 0:
                                mm = pe.matmul(o, qT[:, h * m:h * m + m], Sp[:, h, :], start=False, stop=True)
                        if not last:
                            for h in range(4):
                                mm = pe.matmul(ps[4][:, h * P:h * P + P], kd[i % 2][0:m, h * P:h * P + P], v(i)[0:m, h * P:h * P + P])
                            mm.then_inc(S("b_out"), 1)
                            turn(i + 1)
                        else:
                            for h in range(4):
                                pe.wait_ge(S("b_v_masked"), h + 1)
                                for half in range(2):
                                    n = 2 * h + half
                                    if n >= 2:
                                        pe.wait_ge(S("b_state_new"), n - 1)
                                    pe.matmul(ps[n % 2][:, :], kd[i % 2][0:NS, h * P:h * P + P],
                                              Vx[0:NS, half * 4:half * 4 + 4, :].rearrange("p b e -> p (b e)")).then_inc(S("b_state_add"), 1)
                        share.point("pe", pe)
                        share.point("pe", pe)
                        pe.wait_ge(S("b_y"), i + 1)
                        if i >= 1:
                            pe.wait_ge(S("b_y_taken"), i)
                        for h in range(4):
                            mm = pe.transpose(ps[5][:, h * m:h * m + m], t2[0:m, h * P:h * P + P], ident[0:m, 0:m])
                        mm.then_inc(S("b_y_turned"), 1)
                        share.point("pe", pe)
                    share.end("pe", pe)

                @block.scalar
                def _(act):
                    def gate(i):
                        m = tiles[i][1]
                        act.wait_ge(S(f"b_tile_in{i % 2}"), 16 * (i // 2 + 1))
                        act.activation(g(i)[0:m, :], g(i)[0:m, :], ACT.Silu).then_inc(S("b_inputs"), 1)

                    def take_turned(i):
                        m = tiles[i][1]
                        act.wait_ge(S("b_turned"), i + 1)
                        act.activation(kT[:, 0:4 * m], ps[1][:, 0:4 * m], ACT.Copy)
                        act.activation(qT[:, 0:4 * m], ps[0][:, 0:4 * m], ACT.Copy).then_inc(S("b_turn_taken"), 1)

                    share.point("act", act)
                    gate(0)
                    take_turned(0)
                    for i, (t0, m) in enumerate(tiles):
                        share.point("act", act)
                        if i < 4:
                            gate(i + 1)
                        share.point("act", act)
                        if i < 4:
                            take_turned(i + 1)
                        share.point("act", act)
                        act.wait_ge(S("b_sq"), i + 1)
                        ach.link(act, act.activation(sm[0:m, 1, :], sm[0:m, 1, :], ACT.Ln, bias=eps[0:m], scale=1.0 / P))
                        act.activation(sm[0:m, 1, :], sm[0:m, 1, :], ACT.Exp, scale=-0.5).then_inc(S("b_rstd"), 1)
                        share.point("act", act)
                        act.wait_ge(S("b_y_turned"), i + 1)
                        act.activation(brT[:, 4:8, t0:t0 + m], ps[5][:, 0:4 * m].rearrange("p (h t) -> p h t", h=4), ACT.Copy).then_inc(S("b_y_taken"), 1)
                        share.point("act", act)
                    share.end("act", act)

                @block.vector
                def _(dve):
                    hv = lambda a, m: a[0:m, :].rearrange("p (h d) -> p h d", h=4)
                    L = vch.link

                    def rotate(i):
                        m = tiles[i][1]
                        last = i == 4
                        dve.wait_ge(S(f"b_tile_in{i % 2}"), 16 * (i // 2 + 1))
                        cs = bc(K("cos").rearrange("p (t f) -> p t f", t=5)[0:m, i, :], 1, 4)
                        sn = bc(K("sin").rearrange("p (t f) -> p t f", t=5)[0:m, i, :], 1, 4)
                        a1, a2 = hv(t1, m)[:, :, 0:64], hv(t1, m)[:, :, 64:128]
                        for src, dst in ((q, qr), (k, kr)):
                            x1, x2 = hv(src(i), m)[:, :, 0:64], hv(src(i), m)[:, :, 64:128]
                            y1, y2 = hv(dst, m)[:, :, 0:64], hv(dst, m)[:, :, 64:128]
                            dve.tensor_tensor(y1, x1, cs, ALU.mult)
                            dve.tensor_tensor(a1, x2, sn, ALU.mult)
                            dve.tensor_tensor(y2, x1, sn, ALU.mult)
                            L(dve, dve.tensor_tensor(a2, x2, cs, ALU.mult))
                            dve.tensor_tensor(y1, y1, a1, ALU.subtract)
                            L(dve, dve.tensor_tensor(y2, y2, a2, ALU.add))
                        L(dve, dve.tensor_tensor(hv(qr, m), hv(qr, m), bc(K("rq_s" if last else "rq")[0:m], 2, P), ALU.mult))
                        dve.tensor_tensor(hv(kd[i % 2], m), hv(kr, m), bc(K("rk_s" if last else "rk")[0:m], 2, P), ALU.mult).then_inc(S("b_qk_ready"), 1)

                    share.point("dve", dve)
                    rotate(0)
                    for i, (t0, m) in enumerate(tiles):
                        last = i == 4
                        share.point("dve", dve)
                        dve.wait_ge(S("b_scores"), i + 1)
                        dve.tensor_tensor(A[0:m, 0:4 * m], ps[2][0:m, 0:4 * m], K("rdec_s" if last else "rdec")[0:m], ALU.mult).then_inc(S("b_weights"), 1)
                        share.point("dve", dve)
                        if last:
                            dve.wait_ge(S("b_turn_taken"), i + 1)
                            msk = K("qmask").rearrange("p (b t) -> p b t", b=NB)
                            for h in range(4):
                                if h >= 1:
                                    dve.wait_ge(S("b_q_mask_used"), h)
                                dve.tensor_tensor(qm, bc(qT[:, h * NS:h * NS + NS], 1, NB), msk, ALU.mult).then_inc(S("b_q_masked"), 1)
                            for h in range(4):
                                if h >= 1:
                                    dve.wait_ge(S("b_state_add"), 2 * h)
                                dve.tensor_tensor(Vx[0:NS], bc(v(4)[0:NS, h * P:h * P + P], 1, NB), bc(K("seqhot")[0:NS], 2, P), ALU.mult).then_inc(S("b_v_masked"), 1)
                                for half in range(2):
                                    n = 2 * h + half
                                    dve.wait_ge(S("b_state_add"), n + 1)
                                    if h == 0 and half == 0:
                                        dve.wait_ge(S("b_q_mask_used"), 4)
                                    st = S0[:, half * 4:half * 4 + 4, h, :]
                                    dve.scalar_tensor_tensor(st, st, GAMMA[h] ** TS, ps[n % 2][:, :].rearrange("p (b e) -> p b e", b=4),
                                                             ALU.mult, ALU.add).then_inc(S("b_state_new"), 1)
                        else:
                            rotate(i + 1)
                            dve.wait_ge(S("b_out"), i + 1)
                            for h in range(4):
                                add = ps[4][:, h * P:h * P + P]
                                if i == 0:
                                    ins = dve.tensor_copy(Sp[:, h, :], add)
                                else:
                                    ins = dve.scalar_tensor_tensor(Sp[:, h, :], Sp[:, h, :], GAMMA[h] ** P, add, ALU.mult, ALU.add)
                            if i == 3:
                                ins.then_inc(S("b_prompt_state"), 1)
                            else:
                                L(dve, ins)
                        o = hv(ps[3], m)
                        y, w = hv(t2, m), hv(t1, m)
                        L(dve, dve.tensor_reduce(sm[0:m, 0, :], o, AX, ALU.add))
                        L(dve, dve.tensor_scalar(sm[0:m, 0, :], sm[0:m, 0, :], 1.0 / P, None, ALU.mult))
                        if i >= 1:
                            dve.wait_ge(S("b_y_turned"), i)
                        L(dve, dve.tensor_tensor(y, o, bc(sm[0:m, 0, :], 2, P), ALU.subtract))
                        L(dve, dve.tensor_tensor(w, y, y, ALU.mult))
                        dve.tensor_reduce(sm[0:m, 1, :], w, AX, ALU.add).then_inc(S("b_sq"), 1)
                        share.point("dve", dve)
                        dve.wait_ge(S("b_rstd"), i + 1)
                        L(dve, dve.tensor_tensor(y, y, bc(sm[0:m, 1, :], 2, P), ALU.mult))
                        dve.wait_ge(S("b_inputs"), i + 1)
                        dve.tensor_tensor(t2[0:m, :], t2[0:m, :], g(i)[0:m, :], ALU.mult).then_inc(S("b_y"), 1)
                        share.point("dve", dve)
                        share.point("dve", dve)
                    share.end("dve", dve)

                @block.sync
                def _(sp):
                    for w in range(4):
                        sp.wait_ge(S(f"spilled{w}"), 16 * 5)
                    for i, (t0, m) in enumerate(tiles):
                        if i >= 2:
                            sp.wait_ge(S("b_y"), i - 1)
                        sp.dma_start(inputs[0:m, i % 2], spill[0:4, t0:t0 + m, :].rearrange("j t n -> t j n")).then_inc(S(f"b_tile_in{i % 2}"), 16)
                        if i == 1:
                            for b in range(0, NB, 2):
                                sp.dma_start(S0[:, b:b + 2].rearrange("p b h e -> p (b h) e"),
                                             inp["state_ret"][lay, b:b + 2].rearrange("o b h d e -> d (o b h) e")).then_inc(S("b_state_in"), 16)
                        if i >= 2:
                            stream(sp, min(job0 + i - 1, job0 + 2), l)
                    sp.wait_ge(S("b_y"), 4)
                    for w in range(4):
                        sp.wait_ge(S(f"spilled{w}"), 16 * 10)
                    sp.dma_start(inputs[:, 1], spill[4:8, 0:P, :].rearrange("j t n -> t j n")).then_inc(S("next_tile_in"), 16)
                    sp.wait_ge(S("b_prompt_state"), 1)
                    sp.dma_start(out["ret_prompt"][lay].rearrange("o b h d e -> d (o b h) e"), Sp).then_inc(S("ret_stored"), 16)
                    stream(sp, job0 + 4, l)
                    sp.wait_ge(S("b_state_new"), 8)
                    sp.dma_start(out["ret_sample"][lay].rearrange("o b h d e -> d (o b h) e"), S0.rearrange("p b h e -> p (b h) e")).then_inc(S("ret_stored"), 16)

        def stage_hgrn(l):
            lay = bass.ds(l, 1)
            ar = Arena(arena, 0, ANB)
            inputs = ar.take(2, 4, 512)
            q, k, v, g = ((lambda i, n=n: inputs[:, (i + 1) % 2, n]) for n in range(4))
            S0 = ar.take(NB, 4, P)
            Sp = ar.take(4, P)
            t1, t2 = ar.take(512), ar.take(512)
            sm = ar.take(3, 4)
            dec = ar.take(NB, 4)
            sf = ar.take(512)
            qm = ar.take(NB, NS)
            sc = Arena(brT_, 12 * T, 16 * T)
            qT, kT0, A, kd = sc.take(4 * P), sc.take(4 * P), sc.take(4 * P), sc.take(512)
            sc = Arena(brT_, 0, 4 * T)
            E = sc.take(2, 512)
            Vx = sc.take(NB, P)
            vx = Vx.rearrange("p b e -> p (b e)")
            D, kT = vx[:, 0:512], (kT0, vx[:, 512:1024])
            F1, F2 = vx[:, 0:512], vx[:, 512:1024]
            nlv = [7, 7, 7, 7, 2]
            lv0 = [0, 7, 14, 21, 28]
            weights = [4]
            for i in range(5):
                weights += [1] * (2 * nlv[i] + 1) + [4, 5, 2, 6, 4]
            share = Share("wb11", weights)
            job0 = J["gate11"]
            zbank = (0, 5)
            with nc.Block() as block:
                @block.tensor
                def _(pe):
                    def z_sums(i, x):
                        m = tiles[i][1]
                        if x < nlv[i]:
                            pe.matmul(ps[zbank[x % 2]][0:m, :], K("lv_sum").rearrange("p (l t) -> p l t", l=7)[0:m, x, 0:m], sf[0:m, :]).then_inc(S("c_lv_z"), 1)

                    def start_tile(i):
                        m = tiles[i][1]
                        last = i == 4
                        triu, aft = (K("tri_s")[0:NS], K("after_s")[0:NS]) if last else (tri, after)
                        pe.wait_ge(S("c_logf"), i + 1)
                        pe.matmul(ps[3][0:m, :], triu, sf[0:m, :])
                        pe.matmul(ps[4][0:m, :], aft, sf[0:m, :])
                        for h in range(4):
                            w = sf[0:m, h * P:h * P + P]
                            if last:
                                mm = pe.matmul(ps[5][:, h * NB:h * NB + NB], w, K("seqhot")[0:NS])
                            else:
                                mm = pe.matmul(ps[5][:, h:h + 1], w, ones[:, 0:1])
                        mm.then_inc(S("c_cum"), 1)
                        z_sums(i, 0)
                        pe.wait_ge(S("c_decays"), i + 1)
                        z_sums(i, 1)

                    share.point("pe", pe)
                    start_tile(0)
                    for i, (t0, m) in enumerate(tiles):
                        last = i == 4
                        pe.wait_ge(S("c_q_decayed"), i + 1)
                        for h in range(4):
                            mm = pe.transpose(ps[2][:, h * m:h * m + m], t1[0:m, h * P:h * P + P], ident[0:m, 0:m])
                        mm.then_inc(S("c_turned"), 1)
                        if i >= 1:
                            pe.wait_ge(S("c_y_taken"), i)
                        for x in range(nlv[i] + 1):
                            n = lv0[i] + x
                            if x < nlv[i]:
                                pe.wait_ge(S("c_lv_x"), n + 1)
                                if n >= 1:
                                    pe.wait_ge(S("c_lv_turn_taken"), n)
                                for h in range(4):
                                    mm = pe.transpose(ps[1][:, h * m:h * m + m], t2[0:m, h * P:h * P + P], ident[0:m, 0:m])
                                mm.then_inc(S("c_lv_turned"), 1)
                                z_sums(i, x + 2)
                            share.point("pe", pe)
                            if x >= 1:
                                pe.wait_ge(S("c_lv_turn_taken"), n)
                                if x == 1:
                                    pe.wait_ge(S("c_turn_taken"), i + 1)
                                if n >= 2:
                                    pe.wait_ge(S("c_lv_masked"), n - 1)
                                for h in range(4):
                                    xT_h = kT[(x - 1) % 2][:, h * m:h * m + m]
                                    mm = pe.matmul(ps[2][0:m, h * m:h * m + m], xT_h, xT_h)
                                mm.then_inc(S("c_lv_product"), 1)
                            share.point("pe", pe)
                        pe.wait_ge(S("c_weights"), i + 1)
                        if last:
                            pe.wait_ge(S("c_state_in"), 64)
                        for h in range(4):
                            o = ps[3][0:m, h * P:h * P + P]
                            mm = pe.matmul(o, A[0:m, h * m:h * m + m], v(i)[0:m, h * P:h * P + P], start=True, stop=(i == 0))
                            if last:
                                pe.wait_ge(S("c_q_masked"), h + 1)
                                for b in range(NB):
                                    mm = pe.matmul(o, qm[:, b, :], S0[:, b, h, :], start=False, stop=(b == NB - 1))
                                mm.then_inc(S("c_q_mask_used"), 1)
                            elif i > 0:
                                mm = pe.matmul(o, qT[:, h * m:h * m + m], Sp[:, h, :], start=False, stop=True)
                        if not last:
                            for h in range(4):
                                mm = pe.matmul(ps[4][:, h * P:h * P + P], kd[0:m, h * P:h * P + P], v(i)[0:m, h * P:h * P + P])
                            mm.then_inc(S("c_out"), 1)
                        else:
                            for h in range(4):
                                pe.wait_ge(S("c_v_masked"), h + 1)
                                for half in range(2):
                                    n = 2 * h + half
                                    if n >= 2:
                                        pe.wait_ge(S("c_state_new"), n - 1)
                                    pe.matmul(ps[(0, 5)[n % 2]][:, :], kd[0:NS, h * P:h * P + P],
                                              Vx[0:NS, half * 4:half * 4 + 4, :].rearrange("p b e -> p (b e)")).then_inc(S("c_state_add"), 1)
                        share.point("pe", pe)
                        share.point("pe", pe)
                        if not last:
                            start_tile(i + 1)
                        share.point("pe", pe)
                        pe.wait_ge(S("c_y"), i + 1)
                        for h in range(4):
                            mm = pe.transpose(ps[1][:, h * m:h * m + m], t2[0:m, h * P:h * P + P], ident[0:m, 0:m])
                        mm.then_inc(S("c_y_turned"), 1)
                        share.point("pe", pe)
                    share.end("pe", pe)

                @block.scalar
                def _(act):
                    def gates(i):
                        m = tiles[i][1]
                        if i == 0:
                            act.wait_ge(S("next_tile_in"), 16)
                        else:
                            act.wait_ge(S(f"c_tile_in{i % 2}"), 16 * ((i + 1) // 2))
                        ach.link(act, act.activation(sf[0:m, :], k(i)[0:m, :], ACT.Sigmoid))
                        act.activation(k(i)[0:m, :], k(i)[0:m, :], ACT.Sigmoid, scale=-1.0).then_inc(S("c_gates"), 1)
                        act.activation(q(i)[0:m, :], q(i)[0:m, :], ACT.Silu)
                        act.activation(g(i)[0:m, :], g(i)[0:m, :], ACT.Silu).then_inc(S("c_inputs"), 1)

                    def forget_logs(i):
                        m = tiles[i][1]
                        act.wait_ge(S("c_forget"), i + 1)
                        act.activation(F1[0:m, :], F1[0:m, :], ACT.Ln)
                        act.activation(F2[0:m, :], F2[0:m, :], ACT.Ln).then_inc(S("c_logs"), 1)

                    def decays(i):
                        m = tiles[i][1]
                        act.wait_ge(S("c_cum"), i + 1)
                        act.activation(E[0:m, 1, :], ps[3][0:m, :], ACT.Exp)
                        act.activation(kd[0:m, :], ps[4][0:m, :], ACT.Exp)
                        if i == 4:
                            ins = act.activation(dec, ps[5][:, 0:4 * NB].rearrange("p (h b) -> p b h", h=4), ACT.Exp)
                        else:
                            ins = act.activation(dec[:, 0, :], ps[5][:, 0:4], ACT.Exp)
                        ins.then_inc(S("c_decays"), 1)
                        level_decay(i, 0)

                    def level_decay(i, x):
                        m = tiles[i][1]
                        if x < nlv[i]:
                            act.wait_ge(S("c_lv_z"), lv0[i] + x + 1)
                            if x == 1:
                                act.wait_ge(S("c_q_decayed"), i + 1)
                            if x >= 2:
                                act.wait_ge(S("c_lv_x"), lv0[i] + x - 1)
                            act.activation(E[0:m, x % 2, :], ps[zbank[x % 2]][0:m, :], ACT.Exp).then_inc(S("c_lv_e"), 1)

                    gates(0)
                    forget_logs(0)
                    share.point("act", act)
                    decays(0)
                    for i, (t0, m) in enumerate(tiles):
                        level_decay(i, 1)
                        act.wait_ge(S("c_turned"), i + 1)
                        act.activation(qT[:, 0:4 * m], ps[2][:, 0:4 * m], ACT.Copy).then_inc(S("c_turn_taken"), 1)
                        for x in range(nlv[i] + 1):
                            n = lv0[i] + x
                            if x < nlv[i]:
                                act.wait_ge(S("c_lv_turned"), n + 1)
                                if n >= 2:
                                    act.wait_ge(S("c_lv_product"), n - 1)
                                act.activation(kT[x % 2][:, 0:4 * m], ps[1][:, 0:4 * m], ACT.Copy).then_inc(S("c_lv_turn_taken"), 1)
                                level_decay(i, x + 2)
                            if x == nlv[i] - 1 and i < 4:
                                gates(i + 1)
                            share.point("act", act)
                            share.point("act", act)
                        if i < 4:
                            forget_logs(i + 1)
                        share.point("act", act)
                        act.wait_ge(S("c_sq"), i + 1)
                        ach.link(act, act.activation(sm[0:m, 1, :], sm[0:m, 1, :], ACT.Ln, bias=eps[0:m], scale=1.0 / P))
                        act.activation(sm[0:m, 1, :], sm[0:m, 1, :], ACT.Exp, scale=-0.5).then_inc(S("c_rstd"), 1)
                        share.point("act", act)
                        if i < 4:
                            decays(i + 1)
                        share.point("act", act)
                        act.wait_ge(S("c_y_turned"), i + 1)
                        act.activation(brT[:, 8:12, t0:t0 + m], ps[1][:, 0:4 * m].rearrange("p (h t) -> p h t", h=4), ACT.Copy).then_inc(S("c_y_taken"), 1)
                        share.point("act", act)
                    share.end("act", act)

                @block.vector
                def _(dve):
                    hv = lambda a, m: a[0:m, :].rearrange("p (h d) -> p h d", h=4)
                    L = vch.link

                    def forget(i):
                        m = tiles[i][1]
                        qi, ki, fi = q(i)[0:m, :], k(i)[0:m, :], sf[0:m, :]
                        dve.wait_ge(S("c_gates"), i + 1)
                        L(dve, dve.tensor_tensor(fi, fi, oml[0:m], ALU.mult))
                        L(dve, dve.tensor_tensor(fi, fi, lb[0:m], ALU.add))
                        dve.tensor_scalar(F1[0:m, :], fi, 2.0 ** -60, None, ALU.max)
                        L(dve, dve.tensor_scalar(F2[0:m, :], fi, 1e-30, 2.0 ** -60, ALU.max, ALU.min))
                        dve.tensor_scalar(F2[0:m, :], F2[0:m, :], 2.0 ** 60, None, ALU.mult).then_inc(S("c_forget"), 1)
                        dve.tensor_tensor(ki, ki, oml[0:m], ALU.mult)
                        dve.wait_ge(S("c_inputs"), i + 1)
                        L(dve, dve.tensor_scalar(qi, qi, P ** -0.5, None, ALU.mult))

                    def log_forget(i):
                        m = tiles[i][1]
                        dve.wait_ge(S("c_logs"), i + 1)
                        L(dve, dve.tensor_tensor(sf[0:m, :], F1[0:m, :], F2[0:m, :], ALU.add))
                        dve.tensor_tensor(F2[0:m, :], q(i)[0:m, :], k(i)[0:m, :], ALU.mult).then_inc(S("c_logf"), 1)
                        dve.wait_ge(S("c_logf"), i + 1)
                        L(dve, dve.tensor_reduce(sm[0:m, 2, :], hv(F2, m), AX, ALU.add))

                    share.point("dve", dve)
                    forget(0)
                    log_forget(0)
                    for i, (t0, m) in enumerate(tiles):
                        last = i == 4
                        qi, ki, fi = q(i)[0:m, :], k(i)[0:m, :], sf[0:m, :]
                        dve.wait_ge(S("c_decays"), i + 1)
                        dve.tensor_tensor(t1[0:m, :], qi, E[0:m, 1, :], ALU.mult).then_inc(S("c_q_decayed"), 1)
                        dve.wait_ge(S("c_q_decayed"), i + 1)
                        L(dve, dve.tensor_tensor(qi, qi, ki, ALU.subtract))
                        if i >= 1:
                            dve.wait_ge(S("c_y_turned"), i)

                        def level_x(x):
                            n = lv0[i] + x
                            if x >= 1:
                                dve.wait_ge(S("c_lv_turned"), n)
                            L(dve, dve.scalar_tensor_tensor(t2[0:m, :], qi, K("lv_side")[0:m, x:x + 1], ki, ALU.mult, ALU.add))
                            dve.wait_ge(S("c_lv_e"), n + 1)
                            dve.tensor_tensor(t2[0:m, :], t2[0:m, :], E[0:m, x % 2, :], ALU.mult).then_inc(S("c_lv_x"), 1)

                        def level_add(x):
                            n = lv0[i] + x
                            dve.wait_ge(S("c_lv_product"), n + 1)
                            msk = bc(K("lv_mask").rearrange("p (l t) -> p l t", l=7)[0:m, x, 0:m], 1, 4)
                            dst = A if x == 0 else D
                            dve.tensor_tensor(dst[0:m, 0:4 * m].rearrange("p (h n) -> p h n", h=4),
                                              ps[2][0:m, 0:4 * m].rearrange("p (h n) -> p h n", h=4), msk, ALU.mult).then_inc(S("c_lv_masked"), 1)
                            dve.wait_ge(S("c_lv_masked"), n + 1)
                            if x:
                                ins = dve.tensor_tensor(A[0:m, 0:4 * m], A[0:m, 0:4 * m], D[0:m, 0:4 * m], ALU.add)
                                if x == nlv[i] - 1:
                                    ins.then_inc(S("c_weights"), 1)
                                else:
                                    L(dve, ins)

                        for x in range(nlv[i] + 2):
                            if x < nlv[i]:
                                level_x(x)
                            if x == 0:
                                L(dve, dve.tensor_tensor(kd[0:m, :], ki, kd[0:m, :], ALU.mult))
                            if x >= 1:
                                share.point("dve", dve)
                            if x >= 2:
                                level_add(x - 2)
                            if x <= nlv[i]:
                                share.point("dve", dve)
                        dve.wait_ge(S("c_weights"), i + 1)
                        if last:
                            dve.wait_ge(S("c_turn_taken"), i + 1)
                            msk = K("qmask").rearrange("p (b t) -> p b t", b=NB)
                            for h in range(4):
                                if h >= 1:
                                    dve.wait_ge(S("c_q_mask_used"), h)
                                dve.tensor_tensor(qm, bc(qT[:, h * NS:h * NS + NS], 1, NB), msk, ALU.mult).then_inc(S("c_q_masked"), 1)
                            for h in range(4):
                                if h >= 1:
                                    dve.wait_ge(S("c_state_add"), 2 * h)
                                dve.tensor_tensor(Vx[0:NS], bc(v(4)[0:NS, h * P:h * P + P], 1, NB), bc(K("seqhot")[0:NS], 2, P), ALU.mult).then_inc(S("c_v_masked"), 1)
                                for half in range(2):
                                    n = 2 * h + half
                                    dve.wait_ge(S("c_state_add"), n + 1)
                                    if h == 0 and half == 0:
                                        dve.wait_ge(S("c_q_mask_used"), 4)
                                    st = S0[:, half * 4:half * 4 + 4, h, :]
                                    add = ps[(0, 5)[n % 2]][:, :].rearrange("p (b e) -> p b e", b=4)
                                    L(dve, dve.tensor_tensor(st, st, bc(dec[:, half * 4:half * 4 + 4, h], 2, P), ALU.mult))
                                    dve.tensor_tensor(st, st, add, ALU.add).then_inc(S("c_state_new"), 1)
                        else:
                            forget(i + 1)
                            dve.wait_ge(S("c_out"), i + 1)
                            if i == 0:
                                dve.wait_ge(S("ret_stored"), 32)
                            for h in range(4):
                                add = ps[4][:, h * P:h * P + P]
                                if i == 0:
                                    ins = dve.tensor_copy(Sp[:, h, :], add)
                                else:
                                    ins = dve.scalar_tensor_tensor(Sp[:, h, :], Sp[:, h, :], dec[:, 0, h:h + 1], add, ALU.mult, ALU.add)
                            if i == 3:
                                ins.then_inc(S("c_prompt_state"), 1)
                            else:
                                L(dve, ins)
                        o = hv(ps[3], m)
                        y, w = hv(t2, m), hv(t1, m)
                        for h in range(4):
                            ins = dve.scalar_tensor_tensor(y[:, h], hv(v(i), m)[:, h], sm[0:m, 2, h:h + 1], o[:, h], ALU.mult, ALU.add)
                        L(dve, ins)
                        dve.wait_ge(S("c_turned"), i + 1)
                        L(dve, dve.tensor_tensor(w, y, y, ALU.mult))
                        dve.tensor_reduce(sm[0:m, 1, :], w, AX, ALU.add).then_inc(S("c_sq"), 1)
                        if not last:
                            log_forget(i + 1)
                        share.point("dve", dve)
                        share.point("dve", dve)
                        dve.wait_ge(S("c_rstd"), i + 1)
                        L(dve, dve.tensor_tensor(y, y, bc(sm[0:m, 1, :], 2, P), ALU.mult))
                        L(dve, dve.tensor_tensor(y, y, bc(ghg[0:m], 1, 4), ALU.mult))
                        dve.tensor_tensor(t2[0:m, :], t2[0:m, :], g(i)[0:m, :], ALU.mult).then_inc(S("c_y"), 1)
                        share.point("dve", dve)
                        share.point("dve", dve)
                    share.end("dve", dve)

                @block.sync
                def _(sp):
                    for i, (t0, m) in enumerate(tiles):
                        if i >= 2:
                            sp.wait_ge(S("c_y"), i - 1)
                        if i:
                            sp.dma_start(inputs[0:m, (i + 1) % 2], spill[4:8, t0:t0 + m, :].rearrange("j t n -> t j n")).then_inc(S(f"c_tile_in{i % 2}"), 16)
                        if i == 1:
                            sp.wait_ge(S("ret_stored"), 32)
                            for b in range(0, NB, 2):
                                sp.dma_start(S0[:, b:b + 2].rearrange("p b h e -> p (b h) e"),
                                             inp["state_hgrn"][lay, b:b + 2].rearrange("o b h d e -> d (o b h) e")).then_inc(S("c_state_in"), 16)
                        if i >= 2:
                            stream(sp, min(job0 + i - 1, job0 + 2), l)
                    sp.wait_ge(S("c_prompt_state"), 1)
                    sp.dma_start(out["hgrn_prompt"][lay].rearrange("o b h d e -> d (o b h) e"), Sp).then_inc(S("hgrn_stored"), 16)
                    stream(sp, job0 + 4, l)

        def stage_ssm(l):
            lay = bass.ds(l, 1)
            ar = Arena(arena, 0, ANB)
            dt, a = ar.take(5, 8), ar.take(5, 8)
            xc = ar.take(8, T)
            keep = ar.at
            raw = Arena(brT_, 0, 8 * T).take(8, SEQ + 3)
            ar = Arena(arena, 2 * 4 * 512 + NB * 4 * P + 4 * P, ANB)
            raws = ar.take(8, NB, 7)
            xs_in = ar.take(8, NS)
            cv = Arena(brT_, 12 * T, 16 * T)
            cp, cs = cv.take(DM), cv.take(DM)
            cst_in = cs
            tail = ar.take(8, NB * 3)
            acc, accs = ar.take(2, SEQ), cv.take(2, NS)
            ut, au = ar.take(5, 8), ar.take(5, 8)
            ea = ar.take(8)
            share = Share("wb20", [4] + [1] * 8)
            with nc.Block() as block:
                @block.gpsimd
                def _(pool):
                    pool.memset(raw[:, :, 0:3], 0.0)
                    pool.memset(dt[:, 4, :], 0.0).then_inc(S("d_padded"), 1)

                @block.vector
                def _(dve):
                    L = vch.link
                    share.point("dve", dve)
                    dve.wait_ge(S("conv_in_taken"), 1)
                    dve.wait_ge(S("d_in"), 16 * 5)
                    L(dve, dve.tensor_copy(raws[:, :, :, 3:7], xs_in.rearrange("p c (b t) -> p c b t", b=NB)))
                    dve.tensor_copy(tail.rearrange("p c (b j) -> p c b j", b=NB), raws[:, :, :, 4:7]).then_inc(S("tail_ready"), 1)
                    L(dve, dve.tensor_tensor(ut, dt, bc(dtb, 1, 5), ALU.add))
                    L(dve, dve.tensor_scalar(au, ut, -1.0, None, ALU.mult))
                    dve.tensor_tensor(au, au, ut, ALU.max).then_inc(S("dt_abs"), 1)
                    dve.wait_ge(S("dt_log"), 1)
                    L(dve, dve.scalar_tensor_tensor(dt, ut, 0.0, au, ALU.max, ALU.add))
                    dve.scalar_tensor_tensor(a, dt, -1.0, bc(ea, 1, 5), ALU.mult, ALU.mult)
                    for c in range(8):
                        if c >= 2:
                            dve.wait_ge(S("conv_taken"), c - 1)
                        ap_, as_ = acc[:, c % 2, :], accs[:, c % 2, :].rearrange("p (b t) -> p b t", b=NB)
                        dve.tensor_scalar(ap_, raw[:, c, 0:SEQ], cw[:, 0, c:c + 1], cb[:, c:c + 1], ALU.mult, ALU.add)
                        L(dve, dve.tensor_scalar(as_, raws[:, c, :, 0:4], cw[:, 0, c:c + 1], cb[:, c:c + 1], ALU.mult, ALU.add))
                        for j in range(1, 4):
                            dve.scalar_tensor_tensor(ap_, raw[:, c, j:j + SEQ], cw[:, j, c:c + 1], ap_, ALU.mult, ALU.add)
                            ins = dve.scalar_tensor_tensor(as_, raws[:, c, :, j:j + 4], cw[:, j, c:c + 1], as_, ALU.mult, ALU.add)
                            if j < 3:
                                L(dve, ins)
                        ins.then_inc(S("conv_ready"), 1)
                        share.point("dve", dve)
                    share.end("dve", dve)

                @block.scalar
                def _(act):
                    share.point("act", act)
                    act.wait_ge(S("conv_in_turned"), 1)
                    for c in range(8):
                        ins = act.activation(raws[:, c, :, 0:3], ps[4][:, c * 24:c * 24 + 24].rearrange("p (b j) -> p b j", b=NB), ACT.Copy)
                    ins.then_inc(S("conv_in_taken"), 1)
                    act.wait_ge(S("dt_abs"), 1)
                    act.activation(ea, alog, ACT.Exp)
                    ach.link(act, act.activation(au, au, ACT.Exp, scale=-1.0))
                    act.activation(au, au, ACT.Ln, bias=ones[:, 0:1]).then_inc(S("dt_log"), 1)
                    for c in range(8):
                        if c == 7:
                            act.wait_ge(S("hgrn_stored"), 32)
                        act.wait_ge(S("conv_ready"), c + 1)
                        act.activation(xc[:, c, 0:SEQ], acc[:, c % 2, :], ACT.Silu)
                        act.activation(xc[:, c, SEQ:T], accs[:, c % 2, :], ACT.Silu).then_inc(S("conv_taken"), 1)
                        share.point("act", act)
                    share.end("act", act)
                    act.wait_ge(S("conv_state_turned"), 1)
                    for half in range(2):
                        act.activation(cp[0:3, half * 512:half * 512 + 512], ps[half][0:3, :], ACT.Copy)
                        ins = act.activation(cs[0:24, half * 512:half * 512 + 512], ps[2 + half][0:24, :], ACT.Copy)
                    ins.then_inc(S("conv_state_ready"), 1)

                @block.tensor
                def _(pe):
                    share.point("pe", pe)
                    pe.wait_ge(S("conv_in"), 16)
                    for c in range(8):
                        mm = pe.transpose(ps[4][:, c * 24:c * 24 + 24], cst_in[0:24, c * P:c * P + P], ident[0:24, 0:24])
                    mm.then_inc(S("conv_in_turned"), 1)
                    for c in range(8):
                        share.point("pe", pe)
                    share.end("pe", pe)
                    pe.wait_ge(S("tail_ready"), 1)
                    pe.wait_ge(S("d_in"), 16 * 5)
                    for c in range(8):
                        at = c % 4 * P
                        pe.transpose(ps[c // 4][0:3, at:at + P], raw[:, c, SEQ:SEQ + 3], ident)
                        mm = pe.transpose(ps[2 + c // 4][0:24, at:at + P], tail[:, c, :], ident)
                    mm.then_inc(S("conv_state_turned"), 1)

                @block.sync
                def _(sp):
                    for w in range(4):
                        sp.wait_ge(S(f"spilled{w}"), 16 * (17 if w < 2 else 16))
                    sp.dma_start(cst_in[0:24, :], inp["state_conv"][lay].rearrange("o b j n -> (o b j) n")).then_inc(S("conv_in"), 16)
                    sp.dma_start(xs_in, spill_x[:, SEQ:T].rearrange("(c p) t -> p c t", p=P)).then_inc(S("d_in"), 16)
                    sp.wait_ge(S("d_padded"), 1)
                    sp.dma_start(dt[:, 0:4, :], spill_dt[0:SEQ].rearrange("(t p) h -> p t h", p=P)).then_inc(S("d_in"), 16)
                    sp.dma_start(dt[0:NS, 4, :], spill_dt[SEQ:T]).then_inc(S("d_in"), 16)
                    for half in range(2):
                        sp.dma_start(raw[:, half * 4:half * 4 + 4, 3:SEQ + 3],
                                     spill_x[half * 512:half * 512 + 512, 0:SEQ].rearrange("(c p) t -> p c t", p=P)).then_inc(S("d_in"), 16)
                    S0 = arena[:, 2 * 4 * 512:2 * 4 * 512 + NB * 4 * P].rearrange("p (b h e) -> p (b h) e", b=NB, h=4)
                    sp.dma_start(out["hgrn_sample"][lay].rearrange("o b h d e -> d (o b h) e"), S0).then_inc(S("hgrn_stored"), 16)
                    stream(sp, J["wb21"] + 1, l)
                    sp.wait_ge(S("conv_state_ready"), 1)
                    sp.dma_start(out["conv_prompt"][lay].rearrange("o b j n -> (o b j) n"), cp[0:3, :]).then_inc(S("conv_stored"), 16)
                    sp.dma_start(out["conv_sample"][lay].rearrange("o b j n -> (o b j) n"), cs[0:24, :]).then_inc(S("conv_stored"), 16)
            ar = Arena(arena, keep, ANB)
            z = ar.take(2, 512)
            h0 = Arena(brT_, 0, 8 * T).take(NB, 4, P)
            AW, W = ar.take(8 * P), ar.take(8 * P)
            xn2, xw, hp, y = ar.take(2, 512), ar.take(512), ar.take(512), ar.take(512)
            t_x = AW[:, 512:1024]
            Bn2 = ar.take(2, 256)
            ec2 = ar.take(2, 3, 8)
            wt = ar.take(8)
            ss = ar.take(2)
            dec = ar.take(4, NB)
            t = xw
            hs = (W[:, 0:512], AW[:, 0:512])
            CM = W[:, 512:1024].rearrange("p (g b t) -> p g b t", g=2, b=NB)
            Bx = AW.rearrange("p (b s) -> p b s", b=NB)
            def load_state(sp):
                for b in range(0, NB, 2):
                    sp.dma_start(h0[:, b:b + 2].rearrange("p b q s -> p (b q) s"),
                                 inp["state_ssm"][lay, b:b + 2].rearrange("o b (q x) p s -> (x p) (o b q) s", x=2)).then_inc(S("ssm_in"), 16)

            share = Share("wb21", [1, 4] + [2, 2, 2, 2, 1] * 5)
            job0 = J["gate21"]
            with nc.Block() as block:
                @block.sync
                def _(sp):
                    for i, (t0, m) in enumerate(tiles):
                        if i >= 2:
                            sp.wait_ge(S("d_y"), i - 1)
                        sp.dma_start(z[0:m, i % 2, :], spill[8, t0:t0 + m, :]).then_inc(S(f"z_in{i % 2}"), 16)
                        if i == 1:
                            load_state(sp)
                        if i >= 2:
                            stream(sp, min(job0 + i - 1, job0 + 2), l)
                    stream(sp, job0 + 4, l)
                    sp.wait_ge(S("ssm_new"), 8)
                    sp.dma_start(out["ssm_sample"][lay].rearrange("o b (q x) p s -> (x p) (o b q) s", x=2), h0.rearrange("p b q s -> p (b q) s")).then_inc(S("ssm_stored"), 16)
                    sp.wait_ge(S("ssm_prompt_ready"), 1)
                    sp.dma_start(out["ssm_prompt"][lay].rearrange("o b (q x) p s -> (x p) (o b q) s", x=2), hp.rearrange("p (q s) -> p q s", q=4)).then_inc(S("ssm_stored"), 16)

                @block.tensor
                def _(pe):
                    def front(i):
                        t0, m = tiles[i]
                        triu, aft = (K("tri_s")[0:NS], K("after_s")[0:NS]) if i == 4 else (tri, after)
                        for c in range(4):
                            pe.transpose(ps[0][0:m, c * P:c * P + P], xc[:, c, t0:t0 + m], ident)
                        for c in range(2):
                            pe.transpose(ps[1][0:m, c * P:c * P + P], xc[:, 4 + c, t0:t0 + m], ident)
                        for c in range(2):
                            pe.matmul(ps[2][0:m, c * m:c * m + m], xc[:, 4 + c, t0:t0 + m], xc[:, 6 + c, t0:t0 + m])
                        pe.matmul(ps[2][0:m, 256:264], triu, a[0:m, i, :])
                        mm = pe.matmul(ps[2][0:m, 264:272], aft, a[0:m, i, :])
                        if i < 4:
                            mm = pe.matmul(ps[2][:, 272:280], ones, a[:, i, :])
                        mm.then_inc(S("d_turned"), 1)

                    front(0)
                    share.point("pe", pe)
                    share.point("pe", pe)
                    for i, (t0, m) in enumerate(tiles):
                        xn, Bn, ec = xn2[:, i % 2], Bn2[:, i % 2], ec2[:, i % 2]
                        last = i == 4
                        triu, aft = (K("tri_s")[0:NS], K("after_s")[0:NS]) if last else (tri, after)
                        if last:
                            pe.wait_ge(S("ssm_prompt_ready"), 1)
                        pe.wait_ge(S("d_segs"), i + 1)
                        for h in range(8):
                            mm = pe.matmul(ps[3 + h // 4][0:m, h % 4 * m:h % 4 * m + m], AW[0:m, h * m:h * m + m], triu)
                        mm.then_inc(S("d_seg_sums"), 1)
                        share.point("pe", pe)
                        share.point("pe", pe)
                        pe.wait_ge(S("d_weights"), i + 1)
                        if i >= 1:
                            pe.wait_ge(S("d_y_taken"), i)
                        for h in range(8):
                            mm = pe.matmul(ps[5][0:m, h * 64:h * 64 + 64], W[0:m, h * m:h * m + m], t_x[0:m, h * 64:h * 64 + 64])
                        if not last:
                            for gg in range(2):
                                if i > 0:
                                    pe.matmul(ps[3][0:m, gg * 256:gg * 256 + 256], xc[:, 6 + gg, t0:t0 + m], hp[:, gg * 256:gg * 256 + 256])
                                mm = pe.matmul(ps[4][:, gg * 256:gg * 256 + 256], Bn[0:m, gg * P:gg * P + P], xw[0:m, gg * 256:gg * 256 + 256])
                            mm.then_inc(S("d_out"), 1)
                            front(i + 1)
                        else:
                            mm.then_inc(S("d_out"), 1)
                            pe.wait_ge(S("ssm_in"), 64)

                            def turn_state(b):
                                if b >= 2:
                                    pe.wait_ge(S("hs_taken"), b - 1)
                                for qq in range(4):
                                    mm = pe.transpose(ps[1 + b % 2 * 3][:, qq * P:qq * P + P], h0[:, b, qq, :], ident)
                                mm.then_inc(S("hs_turned"), 1)
                            turn_state(0)
                            pe.wait_ge(S("c_masked"), 1)
                            for b in range(NB):
                                if b < NB - 1:
                                    turn_state(b + 1)
                                pe.wait_ge(S("hs_taken"), b + 1)
                                for gg in range(2):
                                    mm = pe.matmul(ps[3][0:NS, gg * 256:gg * 256 + 256], CM[:, gg, b, :], hs[b % 2][:, gg * 256:gg * 256 + 256],
                                                   start=(b == 0 and gg == 0), stop=(b == NB - 1 and gg == 1), skip_group_check=True)
                                mm.then_inc(S("hs_used"), 1)
                            pe.wait_ge(S("a_spread"), 1)
                            for qq in range(4):
                                mm = pe.matmul(ps[1][:, qq * NB:qq * NB + NB], y[0:NS, qq * P:qq * P + P], K("seqhot")[0:NS])
                            mm.then_inc(S("ssm_decay_sums"), 1)
                            for n in range(8):
                                qq, half = n // 2, n % 2
                                pe.wait_ge(S("b_masked"), qq // 2 + 1)
                                if n >= 2:
                                    pe.wait_ge(S("ssm_new"), n - 1)
                                pe.matmul(ps[(4, 2)[n % 2]][:, :], xw[0:NS, qq * P:qq * P + P],
                                          Bx[0:NS, half * 4:half * 4 + 4, :].rearrange("p b s -> p (b s)")).then_inc(S("ssm_add"), 1)
                        share.point("pe", pe)
                        share.point("pe", pe)
                        pe.wait_ge(S("d_y"), i + 1)
                        for c in range(4):
                            mm = pe.transpose(ps[5][:, c * m:c * m + m], y[0:m, c * P:c * P + P], ident[0:m, 0:m])
                        mm.then_inc(S("d_y_turned"), 1)
                        share.point("pe", pe)
                        if i == 3:
                            for qq in range(4):
                                mm = pe.transpose(ps[4][:, qq * P:qq * P + P], hp[:, qq * P:qq * P + P], ident)
                            mm.then_inc(S("hp_turned"), 1)
                    share.end("pe", pe)

                @block.scalar
                def _(act):
                    def take_front(i):
                        m = tiles[i][1]
                        k = 2 if i == 4 else 3
                        act.wait_ge(S("d_turned"), i + 1)
                        act.activation(xn2[0:m, i % 2, :], ps[0][0:m, :], ACT.Copy)
                        act.activation(Bn2[0:m, i % 2, :], ps[1][0:m, 0:256], ACT.Copy)
                        act.activation(ec2[0:m, i % 2, 0:k, :], ps[2][0:m, 256:256 + 8 * k].rearrange("p (k h) -> p k h", k=k), ACT.Exp).then_inc(S("d_taken"), 1)
                        act.wait_ge(S(f"z_in{i % 2}"), 16 * (i // 2 + 1))
                        act.activation(z[0:m, i % 2, :], z[0:m, i % 2, :], ACT.Silu).then_inc(S("z_gate"), 1)

                    share.point("act", act)
                    take_front(0)
                    share.point("act", act)
                    for i, (t0, m) in enumerate(tiles):
                        last = i == 4
                        act.wait_ge(S("d_seg_sums"), i + 1)
                        for half in range(2):
                            ins = act.activation(W[0:m, half * 4 * m:half * 4 * m + 4 * m], ps[3 + half][0:m, 0:4 * m], ACT.Exp)
                        ins.then_inc(S("d_seg_exp"), 1)
                        share.point("act", act)
                        share.point("act", act)
                        if last:
                            act.wait_ge(S("d_out"), 5)
                            for b in range(NB):
                                act.wait_ge(S("hs_turned"), b + 1)
                                if b >= 2:
                                    act.wait_ge(S("hs_used"), b - 1)
                                act.activation(hs[b % 2][:, :], ps[1 + b % 2 * 3][:, :], ACT.Copy).then_inc(S("hs_taken"), 1)
                            act.wait_ge(S("ssm_decay_sums"), 1)
                            act.activation(dec.rearrange("p q b -> p (q b)"), ps[1][:, 0:32], ACT.Exp).then_inc(S("ssm_decays"), 1)
                        else:
                            take_front(i + 1)
                        share.point("act", act)
                        act.wait_ge(S("d_sq"), i + 1)
                        ach.link(act, act.activation(ss[0:m, :], ss[0:m, :], ACT.Ln, bias=eps[0:m], scale=1.0 / 256))
                        act.activation(ss[0:m, :], ss[0:m, :], ACT.Exp, scale=-0.5).then_inc(S("d_rstd"), 1)
                        share.point("act", act)
                        act.wait_ge(S("d_y_turned"), i + 1)
                        if i == 0:
                            act.wait_ge(S("conv_stored"), 32)
                        act.activation(brT[:, 12:16, t0:t0 + m], ps[5][:, 0:4 * m].rearrange("p (c t) -> p c t", c=4), ACT.Copy).then_inc(S("d_y_taken"), 1)
                        share.point("act", act)
                        if i == 3:
                            act.wait_ge(S("hp_turned"), 1)
                            act.activation(hp[:, :], ps[4][:, :], ACT.Copy).then_inc(S("ssm_prompt_ready"), 1)
                    share.end("act", act)

                @block.vector
                def _(dve):
                    L = vch.link

                    def v3(x, m, k):
                        return x[0:m].rearrange("p (k d) -> p k d", k=k)

                    def segments(i):
                        m = tiles[i][1]
                        aft = K("after_s")[0:NS] if i == 4 else after
                        dve.tensor_tensor(AW[0:m, 0:8 * m].rearrange("p (h n) -> p h n", h=8), bc(aft, 1, 8), bc(a[0:m, i, :], 2, m), ALU.mult).then_inc(S("d_segs"), 1)

                    share.point("dve", dve)
                    segments(0)
                    share.point("dve", dve)
                    for i, (t0, m) in enumerate(tiles):
                        last = i == 4
                        triu = K("tri_s")[0:NS] if last else tri
                        xn, Bn, ec = xn2[:, i % 2], Bn2[:, i % 2], ec2[:, i % 2]
                        dve.wait_ge(S("d_taken"), i + 1)
                        cbm = ps[2][0:m, 0:2 * m].rearrange("p (g n) -> p g n", g=2)
                        L(dve, dve.tensor_tensor(v3(y, m, 1)[:, 0, 0:2 * m].rearrange("p (g n) -> p g n", g=2), cbm, bc(triu, 1, 2), ALU.mult))
                        L(dve, dve.tensor_tensor(wt[0:m, :], ec[0:m, 1, :], dt[0:m, i, :], ALU.mult))
                        L(dve, dve.tensor_tensor(v3(xw, m, 8), v3(xn, m, 8), bc(wt[0:m, :], 2, 64), ALU.mult))
                        dve.wait_ge(S("d_seg_exp"), i + 1)
                        L(dve, dve.tensor_tensor(v3(t_x, m, 8), v3(xn, m, 8), bc(dt[0:m, i, :], 2, 64), ALU.mult))
                        dve.tensor_tensor(W[0:m, 0:8 * m].rearrange("p (g h n) -> p g h n", g=2, h=4), W[0:m, 0:8 * m].rearrange("p (g h n) -> p g h n", g=2, h=4),
                                          bc(y[0:m, 0:2 * m].rearrange("p (g n) -> p g n", g=2), 2, 4), ALU.mult).then_inc(S("d_weights"), 1)
                        share.point("dve", dve)
                        share.point("dve", dve)
                        dve.wait_ge(S("d_out"), i + 1)
                        if last:
                            msk = K("qmask").rearrange("p (b t) -> p b t", b=NB)
                            dve.tensor_copy(v3(y, NS, 8), bc(a[0:NS, 4, :], 2, 64)).then_inc(S("a_spread"), 1)
                            for gg in range(2):
                                ins = dve.tensor_tensor(CM[:, gg], bc(xc[:, 6 + gg, SEQ:T], 1, NB), msk, ALU.mult)
                            ins.then_inc(S("c_masked"), 1)
                            dve.wait_ge(S("ssm_decays"), 1)
                            dve.wait_ge(S("hs_used"), 8)
                            for n in range(8):
                                qq, half = n // 2, n % 2
                                if n % 4 == 0:
                                    if n:
                                        dve.wait_ge(S("ssm_add"), 4)
                                    dve.tensor_tensor(Bx[0:NS], bc(Bn[0:NS, qq // 2 * P:qq // 2 * P + P], 1, NB), bc(K("seqhot")[0:NS], 2, P), ALU.mult).then_inc(S("b_masked"), 1)
                                dve.wait_ge(S("ssm_add"), n + 1)
                                st = h0[:, half * 4:half * 4 + 4, qq, :]
                                L(dve, dve.tensor_tensor(st, st, bc(dec[:, qq, half * 4:half * 4 + 4], 2, P), ALU.mult))
                                dve.tensor_tensor(st, st, ps[(4, 2)[n % 2]][:, :].rearrange("p (b s) -> p b s", b=4), ALU.add).then_inc(S("ssm_new"), 1)
                            dve.wait_ge(S("ssm_new"), 8)
                        else:
                            if i == 0:
                                L(dve, dve.tensor_copy(hp[:, :], ps[4][:, :]))
                            else:
                                L(dve, dve.tensor_tensor(v3(hp, P, 8), v3(hp, P, 8), bc(ec[:, 2, :], 2, 64), ALU.mult))
                                L(dve, dve.tensor_tensor(hp[:, :], hp[:, :], ps[4][:, :], ALU.add))
                        dve.wait_ge(S("z_gate"), i + 1)
                        L(dve, dve.tensor_tensor(v3(t, m, 8), v3(xn, m, 8), bc(dskip[0:m, :], 2, 64), ALU.mult))
                        L(dve, dve.tensor_tensor(t[0:m, :], t[0:m, :], ps[5][0:m, :], ALU.add))
                        if i > 0:
                            L(dve, dve.tensor_tensor(v3(y, m, 8), ps[3][0:m, :].rearrange("p (k d) -> p k d", k=8), bc(ec[0:m, 0, :], 2, 64), ALU.mult))
                            L(dve, dve.tensor_tensor(t[0:m, :], t[0:m, :], y[0:m, :], ALU.add))
                        L(dve, dve.tensor_tensor(y[0:m, :], t[0:m, :], z[0:m, i % 2, :], ALU.mult))
                        L(dve, dve.tensor_tensor(t[0:m, :], y[0:m, :], y[0:m, :], ALU.mult))
                        dve.tensor_reduce(ss[0:m, :], v3(t, m, 2), AX, ALU.add).then_inc(S("d_sq"), 1)
                        if not last:
                            segments(i + 1)
                        share.point("dve", dve)
                        share.point("dve", dve)
                        dve.wait_ge(S("d_rstd"), i + 1)
                        L(dve, dve.tensor_tensor(v3(y, m, 2), v3(y, m, 2), bc(ss[0:m, :], 2, 256), ALU.mult))
                        dve.tensor_tensor(y[0:m, :], y[0:m, :], gssm[0:m, :], ALU.mult).then_inc(S("d_y"), 1)
                        dve.wait_ge(S("d_y_turned"), i + 1)
                        share.point("dve", dve)
                    share.end("dve", dve)

        def stage_merge(l):
            with nc.Block() as block:
                @block.sync
                def _(sp):
                    stream(sp, J["wo1"] + 3, l)
                    sp.wait_ge(S("ssm_stored"), 32)

                @block.tensor
                def _(pe):
                    finish_to("pe", pe, "wo1")

                @block.scalar
                def _(act):
                    finish_to("act", act, "wo1")

                @block.vector
                def _(dve):
                    finish_to("dve", dve, "wo1")

        def stage_ff(l):
            ar = Arena(arena, 0, AN - 4 * T)
            ff = ar.take(FC, T)
            ff_ref[0] = ff
            with nc.Block() as block:
                @block.sync
                def _(sp):
                    stream(sp, len(jobs), l)

                @block.tensor
                def _(pe):
                    rms_pe(pe)
                    finish_to("pe", pe, "gu10")
                    sem, n = taken_by(len(table) - 1)
                    pe.wait_ge(S(sem), n)
                    for db in range(2):
                        for r in range(3):
                            j = J[f"dn{db}{r}"]
                            arrived(pe, j)
                            for c in range(min(8, FC - 8 * r)):
                                fc = 8 * r + c
                                for dc in range(4):
                                    w = slot3(j)[:, c, dc * P:dc * P + P]
                                    if db and fc == 0:
                                        pe.wait_ge(S("down_taken"), dc + 1)
                                    for half in range(2):
                                        mm = pe.matmul(ps[2 * dc + half][:, 0:HALF], w, ff[:, fc, half * HALF:half * HALF + HALF],
                                                       start=(fc == 0), stop=(fc == FC - 1))
                            mm.then_inc(S("down_job_done"), 1)

                @block.scalar
                def _(act):
                    rms_act(act)
                    finish_to("act", act, "gu10")

                @block.vector
                def _(dve):
                    rms_dve(dve, g2, False, l)
                    finish_to("dve", dve, "gu10")
                    for db in range(2):
                        dve.wait_ge(S("down_job_done"), 3 * (db + 1))
                        for dc in range(4):
                            for half in range(2):
                                x = xT[:, db * 4 + dc, half * HALF:half * HALF + HALF]
                                ins = dve.tensor_tensor(x, x, ps[2 * dc + half][:, 0:HALF], ALU.add)
                            ins.then_inc(S("down_taken"), 1)

        with nc.Fori(0, DEPTH) as l:
            part(stage_a, l)
            part(stage_retention, l)
            part(stage_hgrn, l)
            part(stage_ssm, l)
            part(stage_merge, l)
            part(stage_ff, l)
            with nc.Block() as block:
                @block.sync
                def _(sp):
                    for name in LAYER_SEMS:
                        sp.sem_clear(S(name))

        def epilogue():
            ar = Arena(arena, 0, AN)
            yn = ar.take(5, DM)
            with nc.Block() as block:
                @block.tensor
                def _(pe):
                    for u in range(10):
                        i, half = u // 2, u % 2
                        t0, m = tiles[i]
                        if u >= 2:
                            pe.wait_ge(S("end_taken"), u - 1)
                        for c in range(4):
                            mm = pe.transpose(ps[u % 2][0:m, c * P:c * P + P], xT[:, half * 4 + c, t0:t0 + m], ident)
                        mm.then_inc(S("end_turned"), 1)

                @block.scalar
                def _(act):
                    for u in range(10):
                        i, half = u // 2, u % 2
                        m = tiles[i][1]
                        act.wait_ge(S("end_turned"), u + 1)
                        act.activation(yn[0:m, i, half * 512:half * 512 + 512], ps[u % 2][0:m, :], ACT.Copy).then_inc(S("end_taken"), 1)

                @block.sync
                def _(sp):
                    sp.wait_ge(S("end_taken"), 10)
                    sp.dma_start(out["y_prompt"].rearrange("o (t p) d -> p (o t) d", p=P), yn[:, 0:4, :]).then_inc(S("end_stored"), 16)
                    sp.dma_start(out["y_sample"].rearrange("b t d -> (b t) d"), yn[0:NS, 4, :]).then_inc(S("end_stored"), 16)
                    sp.wait_ge(S("end_stored"), 32)

        part(epilogue)


OUTS = [("y_prompt", (1, SEQ, DM)), ("y_sample", (NB, TS, DM)),
        ("k_prompt", (DEPTH, 1, SEQ, 4, 64)), ("v_prompt", (DEPTH, 1, SEQ, 4, 64)), ("kidx_prompt", (DEPTH, 1, SEQ, 64)),
        ("ret_prompt", (DEPTH, 1, 4, P, P)), ("hgrn_prompt", (DEPTH, 1, 4, P, P)), ("ssm_prompt", (DEPTH, 1, 8, 64, P)),
        ("conv_prompt", (DEPTH, 1, 3, DM)),
        ("k_sample", (DEPTH, NB, TS, 4, 64)), ("v_sample", (DEPTH, NB, TS, 4, 64)), ("kidx_sample", (DEPTH, NB, TS, 64)),
        ("ret_sample", (DEPTH, NB, 4, P, P)), ("hgrn_sample", (DEPTH, NB, 4, P, P)), ("ssm_sample", (DEPTH, NB, 8, 64, P)),
        ("conv_sample", (DEPTH, NB, 3, DM))]


def build(nc, arrays):
    inp = {n: nc.dram_tensor(f"in_{n}", a.shape, mybir.dt.from_np(a.dtype), kind="ExternalInput").ap() for n, a in arrays.items()}
    out = {n: nc.dram_tensor(f"out_{n}", s, F32, kind="ExternalOutput").ap() for n, s in OUTS}
    trunk(nc, inp, out)


def kernel(**inputs):
    import concourse.bacc as bacc
    from concourse.bass_utils import run_bass_kernel_spmd

    arrays = {n: np.ascontiguousarray(a) for n, a in inputs.items()}
    arrays["consts"] = constants()
    nc = bacc.Bacc("TRN2", target_bir_lowering=False, num_devices=1)
    build(nc, arrays)
    r = run_bass_kernel_spmd(nc, [{f"in_{n}": a for n, a in arrays.items()}], core_ids=[0])
    return tuple(r.results[0][f"out_{n}"] for n, _ in OUTS)
```
